# Optimizing a Trainium2 kernel written in Bass

```python
import jax
import jax.numpy as jnp
from jax import lax
import numpy as np

D_MODEL = 1024
BATCH = 1
SEQ = 128
DEPTH = 2
DEC_BATCH = 1
DEC_SEQ = 512
PAST_LEN = 128

GRID_W = 64
HEAD_DIM = 64
ATT_HEADS = 8
ATT_KV = 2
ATT_GROUP = ATT_HEADS // ATT_KV
WIN_HEADS = 8
WIN_KV = 2
WIN_GROUP = WIN_HEADS // WIN_KV
WINDOW = 128
Q_BLOCK = 128
ML_HEADS = 4
ML_DK = 64
ML_DV = 128
ML_CHUNK = 128
BRANCH_W = 512
N_BRANCH = 3
ROPE_THETA = 10000.0
AXIS_DIM = HEAD_DIM // 2
LN_EPS = 1e-6
RMS_EPS = 1e-6
F32 = jnp.float32

SPLIT_SIZES = (
    ATT_HEADS * HEAD_DIM, ATT_KV * HEAD_DIM, ATT_KV * HEAD_DIM, BRANCH_W,
    ML_HEADS * ML_DK, ML_HEADS * ML_DK, ML_HEADS * ML_DV, ML_HEADS * ML_DV,
    4 * ML_HEADS, BRANCH_W,
    WIN_HEADS * HEAD_DIM, WIN_KV * HEAD_DIM, WIN_KV * HEAD_DIM, BRANCH_W,
    N_BRANCH * D_MODEL,
)
N_IN = sum(SPLIT_SIZES)

kernel_name = 'hybrid_diffusion_prefix_trunk'

def layer_norm(x):
    xf = x.astype(F32)
    mu = jnp.mean(xf, axis=-1, keepdims=True)
    var = jnp.mean(jnp.square(xf - mu), axis=-1, keepdims=True)
    return (xf - mu) * lax.rsqrt(var + LN_EPS)

def rms_norm(x, g):
    xf = x.astype(F32)
    y = xf * lax.rsqrt(jnp.mean(jnp.square(xf), axis=-1, keepdims=True) + RMS_EPS)
    return (y * g.astype(F32)).astype(x.dtype)

def split_columns(p):
    idx = [int(s) for s in np.cumsum(SPLIT_SIZES)[:-1]]
    return jnp.split(p, idx, axis=-1)

def q_heads(x, n_kv, n_group):
    B, T, _ = x.shape
    return x.reshape(B, T, n_kv, n_group, HEAD_DIM).transpose(0, 2, 3, 1, 4)

def kv_heads(x, n_kv):
    B, T, _ = x.shape
    return x.reshape(B, T, n_kv, HEAD_DIM).transpose(0, 2, 1, 3)

def merge_heads(o):
    B, KV, G, T, HD = o.shape
    return o.transpose(0, 3, 1, 2, 4).reshape(B, T, KV * G * HD)

def axial_rope(T, dtype):
    rows = T // GRID_W
    row = jnp.repeat(jnp.arange(rows, dtype=F32), GRID_W)
    col = jnp.tile(jnp.arange(GRID_W, dtype=F32), rows)
    inv = ROPE_THETA ** (-jnp.arange(0, AXIS_DIM, 2, dtype=F32) / AXIS_DIM)
    ar = row[:, None] * inv
    ac = col[:, None] * inv
    ang = jnp.concatenate([ar, ar, ac, ac], axis=-1)
    return jnp.cos(ang).astype(dtype), jnp.sin(ang).astype(dtype)

def apply_rope(x, cos, sin):
    half = AXIS_DIM // 2

    def rot(h):
        return jnp.concatenate([-h[..., half:], h[..., :half]], axis=-1)

    xr = jnp.concatenate([rot(x[..., :AXIS_DIM]), rot(x[..., AXIS_DIM:])], axis=-1)
    return x * cos + xr * sin

def softmax_with_sink(s, sink):
    s = s.astype(F32)
    if sink is None:
        return jax.nn.softmax(s, axis=-1)
    sk = sink.astype(F32).reshape((1,) + sink.shape + (1,) * (s.ndim - 3))
    mx = jnp.maximum(jnp.max(s, axis=-1, keepdims=True), sk)
    e = jnp.exp(s - mx)
    return e / (jnp.sum(e, axis=-1, keepdims=True) + jnp.exp(sk - mx))

def attend_blocks(q, k, v, sink):
    B, KV, G, T, HD = q.shape
    nb = T // Q_BLOCK
    qb = jnp.moveaxis(q.reshape(B, KV, G, nb, Q_BLOCK, HD), 3, 0)

    def one_block(qi):
        s = jnp.einsum('bkgqd,bksd->bkgqs', qi, k).astype(F32) * (HD ** -0.5)
        p = softmax_with_sink(s, sink)
        return jnp.einsum('bkgqs,bksd->bkgqd', p.astype(v.dtype), v)

    o = lax.map(one_block, qb)
    return jnp.moveaxis(o, 0, 3).reshape(B, KV, G, T, HD)

def attend_band(q, k, v, kc, vc, sink):
    B, KV, G, T, HD = q.shape
    nb = T // Q_BLOCK
    pad = ((0, 0), (0, 0), (Q_BLOCK, Q_BLOCK), (0, 0))
    kp = jnp.pad(k, pad).reshape(B, KV, nb + 2, Q_BLOCK, HD)
    vp = jnp.pad(v, pad).reshape(B, KV, nb + 2, Q_BLOCK, HD)
    kband = jnp.concatenate([kp[:, :, :-2], kp[:, :, 1:-1], kp[:, :, 2:]], axis=3)
    vband = jnp.concatenate([vp[:, :, :-2], vp[:, :, 1:-1], vp[:, :, 2:]], axis=3)
    qb = q.reshape(B, KV, G, nb, Q_BLOCK, HD)
    scale = HD ** -0.5
    s_band = jnp.einsum('bkgnqd,bknsd->bkgnqs', qb, kband).astype(F32) * scale
    s_ctx = jnp.einsum('bkgnqd,bksd->bkgnqs', qb, kc).astype(F32) * scale
    blk = jnp.arange(nb)[:, None, None] * Q_BLOCK
    qpos = blk + jnp.arange(Q_BLOCK)[None, :, None]
    kpos = blk - Q_BLOCK + jnp.arange(3 * Q_BLOCK)[None, None, :]
    valid = (jnp.abs(kpos - qpos) <= WINDOW) & (kpos >= 0) & (kpos < T)
    s_band = jnp.where(valid, s_band, -jnp.inf)
    p = softmax_with_sink(jnp.concatenate([s_band, s_ctx], axis=-1), sink).astype(v.dtype)
    nband = 3 * Q_BLOCK
    o = (jnp.einsum('bkgnqs,bknsd->bkgnqd', p[..., :nband], vband)
         + jnp.einsum('bkgnqs,bksd->bkgnqd', p[..., nband:], vc))
    return o.reshape(B, KV, G, T, HD)

def mlstm_chunkwise(q, k, v, i_pre, f_log, C0, n0, m0):
    B, H, T, _ = q.shape
    L = ML_CHUNK
    N = T // L

    def chunks(a):
        return jnp.moveaxis(a.reshape((B, H, N, L) + a.shape[3:]), 2, 0)

    lower = jnp.tril(jnp.ones((L, L), dtype=bool))

    def step(carry, xs):
        C, n, m = carry
        qb, kb, vb, ib, fb = xs
        b = jnp.cumsum(fb, axis=-1)
        a = b + m[..., None]
        D = jnp.where(lower, b[..., :, None] - b[..., None, :] + ib[..., None, :], -jnp.inf)
        mt = jnp.maximum(a, jnp.max(D, axis=-1))
        s = jnp.einsum('bhtd,bhsd->bhts', qb, kb) * jnp.exp(D - mt[..., None])
        w_inter = jnp.exp(a - mt)
        num = (jnp.einsum('bhts,bhsv->bhtv', s, vb)
               + w_inter[..., None] * jnp.einsum('bhvd,bhtd->bhtv', C, qb))
        den = jnp.sum(s, axis=-1) + w_inter * jnp.einsum('bhd,bhtd->bht', n, qb)
        h = num / jnp.maximum(jnp.abs(den), jnp.exp(-mt))[..., None]
        b_last = b[..., -1]
        g = b_last[..., None] - b + ib
        m_new = jnp.maximum(b_last + m, jnp.max(g, axis=-1))
        ws = jnp.exp(g - m_new[..., None])
        wc = jnp.exp(b_last + m - m_new)
        C_new = wc[..., None, None] * C + jnp.einsum('bhs,bhsv,bhsd->bhvd', ws, vb, kb)
        n_new = wc[..., None] * n + jnp.einsum('bhs,bhsd->bhd', ws, kb)
        return (C_new, n_new, m_new), h

    init = (C0.astype(F32), n0.astype(F32), m0.astype(F32))
    (C, n, m), hs = lax.scan(step, init, tuple(chunks(a) for a in (q, k, v, i_pre, f_log)))
    h = jnp.moveaxis(hs, 0, 2).reshape(B, H, T, v.shape[-1])
    return h, C, n, m

def mlstm_bidir(q, k, v, o, gates, gate_bias, C0, n0, m0):
    B, T, _ = q.shape

    def heads(a, d):
        return a.astype(F32).reshape(B, T, ML_HEADS, d).transpose(0, 2, 1, 3)

    qh = heads(q, ML_DK)
    kh = heads(k, ML_DK) * (ML_DK ** -0.5)
    vh = heads(v, ML_DV)
    g = (gates.astype(F32).reshape(B, T, 4, ML_HEADS) + gate_bias.astype(F32)).transpose(0, 2, 3, 1)
    i_f, f_f = g[:, 0], jax.nn.log_sigmoid(g[:, 1])
    i_b, f_b = g[:, 2], jax.nn.log_sigmoid(g[:, 3])
    h_f, Cf, nf, mf = mlstm_chunkwise(qh, kh, vh, i_f, f_f, C0[:, 0], n0[:, 0], m0[:, 0])

    def rev(a):
        return jnp.flip(a, axis=2)

    h_b, Cb, nb, mb = mlstm_chunkwise(rev(qh), rev(kh), rev(vh), rev(i_b), rev(f_b),
                                      C0[:, 1], n0[:, 1], m0[:, 1])
    h = (h_f + rev(h_b)).transpose(0, 2, 1, 3).reshape(B, T, ML_HEADS * ML_DV)
    y = jax.nn.sigmoid(o.astype(F32)) * h
    return (y.astype(q.dtype), jnp.stack([Cf, Cb], axis=1), jnp.stack([nf, nb], axis=1),
            jnp.stack([mf, mb], axis=1))

def modulate_project(x, mod, w_in):
    shift, scale, gate = jnp.split(mod, 3, axis=-1)
    u = (layer_norm(x) * (1.0 + scale) + shift).astype(x.dtype)
    return split_columns(u @ w_in), gate

def merge_residual(x, ys, zs, g_merge, gate, w_branch, w_out, ln_g, ln_b, alpha):
    gates = jnp.split(jax.nn.sigmoid(g_merge), N_BRANCH, axis=-1)
    merged = sum(gb * ((yb * jax.nn.silu(zb)) @ w_branch[i])
                 for i, (yb, zb, gb) in enumerate(zip(ys, zs, gates)))
    h = alpha * x + gate * (merged @ w_out)
    return (layer_norm(h) * ln_g + ln_b).astype(x.dtype)

def context_layer(x, mod, lp, alpha):
    w_in, qk_gain, sink, gate_bias, w_branch, w_out, ln_g, ln_b = lp
    parts, gate = modulate_project(x, mod, w_in)
    qa, ka, va, za, qm, km, vm, om, gm, zm, qw, kw, vw, zw, g_merge = parts
    B = x.shape[0]
    qa = rms_norm(q_heads(qa, ATT_KV, ATT_GROUP), qk_gain[0])
    ka = rms_norm(kv_heads(ka, ATT_KV), qk_gain[1])
    va = kv_heads(va, ATT_KV)
    ya = merge_heads(attend_blocks(qa, ka, va, None))
    qw = q_heads(qw, WIN_KV, WIN_GROUP)
    kw = kv_heads(kw, WIN_KV)
    vw = kv_heads(vw, WIN_KV)
    yw = merge_heads(attend_blocks(qw, kw, vw, sink))
    C0 = jnp.zeros((B, 2, ML_HEADS, ML_DV, ML_DK), F32)
    n0 = jnp.zeros((B, 2, ML_HEADS, ML_DK), F32)
    m0 = jnp.zeros((B, 2, ML_HEADS), F32)
    ym, Cm, nm, mm = mlstm_bidir(qm, km, vm, om, gm, gate_bias, C0, n0, m0)
    x_new = merge_residual(x, (ya, ym, yw), (za, zm, zw), g_merge, gate, w_branch, w_out, ln_g, ln_b, alpha)
    return x_new, (ka, va, kw, vw, Cm, nm, mm)

def latent_layer(x, mod, ctx, lp, alpha):
    w_in, qk_gain, sink, gate_bias, w_branch, w_out, ln_g, ln_b = lp
    ck_a, cv_a, ck_w, cv_w, C0, n0, m0 = ctx
    parts, gate = modulate_project(x, mod, w_in)
    qa, ka, va, za, qm, km, vm, om, gm, zm, qw, kw, vw, zw, g_merge = parts
    cos, sin = axial_rope(x.shape[1], x.dtype)
    qa = apply_rope(rms_norm(q_heads(qa, ATT_KV, ATT_GROUP), qk_gain[0]), cos, sin)
    ka = apply_rope(rms_norm(kv_heads(ka, ATT_KV), qk_gain[1]), cos, sin)
    va = kv_heads(va, ATT_KV)
    k_all = jnp.concatenate([ka, ck_a.astype(ka.dtype)], axis=2)
    v_all = jnp.concatenate([va, cv_a.astype(va.dtype)], axis=2)
    ya = merge_heads(attend_blocks(qa, k_all, v_all, None))
    qw = apply_rope(q_heads(qw, WIN_KV, WIN_GROUP), cos, sin)
    kw = apply_rope(kv_heads(kw, WIN_KV), cos, sin)
    vw = kv_heads(vw, WIN_KV)
    yw = merge_heads(attend_band(qw, kw, vw, ck_w.astype(kw.dtype), cv_w.astype(vw.dtype), sink))
    ym, _, _, _ = mlstm_bidir(qm, km, vm, om, gm, gate_bias, C0, n0, m0)
    return merge_residual(x, (ya, ym, yw), (za, zm, zw), g_merge, gate, w_branch, w_out, ln_g, ln_b, alpha)

def setup_inputs(seed: int = 0) -> dict:
    key = jax.random.key(seed)
    ks = jax.random.split(key, 21)
    D = D_MODEL
    beta = (8.0 * DEPTH) ** -0.25

    def nrm(k, shape, scale=1.0):
        return jax.random.normal(k, shape, F32) * scale

    gate_bias_base = jnp.array([0.0, 3.0, 0.0, 3.0], F32)[None, :, None]
    return {
        'x_prompt': nrm(ks[0], (BATCH, SEQ, D)),
        'x_sample': nrm(ks[1], (DEC_BATCH, DEC_SEQ, D)),
        'cache_attn_k': nrm(ks[2], (DEC_BATCH, DEPTH, ATT_KV, PAST_LEN, HEAD_DIM)),
        'cache_attn_v': nrm(ks[3], (DEC_BATCH, DEPTH, ATT_KV, PAST_LEN, HEAD_DIM)),
        'cache_win_k': nrm(ks[4], (DEC_BATCH, DEPTH, WIN_KV, PAST_LEN, HEAD_DIM)),
        'cache_win_v': nrm(ks[5], (DEC_BATCH, DEPTH, WIN_KV, PAST_LEN, HEAD_DIM)),
        'state_mlstm_C': nrm(ks[6], (DEC_BATCH, DEPTH, 2, ML_HEADS, ML_DV, ML_DK), 0.1),
        'state_mlstm_n': nrm(ks[7], (DEC_BATCH, DEPTH, 2, ML_HEADS, ML_DK), 0.3),
        'state_mlstm_m': nrm(ks[8], (DEC_BATCH, DEPTH, 2, ML_HEADS)),
        'c': nrm(ks[9], (DEC_BATCH, D)),
        'c_ctx': nrm(ks[10], (D,)),
        'w_mod': nrm(ks[11], (DEPTH, D, 3 * D), 0.5 * D ** -0.5),
        'b_mod': nrm(ks[12], (DEPTH, 3 * D), 0.02),
        'w_in': nrm(ks[13], (DEPTH, D, N_IN), D ** -0.5),
        'qk_gain': 1.0 + nrm(ks[14], (DEPTH, 2, HEAD_DIM), 0.02),
        'sink_logit': nrm(ks[15], (DEPTH, WIN_KV, WIN_GROUP), 0.5),
        'mlstm_gate_bias': gate_bias_base + nrm(ks[16], (DEPTH, 4, ML_HEADS), 0.1),
        'w_branch': nrm(ks[17], (DEPTH, N_BRANCH, BRANCH_W, D), BRANCH_W ** -0.5),
        'w_out': nrm(ks[18], (DEPTH, D, D), beta * D ** -0.5),
        'ln_gain': 1.0 + nrm(ks[19], (DEPTH, D), 0.02),
        'ln_bias': nrm(ks[20], (DEPTH, D), 0.02),
    }

def reference(x_prompt, x_sample, cache_attn_k, cache_attn_v, cache_win_k, cache_win_v,
              state_mlstm_C, state_mlstm_n, state_mlstm_m, c, c_ctx, w_mod, b_mod, w_in,
              qk_gain, sink_logit, mlstm_gate_bias, w_branch, w_out, ln_gain, ln_bias):
    alpha = (2.0 * DEPTH) ** 0.25
    xp = x_prompt
    xs = x_sample
    ak, av, wk, wv, sC, sn, sm = [], [], [], [], [], [], []
    for l in range(DEPTH):
        lp = (w_in[l], qk_gain[l], sink_logit[l], mlstm_gate_bias[l], w_branch[l], w_out[l],
              ln_gain[l], ln_bias[l])
        mod_ctx = jax.nn.silu(c_ctx) @ w_mod[l] + b_mod[l]
        xp, ctx_t = context_layer(xp, mod_ctx, lp, alpha)
        ak.append(ctx_t[0]); av.append(ctx_t[1]); wk.append(ctx_t[2]); wv.append(ctx_t[3])
        sC.append(ctx_t[4]); sn.append(ctx_t[5]); sm.append(ctx_t[6])
        mod_lat = (jax.nn.silu(c) @ w_mod[l] + b_mod[l])[:, None, :]
        ctx_cache = (cache_attn_k[:, l], cache_attn_v[:, l], cache_win_k[:, l], cache_win_v[:, l],
                     state_mlstm_C[:, l], state_mlstm_n[:, l], state_mlstm_m[:, l])
        xs = latent_layer(xs, mod_lat, ctx_cache, lp, alpha)
    new_attn_k = jnp.stack(ak, axis=1)
    new_attn_v = jnp.stack(av, axis=1)
    new_win_k = jnp.stack(wk, axis=1)
    new_win_v = jnp.stack(wv, axis=1)
    new_mlstm_C = jnp.stack(sC, axis=1)
    new_mlstm_n = jnp.stack(sn, axis=1)
    new_mlstm_m = jnp.stack(sm, axis=1)
    return (xp, xs, new_attn_k, new_attn_v, new_win_k, new_win_v, new_mlstm_C, new_mlstm_n, new_mlstm_m)


_drawn_inputs = setup_inputs


def setup_inputs(seed=0):
    import zlib

    import numpy as np

    out = dict(_drawn_inputs(seed))
    spreads = {}
    factors = {'cache_attn_k': 8.0,
     'cache_attn_v': 8.0,
     'cache_win_k': 8.0,
     'cache_win_v': 8.0,
     'state_mlstm_C': 8.0,
     'state_mlstm_n': 7.556,
     'state_mlstm_m': 7.739,
     'qk_gain': 2.736,
     'sink_logit': 64.0}
    for name, (base, spread) in spreads.items():
        noise = np.random.default_rng([zlib.crc32(name.encode()), seed]).standard_normal(out[name].shape)
        drawn = base * np.exp(spread * noise) if base else spread * noise
        out[name] = jnp.asarray(drawn.astype(out[name].dtype))
    for name, factor in factors.items():
        out[name] = (out[name] * factor).astype(out[name].dtype)
    return out
```

```python
from contextlib import ExitStack

import concourse.bass as bass
from concourse import mybir

F32 = mybir.dt.float32
F32R = mybir.dt.float32r
BF16 = mybir.dt.bfloat16
ALU = mybir.AluOpType
ACT = mybir.ActivationFunctionType
AX = mybir.AxisListType

P = 128
DEPTH = 2
D = 1024
KD = D // P
LT = 4
T = LT + 1
TOK = T * P
HD = 64
NH = 8
KV = 2
MH = 4
DV = 128
BW = 512
HALF = 512
SCALE = HD ** -0.5
EPS = 1e-6
ALPHA = (2.0 * DEPTH) ** 0.25

COL_A = 0
COL_B = COL_A + NH * HD + 2 * KV * HD + BW
COL_B_GATES = COL_B + 2 * MH * HD + 2 * MH * DV
COL_C = COL_B_GATES + 4 * MH + BW
COL_G = COL_C + NH * HD + 2 * KV * HD + BW
BRANCH = {"A": 0, "B": 1, "C": 2}
MERGE_ORDER = ("A", "C", "B")

CHUNKS = [(0, 0), (1, 3), (0, 1), (1, 2), (0, 2), (1, 1), (0, 3), (1, 0), (0, LT), (1, LT)]
ROW0 = (0, 32)
GR = 36

UNITS = [(h, t) for h in range(NH) for t in range(T)]


def key_blocks(branch, t):
    if t == LT:
        return [LT]
    if branch == "A":
        return list(range(LT)) + [T]
    return [b for b in (t - 1, t, t + 1) if 0 <= b < LT] + [T]


class Pieces:

    def __init__(self):
        self.items = []
        self.first = {}
        self.chunk = {}
        self.last = {}
        self.inner = []

    def add(self, key, matrix, blocks, col, width):
        self.first[key] = len(self.items)
        self.chunk[key] = blocks // 2
        for k in range(0, blocks, 2):
            self.inner.append(len(self.items) - len(self.last))
            self.items.append((matrix, k, col, width))
        self.last[len(self.items) - 1] = key if key[0] == "mod" else (*key, T - 1)


class PsumPlan:

    def __init__(self):
        self.count = [0] * 8
        self.last = [None] * 8
        self.use = {}
        self.rolling = 0

    def take(self, key, *banks):
        before = sorted({self.last[b] for b in banks if self.last[b]})
        lead = banks[0]
        self.count[lead] += 1
        for b in banks:
            self.last[b] = (lead, self.count[lead])
        self.use[key] = (lead, self.count[lead], before)

    def roll(self, key):
        self.take(key, self.rolling % 8)
        self.rolling += 1

    def bank(self, key):
        return self.use[key][0]


def plan_layer():
    pieces, psum = Pieces(), PsumPlan()
    for c in range(6):
        pieces.add(("mod", c), "mod", KD, c * HALF, HALF)
        psum.take(("mod", c), c)
    psum.take("modT", 6)
    for i in range(4):
        psum.take(("gate", i), 7 - i % 2)
    for t in range(T):
        b = 2 * (t % 3)
        psum.take(("xT", t), b, b + 1)
    for br in MERGE_ORDER:
        if br != "B":
            base = COL_A if br == "A" else COL_C
            for name, col, width in (("kv", NH * HD, 2 * KV * HD), ("q", 0, NH * HD),
                                     ("z", NH * HD + 2 * KV * HD, BW)):
                pieces.add((br, name), "in", KD, base + col, width)
                for t in range(T):
                    psum.roll((br, name, t))
            for t in range(T + 1):
                e = t % 2
                if t < T:
                    psum.take((br, "qT", t), 2 * e, 2 * e + 1)
                psum.take((br, "kT", t), 4 + e)
                if t < T:
                    psum.take((br, "zT", t), 6 + e)
            for s in range(len(UNITS) + 3):
                if s < len(UNITS):
                    psum.take((br, "S", s), 2 * (s % 2), 2 * (s % 2) + 1)
                if 2 <= s < len(UNITS) + 2:
                    psum.take((br, "PT", s - 2), 4, 5)
                if s >= 3 and UNITS[s - 3][1] == LT:
                    h = UNITS[s - 3][0]
                    if h == 0:
                        psum.take((br, "Octx"), 7)
                    if h % 2 == 0:
                        psum.take((br, "O", h // 2), 6)
        else:
            for name, col in (("qk", 0), ("v", 512), ("gates", None), ("o", 1024),
                              ("T", None), ("z", COL_B_GATES + 4 * MH - COL_B)):
                if name == "gates":
                    psum.roll(("B", "gates", 0))
                    psum.roll(("B", "gates", 1))
                elif name == "T":
                    for t in range(T):
                        psum.roll(("B", "qkT", t))
                    psum.roll(("B", "C0T"))
                else:
                    pieces.add(("B", name), "in", KD, COL_B + col, HALF)
                    for t in range(T):
                        psum.roll(("B", name, t))
            for t in range(T):
                psum.take(("B", "cols", t), t % 2)
            psum.take(("B", "wcb"), 2)
            for k in range(len(CHUNKS) + 1):
                if k < len(CHUNKS):
                    psum.take(("B", "ST", k), 0, 1)
                    psum.take(("B", "GB", k), 2 + k % 2)
                if k >= 1:
                    d, t = CHUNKS[k - 1]
                    psum.take(("B", "ND", k - 1), 4, 5)
                    if t != LT:
                        psum.take(("B", "IN", k - 1), 6, 7)
                    psum.take(("B", "CS", k - 1), 2 + (k - 1) % 2)
            for t in range(T):
                psum.take(("B", "yT", t), t % 2)
        for hf in range(2):
            i = BRANCH[br]
            pieces.add((br, "G", hf), "in", KD, COL_G + i * D + hf * HALF, HALF)
            pieces.add((br, "BR", hf), ("branch", i), BW // P, hf * HALF, HALF)
            for name in ("G", "BR"):
                for t in range(T):
                    psum.roll((br, name, hf, t))
    for t in range(T):
        b = 2 * (t % 3)
        psum.take(("mT", t), b, b + 1)
    for hf in range(2):
        pieces.add(("out", hf), "out", KD, hf * HALF, HALF)
        for t in range(T):
            psum.roll(("out", hf, t))
    return pieces, psum


def trunk_kernel(nc, x_prompt, x_sample, cache_attn_k, cache_attn_v, cache_win_k, cache_win_v,
                 state_C, state_n, state_m, c, c_ctx, w_mod, b_mod, w_in, qk_gain, sink_logit,
                 gate_bias, w_branch, w_out, ln_gain, ln_bias, consts,
                 y_prompt, y_sample, new_attn_k, new_attn_v, new_win_k, new_win_v,
                 new_C, new_n, new_m):
    pieces, psum = plan_layer()
    NP = len(pieces.items)

    ctx = ExitStack()
    with ctx:
        ctx.enter_context(nc.allow_non_contiguous_dma(reason="states and columns of a few elements"))
        place = [0]
        base = nc.sbuf_base + (-nc.sbuf_base) % 64

        def at(name, shape, dt, offset):
            return nc.alloc_sbuf_tensor_at(name, shape, dt, offset=base + offset)

        def fixed(name, shape, dt, size=4):
            n = size
            for s in shape[1:]:
                n *= s
            n += -n % 32
            where = place[0]
            place[0] += n
            return at(name, shape, dt, where)

        def sem(name):
            return ctx.enter_context(nc.semaphore(name))

        act_T = fixed("act_T", [P, 2, KD, TOK], F32R)
        raw = fixed("raw", [P, 3, 2, HALF], F32)
        wsp = fixed("wsp", [P, 2, 2, 2, HALF], F32R)
        merged = fixed("merged", [P, T, D], F32)
        gate_bc = fixed("gate_bc", [P, 2, D], F32)
        ident = fixed("ident", [P, P], F32)
        rope = fixed("rope", [P, 2, LT, HD], F32)
        masks = fixed("masks", [P, 5, P], BF16, 2)
        ones = fixed("ones", [P, P], F32)
        cached = fixed("cached", [P, 2, 2, KV * HD], F32)
        C0 = fixed("C0", [P, 2, MH, HD], F32)
        n0 = fixed("n0", [P, 2, 2], F32)
        gains = fixed("gains", [P, 2, HD], F32)
        sink = fixed("sink", [P, 2, NH], F32)
        modc = fixed("modc", [P, 2 * KD, 2], F32)
        csil = fixed("csil", [P, 2, KD, 2], F32R)
        crow = fixed("crow", [2 * KD, 3, P], F32)
        gwraw = fixed("gwraw", [P, KD, 4 * MH], F32)
        gbias = fixed("gbias", [P, 1], F32)
        mcol = fixed("mcol", [P, 8], F32)
        half_neg = fixed("half_neg", [P, 16], F32)
        stats = fixed("stats", [P, T, 2, 6], F32)
        mv = fixed("mv", [P, T, 2], F32)
        ve = fixed("ve", [P, T], F32)
        rstd = fixed("rstd", [P, T], F32)
        ms = fixed("ms", [P, T, 10], F32)
        rms = fixed("rms", [P, T, 10], F32)
        nmx = fixed("nmx", [P, 4], F32)
        nm = fixed("nm", [P, 4], F32)
        lsum = fixed("lsum", [P, 4], F32)
        sexp = fixed("sexp", [P, 4], F32)
        den = fixed("den", [P, 4], F32)
        rden = fixed("rden", [P, 4], F32)
        dn = fixed("dn", [P, 2, 2, 2], F32)
        rdn = fixed("rdn", [P, 2, 2, 2], F32)
        wcb = fixed("wcb", [P, 4, T], F32)
        y_at = place[0]
        place[0] += 2 * 4 * TOK * 4
        yT = at("yT", [P, 2, 4, TOK], F32R, y_at)
        tokq = at("tokq", [P, T, NH, 2, HD], F32, y_at)
        tokqk = at("tokqk", [P, T, 2, MH * HD], F32, y_at)
        gw = at("gw", [P, 2, KD, P], F32R, y_at + T * 2048)
        kw = at("kw", [P, 2, MH * HD], F32, y_at + T * 2048 + 2 * KD * P * 4)
        arena = place[0]
        xh = at("xh", [P, T, D], F32, arena)
        modrow = at("modrow", [2, 3 * D], F32, arena + 20480)
        bmod = at("bmod", [2, 3 * D], F32, arena + 32768)
        utmp = at("utmp", [P, 2, KD, P], F32, arena + 45056)
        lnrow = at("lnrow", [P, 2, D], F32, arena + 44544)
        ot = at("ot", [P, 2, HALF], F32, arena + 52736)
        cst = at("cst", [P, 4, P], F32, arena + 20480)
        kvt = at("kvt", [P, T, 2, KV * HD], F32, arena)
        pr = at("pr", [P, 3, T * P], F32, arena + 5120)
        zt = at("zt", [P, T, HALF], F32, arena + 29696)
        zT = at("zT", [P, 4, TOK], F32, arena + 12800)
        pT = at("pT", [P, 2, T * HALF + P], F32, arena + 23040)
        rtmp = at("rtmp", [P, 640], F32, arena + 23040)
        ks = at("ks", [P, 2, KV, 2, 2, HD], F32, arena + 25600)
        ytmp = at("ytmp", [P, HALF], F32, arena + 44544)
        qT = at("qT", [P, NH, TOK], F32R, arena + 46592)
        kT = at("kT", [P, KV, 2, TOK + P], F32R, arena + 67072)
        tg = at("tg", [P, T, HALF], F32, arena + 23040)
        mt = at("mt", [P, 2, HALF], F32, arena + 33280)
        v1 = at("v1", [P, T, MH, DV + 1], F32, arena)
        zo = at("zo", [P, T, HALF], F32, arena + 10336)
        hs = at("hs", [P, T, HALF], F32, arena + 20576)
        qTm = at("qTm", [P, 2, TOK], F32, arena + 30816)
        kTm = at("kTm", [P, 2, TOK], F32, arena + 35936)
        cols = at("cols", [P, T, 4, GR], F32, arena + 41056)
        em = at("em", [P, 2, 2, 2 * P], F32, arena + 43936)
        sT = at("sT", [P, 2, 2, 2, P], F32, arena + 48032)
        nd = at("nd", [P, 2, 2, 2, DV + 1], F32, arena + 52128)
        t3 = at("t3", [P, 2, 2, DV + 1], F32, arena + 56256)
        CT = at("CT", [P, 2, 2, DV + 1], F32, arena + 58336)
        rw, rf, rb, rg, r1 = (at(n, [P, TOK], F32, arena + 60416 + 2560 * i)
                              for i, n in enumerate(("rw", "rf", "rb", "rg", "r1")))
        co = at("co", [P, 2, HALF], F32, arena + 60416)
        t4 = at("t4", [P, HALF], F32, arena + 73216)

        pb = ctx.enter_context(nc.psum_tensor("pb", [P, 8, HALF], F32))

        bank_full = [sem(f"bank_full{b}") for b in range(8)]
        bank_done = [sem(f"bank_done{b}") for b in range(8)]
        raw_in = [sem(f"raw_in{i}") for i in range(3)]
        raw_used = sem("raw_used")
        split_used = sem("split_used")
        small_in = sem("small_in")
        late_in = sem("late_in")
        stored = sem("stored")
        var_ready = sem("var_ready")
        rstd_ready = sem("rstd_ready")
        xn_ready = sem("xn_ready")
        u_hi = sem("u_hi")
        u_ready = sem("u_ready")
        pre_done = sem("pre_done")
        q_hi = sem("q_hi")
        q_ready = sem("q_ready")
        k_hi = sem("k_hi")
        k_ready = sem("k_ready")
        z_tanh = sem("z_tanh")
        nm_ready = sem("nm_ready")
        sink_done = sem("sink_done")
        p_ready = sem("p_ready")
        pv_even = sem("pv_even")
        y_hi = sem("y_hi")
        y_ready = sem("y_ready")
        gw_ready = sem("gw_ready")
        rows_dve = sem("rows_dve")
        rows_act = sem("rows_act")
        zo_ready = sem("zo_ready")
        kw_ready = sem("kw_ready")
        hy_ready = sem("hy_ready")
        m_hi = sem("m_hi")
        merged_ready = sem("merged_ready")
        o_ready = sem("o_ready")
        act_step, dve_step, pool_step = sem("act_step"), sem("dve_step"), sem("pool_step")
        per_layer = [*bank_full, *bank_done, *raw_in, raw_used, split_used, small_in, late_in,
                     stored, var_ready, rstd_ready, xn_ready, u_hi, u_ready, pre_done,
                     q_hi, q_ready, k_hi, k_ready, z_tanh, nm_ready, sink_done, p_ready, pv_even,
                     y_hi, y_ready, gw_ready, rows_dve, rows_act, zo_ready, kw_ready, hy_ready,
                     m_hi, merged_ready, o_ready, act_step, dve_step, pool_step]
        first_in = sem("first_in")
        x_saved = sem("x_saved")
        init_dve, init_act, init_pe = sem("init_dve"), sem("init_act"), sem("init_pe")
        init_pool = sem("init_pool")
        at_end = {n: sem(f"at_end_{n}") for n in ("pe", "act", "dve", "pool")}
        go_on = sem("go_on")

        block = ctx.enter_context(nc.Block())

        def wait_full(eng, key):
            lead, n, _ = psum.use[key]
            eng.wait_ge(bank_full[lead], n)

        def wait_done(eng, key):
            lead, n, _ = psum.use[key]
            eng.wait_ge(bank_done[lead], n)

        def full(key):
            return bank_full[psum.bank(key)], 1

        def done(key):
            return bank_done[psum.bank(key)], 1

        def bank(key, second=0):
            return pb[:, psum.bank(key) + second, :]

        def pair(key, inner):
            b = psum.bank(key)
            return pb[:, b:b + 2, :].rearrange("p b (n i) -> p (b n) i", i=inner)

        def wait_y(eng, bi, br):
            if br == "B":
                for t in range(T):
                    wait_done(eng, ("B", "yT", t))
            else:
                eng.wait_ge(y_ready, T * (bi + 1))

        def meet(eng, name, l):
            eng.drain().then_inc(at_end[name], 1)
            eng.wait_ge(go_on, l + 1)

        def tile_cols(t):
            return slice(t * P, (t + 1) * P)

        @block.sync
        def _(sp):
            sp.dma_start(ident[:, :], consts[:, 0:P]).then_inc(first_in, 16)
            sp.dma_start(rope[:, :, :, :].rearrange("p a t d -> p (a t d)"),
                         consts[:, P:P + 2 * LT * HD]).then_inc(first_in, 16)
            sp.dma_start(cst[:, :, :].rearrange("p a q -> p (a q)"),
                         consts[:, P + 2 * LT * HD:]).then_inc(first_in, 16)
            sp.dma_start(crow[0:KD, 0, :], c.rearrange("a (k p) -> (a k) p", p=P)).then_inc(first_in, 16)
            sp.dma_start(crow[KD:2 * KD, 0, :], c_ctx.rearrange("(k p) -> k p", p=P)).then_inc(first_in, 16)
            sp.dma_start(xh[:, 0:LT, :], x_sample.rearrange("a (t p) d -> p (a t) d", p=P)).then_inc(first_in, 16)
            sp.dma_start(xh[:, LT, :], x_prompt[0, :, :]).then_inc(first_in, 16)
            sp.wait_ge(first_in, 7 * 16)
            sp.dma_start(y_sample.rearrange("a (t p) d -> p (a t) d", p=P), xh[:, 0:LT, :]).then_inc(x_saved, 16)
            sp.dma_start(y_prompt[0, :, :], xh[:, LT, :]).then_inc(x_saved, 16)
            sp.wait_ge(x_saved, 32)
            sp.wait_ge(init_dve, 1)
            sp.wait_ge(init_pool, 3)

            with sp.Fori(0, DEPTH) as l:
                def of_layer(ap, pattern, **k):
                    return ap[bass.ds(l, 1)].rearrange(pattern, **k)

                def load_piece(p):
                    matrix, k, col, width = pieces.items[p]
                    if p >= 3:
                        sp.wait_ge(raw_used, p - 2)
                    rows = slice(k * P, (k + 2) * P)
                    if matrix == "mod":
                        src = w_mod[bass.ds(l, 1), rows, col:col + width]
                    elif matrix == "in":
                        src = w_in[bass.ds(l, 1), rows, col:col + width]
                    elif matrix == "out":
                        src = w_out[bass.ds(l, 1), rows, col:col + width]
                    else:
                        i = matrix[1]
                        src = w_branch[bass.ds(l, 1), i, rows, col:col + width]
                    sp.dma_start(raw[:, p % 3, :, 0:width], src.rearrange("a (k p) n -> p (a k) n", p=P))\
                        .then_inc(raw_in[p % 3], 16)

                def store_kv(i, k_out, v_out):
                    if i == 0:
                        sp.wait_ge(pre_done, T)
                    else:
                        wait_done(sp, ("C", "kv", LT))
                    for which, out in ((0, k_out), (1, v_out)):
                        sp.dma_start(of_layer(out[0], "a v s d -> s (a v) d"),
                                     kvt[:, LT, which, :].rearrange("s (v d) -> s v d", v=KV))\
                            .then_inc(stored, 16)

                for p in range(3):
                    load_piece(p)
                sp.dma_start(bmod[:, :], b_mod[bass.ds(l, 1), :].to_broadcast([2, 3 * D])).then_inc(small_in, 16)
                for i, (k, v) in enumerate(((cache_attn_k, cache_attn_v), (cache_win_k, cache_win_v))):
                    for j, a in enumerate((k, v)):
                        sp.dma_start(cached[:, i, j, :].rearrange("s (v d) -> s v d", v=KV),
                                     of_layer(a[0], "a v s d -> s (a v) d")).then_inc(small_in, 16)
                sp.dma_start(C0[:, :, :, :].rearrange("v a h d -> v (a h) d"),
                             of_layer(state_C[0], "l a h v d -> v (l a h) d")).then_inc(small_in, 16)
                for d in range(2):
                    sp.dma_start(n0[:, d, :], state_n[0, bass.ds(l, 1), d].rearrange(
                        "l (j e) d -> (l e d) j", e=2)).then_inc(small_in, 16)
                    sp.dma_start(mcol[ROW0[d]:ROW0[d] + MH, 3 * d:3 * d + 1],
                                 state_m[0, bass.ds(l, 1), d].rearrange("l h -> h l")).then_inc(small_in, 16)
                    for g in range(2):
                        r = 64 * g + ROW0[d]
                        sp.dma_start(gbias[r:r + MH, 0:1],
                                     gate_bias[bass.ds(l, 1), 2 * d + g].rearrange("l h -> h l"))\
                            .then_inc(small_in, 16)
                sp.dma_start(gains[:, :, :].rearrange("p a d -> p (a d)"),
                             of_layer(qk_gain, "l a d -> l (a d)").to_broadcast([P, 2 * HD])).then_inc(small_in, 16)
                sp.dma_start(sink[:, 0, :],
                             of_layer(sink_logit, "l v g -> l (v g)").to_broadcast([P, NH])).then_inc(small_in, 16)
                sp.dma_start(gwraw[:, :, :], w_in[bass.ds(l, 1), :, COL_B_GATES:COL_B_GATES + 4 * MH]
                             .rearrange("l (k p) n -> p (l k) n", p=P)).then_inc(small_in, 16)
                for p in range(3, NP):
                    if p == pieces.first[("A", "G", 0)]:
                        store_kv(0, new_attn_k, new_attn_v)
                    if p == pieces.first[("C", "G", 0)]:
                        store_kv(1, new_win_k, new_win_v)
                    if p == pieces.first[("out", 0)]:
                        sp.wait_ge(hy_ready, T)
                        wait_full(sp, ("B", "yT", T - 1))
                        sp.dma_start(xh[:, 0:LT, :], y_sample.rearrange("a (t p) d -> p (a t) d", p=P)).then_inc(late_in, 16)
                        sp.dma_start(xh[:, LT, :], y_prompt[0, :, :]).then_inc(late_in, 16)
                        for i, a in enumerate((ln_gain, ln_bias)):
                            sp.dma_start(lnrow[:, i, :], a[bass.ds(l, 1), :].to_broadcast([P, D])).then_inc(late_in, 16)
                        for d in range(2):
                            wait_done(sp, ("B", "CS", CHUNKS.index((d, LT))))
                            sp.dma_start(of_layer(new_C[0], "l a h v d -> l a v h d")[0, d],
                                         co[:, d, 0:256].rearrange("v (h d) -> v h d", h=MH)).then_inc(stored, 16)
                            sp.dma_start(new_n[0, bass.ds(l, 1), d].rearrange("l h d -> l (h d)"),
                                         co[0:1, d, 256:512]).then_inc(stored, 16)
                            sp.dma_start(new_m[0, bass.ds(l, 1), d].rearrange("l h -> h l"),
                                         mcol[ROW0[d]:ROW0[d] + MH, 5:6]).then_inc(stored, 16)
                    load_piece(p)
                for t in range(T):
                    sp.wait_ge(o_ready, t + 1)
                    dst = y_prompt[0, :, :] if t == LT else y_sample[0, tile_cols(t), :]
                    sp.dma_start(dst, xh[:, t, :]).then_inc(stored, 16)
                sp.wait_ge(stored, 16 * (4 + 6 + T))
                for name in at_end:
                    sp.wait_ge(at_end[name], 1)
                for s in (*per_layer, *at_end.values()):
                    sp.sem_clear(s)
                sp.drain().then_inc(go_on, 1)

        @block.gpsimd
        def _(pool):
            pool.memset(half_neg[:, :], -0.5).then_inc(init_pool, 1)
            pool.memset(mcol[:, :], 0.0).then_inc(init_pool, 1)
            pool.memset(gbias[:, :], 0.0).then_inc(init_pool, 1)
            pool.wait_ge(init_pool, 3)
            with pool.Fori(0, DEPTH) as l:
                def inv_sqrt(dst, src, n):
                    pool.wait_ge(var_ready, n)
                    pool.tensor_tensor(dst, src, half_neg[:, 0:src.shape[1]], ALU.pow).then_inc(rstd_ready, 1)

                for p in range(NP):
                    width = pieces.items[p][3]
                    pool.wait_ge(raw_in[p % 3], 16 * (p // 3 + 1))
                    if p - 2 in pieces.last:
                        wait_full(pool, pieces.last[p - 2])
                    elif p >= 2:
                        pool.wait_ge(split_used, pieces.inner[p - 2] + 1)
                    hi, lo = (wsp[:, p % 2, i, :, 0:width] for i in range(2))
                    pool.tensor_copy(hi, raw[:, p % 3, :, 0:width]).then_inc(pool_step, 1)
                    pool.wait_ge(pool_step, p + 1)
                    pool.tensor_tensor(lo, raw[:, p % 3, :, 0:width], hi.bitcast(F32), ALU.subtract)\
                        .then_inc(raw_used, 1)
                    if p == 1:
                        inv_sqrt(rstd[:, :], ve[:, :], 1)
                    if p == pieces.first[("A", "z")] + 1:
                        for t in range(T):
                            inv_sqrt(rms[:, t, :], ms[:, t, :], 2 + t)
                for t in range(T):
                    inv_sqrt(rstd[:, t:t + 1], ve[:, t:t + 1], 2 + T + t)
                meet(pool, "pool", l)

        @block.tensor
        def _(pe):
            pe.wait_ge(init_dve, 2)
            pe.transpose(pb[:, 7, 0:2 * KD], crow[:, 2, :], ident[0:2 * KD, 0:2 * KD]).then_inc(init_pe, 1)
            pe.wait_ge(init_dve, 3)

            with pe.Fori(0, DEPTH) as l:
                def acquire(key):
                    for lead, n in psum.use[key][2]:
                        pe.wait_ge(bank_done[lead], n)

                def product(chunk, lhs, tiles, keys, width=HALF, rows=P):
                    first, count = pieces.first[chunk], pieces.chunk[chunk]
                    for i in range(count):
                        p = first + i
                        pe.wait_ge(raw_used, p + 1)
                        for t in tiles:
                            if i == 0:
                                acquire(keys[t])
                            dst = pb[0:rows, psum.bank(keys[t]), 0:width]
                            for j in range(2):
                                k = 2 * i + j
                                for n, (a, w) in enumerate(((0, 0), (0, 1), (1, 0))):
                                    mm = pe.matmul(dst, lhs(a, k, t), wsp[:, p % 2, w, j, 0:width],
                                                   start=(k == 0 and n == 0),
                                                   stop=(i == count - 1 and j == 1 and n == 2))
                            if i == count - 1 and t != tiles[-1]:
                                mm.then_inc(*full(keys[t]))
                        if i == count - 1:
                            mm.then_inc(*full(keys[tiles[-1]]))
                        else:
                            mm.then_inc(split_used, 1)

                def act_lhs(a, k, t):
                    return act_T[:, a, k, tile_cols(t)]

                def y_lhs(a, k, t):
                    return yT[:, a, k, tile_cols(t)]

                def project(chunk, lhs=act_lhs, width=HALF):
                    product(chunk, lhs, range(T), [(*chunk, t) for t in range(T)], width)

                def transpose_blocks(key, src, n, ready=None):
                    acquire(key)
                    for i in range(n):
                        b = psum.bank(key) + i // 4
                        mm = pe.transpose(pb[:, b, tile_cols(i % 4)], src(i), ident[:, :])
                    mm.then_inc(*full(key))

                for n in range(6):
                    product(("mod", n), lambda a, k, t: csil[:, a, k, :], [0], [("mod", n)], rows=2)
                acquire("modT")
                for n in range(4):
                    wait_done(pe, ("mod", n))
                for i in range(2 * KD):
                    mm = pe.transpose(pb[:, 6, 2 * i:2 * i + 2], modrow[:, tile_cols(i)], ident[0:2, 0:2])
                mm.then_inc(*full("modT"))
                for n in (4, 5):
                    wait_done(pe, ("mod", n))
                for i in range(4):
                    acquire(("gate", i))
                    which, hf = i // 2, i % 2
                    pe.matmul(bank(("gate", i)), ident[0:2, which:which + 1].to_broadcast([2, P]),
                              modrow[:, 2 * D + hf * HALF:2 * D + (hf + 1) * HALF], start=True, stop=True)\
                        .then_inc(*full(("gate", i)))
                for t in range(T):
                    pe.wait_ge(xn_ready, t + 1)
                    transpose_blocks(("xT", t), lambda i: xh[:, t, tile_cols(i)], KD)
                pe.wait_ge(u_ready, T)

                def attention(br):
                    bi = 0 if br == "A" else 1
                    for name, width in (("kv", 256), ("q", HALF), ("z", HALF)):
                        project((br, name), width=width)
                    for t in range(T + 1):
                        if t < T:
                            pe.wait_ge(q_ready, bi * T + t + 1)
                            transpose_blocks((br, "qT", t),
                                             lambda i: tokq[:, t, i, :, :].rearrange("p a d -> p (a d)"), NH)
                        pe.wait_ge(k_ready, bi * (T + 1) + t + 1)
                        transpose_blocks((br, "kT", t), lambda i: ks[:, t % 2, i // 2, i % 2, :, :]
                                         .rearrange("p a d -> p (a d)"), 2 * KV)
                        if t < T:
                            wait_done(pe, (br, "z", t))
                            transpose_blocks((br, "zT", t), lambda i: zt[:, t, tile_cols(i)], 4)
                    for t in range(T + 1):
                        if t < T:
                            wait_done(pe, (br, "qT", t))
                        wait_done(pe, (br, "kT", t))

                    def scores(s):
                        h, t = UNITS[s]
                        kv = h // (NH // KV)
                        key = (br, "S", s)
                        blocks = key_blocks(br, t)
                        own = [b for b in blocks if b < T]
                        n = len(own) * P
                        acquire(key)
                        q = qT[:, h, tile_cols(t)]
                        if T in blocks:
                            dst = pb[:, psum.bank(key) + 1, 0:P] if br == "A" else pb[:, psum.bank(key), n:n + P]
                            for a in range(2):
                                pe.matmul(dst, q, kT[:, kv, a, TOK:TOK + P], start=(a == 0), stop=(a == 1))
                        last = []
                        if br == "C" and t < LT:
                            last = [(own.index(b), m) for b, m in ((t - 1, 1), (t + 1, 2)) if b in own]
                        for a in range(2):
                            mm = pe.matmul(pb[:, psum.bank(key), 0:n], q,
                                           kT[:, kv, a, own[0] * P:own[0] * P + n],
                                           start=(a == 0), stop=(a == 1 and not last))
                        for i, m in last:
                            mm = pe.matmul(pb[:, psum.bank(key), tile_cols(i)], masks[:, 0, :], masks[:, m, :],
                                           start=False, stop=(i == last[-1][0]))
                        mm.then_inc(*full(key))

                    def probs_T(s):
                        h, t = UNITS[s]
                        n = len(key_blocks(br, t))
                        acquire((br, "PT", s))
                        pe.wait_ge(p_ready, bi * len(UNITS) + s + 1)
                        b = psum.bank((br, "PT", s))
                        for i in range(n):
                            mm = pe.transpose(pb[:, b + i // 4, tile_cols(i % 4)], pr[:, s % 3, tile_cols(i)],
                                              ident[:, :])
                        mm.then_inc(*full((br, "PT", s)))

                    def values(h):
                        kv = h // (NH // KV)
                        r = slice((h % 2) * HD, (h % 2 + 1) * HD)
                        j = h // 2
                        if h == 0:
                            acquire((br, "Octx"))
                        if h % 2 == 0:
                            acquire((br, "O", j))
                        wait_done(pe, (br, "PT", UNITS.index((h, LT))))
                        vs = slice(kv * HD, (kv + 1) * HD)
                        mm = pe.matmul(pb[r, psum.bank((br, "Octx")), tile_cols(j)], kvt[:, LT, 1, vs],
                                       pT[:, h % 2, T * HALF:], start=True, stop=True)
                        if h == NH - 1:
                            mm.then_inc(*full((br, "Octx")))
                        o = psum.bank((br, "O", j))
                        pe.matmul(pb[r, o, :], cached[:, bi, 1, vs], pT[:, h % 2, LT * HALF:T * HALF],
                                  start=True, stop=False)
                        for b in range(LT):
                            q0, q1 = (0, LT) if br == "A" else (max(b - 1, 0), min(b + 2, LT))
                            mm = pe.matmul(pb[r, o, q0 * P:q1 * P], kvt[:, b, 1, vs],
                                           pT[:, h % 2, b * HALF + q0 * P:b * HALF + q1 * P],
                                           start=False, stop=(b == LT - 1))
                        if h % 2:
                            mm.then_inc(*full((br, "O", j)))
                        else:
                            mm.then_inc(pv_even, 1)

                    for s in range(len(UNITS) + 3):
                        if s < len(UNITS):
                            scores(s)
                        if 2 <= s < len(UNITS) + 2:
                            probs_T(s - 2)
                        if s >= 3 and UNITS[s - 3][1] == LT:
                            values(UNITS[s - 3][0])

                def mlstm():
                    project(("B", "qk"))
                    project(("B", "v"))
                    pe.wait_ge(gw_ready, 1)
                    for i, cs in enumerate((slice(0, HALF), slice(HALF, TOK))):
                        acquire(("B", "gates", i))
                        for k in range(KD):
                            for n, (a, w) in enumerate(((0, 0), (0, 1), (1, 0))):
                                mm = pe.matmul(pb[:, psum.bank(("B", "gates", i)), 0:cs.stop - cs.start],
                                               gw[:, w, k, :], act_T[:, a, k, cs],
                                               start=(k == 0 and n == 0), stop=(k == KD - 1 and n == 2))
                        mm.then_inc(*full(("B", "gates", i)))
                    project(("B", "o"))
                    for t in range(T):
                        wait_done(pe, ("B", "qk", t))
                        transpose_blocks(("B", "qkT", t), lambda i: tokqk[:, t, i // 2, tile_cols(i % 2)], 4)
                    transpose_blocks(("B", "C0T"), lambda i: C0[:, i // 2, 2 * (i % 2):2 * (i % 2) + 2, :]
                                     .rearrange("v h d -> v (h d)"), 4)
                    project(("B", "z"))
                    pe.wait_ge(rows_act, 4)
                    for t in range(T):
                        acquire(("B", "cols", t))
                        for i, r in enumerate((rw, r1, rb, rf)):
                            mm = pe.transpose(pb[:, psum.bank(("B", "cols", t)), i * GR:(i + 1) * GR],
                                              r[0:GR, tile_cols(t)], ident[0:GR, 0:GR])
                        mm.then_inc(*full(("B", "cols", t)))
                    acquire(("B", "wcb"))
                    for d in range(2):
                        last = r1[0:GR, (P - 1 if d == 0 else 0)::P]
                        for h in range(MH):
                            r = ROW0[d] + h
                            n = (2 * d + h // 2) * T
                            mm = pe.matmul(pb[(h % 2) * HD:(h % 2 + 1) * HD, psum.bank(("B", "wcb")), n:n + T],
                                           ident[0:GR, r:r + 1].to_broadcast([GR, HD]), last,
                                           start=True, stop=True)
                    mm.then_inc(*full(("B", "wcb")))
                    for t in range(T):
                        wait_done(pe, ("B", "qkT", t))
                        wait_done(pe, ("B", "v", t))

                    def scores(k):
                        d, t = CHUNKS[k]
                        acquire(("B", "ST", k))
                        for h in range(MH):
                            r = slice((h % 2) * HD, (h % 2 + 1) * HD)
                            mm = pe.matmul(pb[:, psum.bank(("B", "ST", k)) + h % 2, tile_cols(h // 2)],
                                           kTm[r, h // 2, tile_cols(t)], qTm[r, h // 2, tile_cols(t)],
                                           start=True, stop=True)
                        mm.then_inc(*full(("B", "ST", k)))
                        acquire(("B", "GB", k))
                        b = psum.bank(("B", "GB", k))
                        pe.matmul(pb[:, b, :].rearrange("p (h q) -> p h q", h=MH), masks[:, 0, :],
                                  masks[:, 3 + d, :].unsqueeze(1).to_broadcast([P, MH, P]), start=True, stop=False)
                        for h in range(MH):
                            r = ROW0[d] + h
                            mm = pe.matmul(pb[:, b, tile_cols(h)], ident[0:GR, r:r + 1].to_broadcast([GR, P]),
                                           rg[0:GR, tile_cols(t)], start=False, stop=(h == MH - 1))
                        mm.then_inc(*full(("B", "GB", k)))

                    def outputs(k):
                        d, t = CHUNKS[k]
                        w = DV + 1
                        acquire(("B", "ND", k))
                        wait_done(pe, ("B", "ST", k))
                        for h in range(MH):
                            dst = pb[:, psum.bank(("B", "ND", k)) + h % 2, (h // 2) * 256:(h // 2) * 256 + w]
                            mm = pe.matmul(dst, sT[:, k % 2, h % 2, h // 2, :], v1[:, t, h, :], start=True, stop=True)
                        mm.then_inc(*full(("B", "ND", k)))
                        if t != LT:
                            acquire(("B", "IN", k))
                            wait_done(pe, ("B", "CS", k - 2) if k >= 2 else ("B", "C0T"))
                            for h in range(MH):
                                r = slice((h % 2) * HD, (h % 2 + 1) * HD)
                                dst = pb[:, psum.bank(("B", "IN", k)) + h % 2, (h // 2) * 256:(h // 2) * 256 + w]
                                mm = pe.matmul(dst, qTm[r, h // 2, tile_cols(t)], CT[r, d, h // 2, :],
                                               start=True, stop=True)
                            mm.then_inc(*full(("B", "IN", k)))
                        acquire(("B", "CS", k))
                        pe.wait_ge(kw_ready, k + 1)
                        b = psum.bank(("B", "CS", k))
                        if t != LT:
                            for h in range(MH):
                                r = slice((h % 2) * HD, (h % 2 + 1) * HD)
                                mm = pe.matmul(pb[r, b, (h // 2) * 256:(h // 2) * 256 + w],
                                               kw[:, k % 2, h * HD:(h + 1) * HD], v1[:, t, h, :],
                                               start=True, stop=True)
                        else:
                            for h in range(MH):
                                pe.matmul(pb[:, b, h * HD:(h + 1) * HD], v1[:, t, h, 0:DV],
                                          kw[:, k % 2, h * HD:(h + 1) * HD], start=True, stop=True)
                            mm = pe.matmul(pb[0:1, b, 256:512], ones[:, 0:1], kw[:, k % 2, :],
                                           start=True, stop=True)
                        mm.then_inc(*full(("B", "CS", k)))

                    for t in range(T):
                        wait_done(pe, ("B", "cols", t))
                    for k in range(len(CHUNKS) + 1):
                        if k < len(CHUNKS):
                            scores(k)
                        if k >= 1:
                            outputs(k - 1)
                    for t in range(T):
                        pe.wait_ge(hy_ready, t + 1)
                        transpose_blocks(("B", "yT", t), lambda i: hs[:, t, tile_cols(i)], 4)

                for bi, br in enumerate(MERGE_ORDER):
                    if br == "B":
                        mlstm()
                    else:
                        attention(br)
                    for hf in range(2):
                        project((br, "G", hf))
                        if hf == 0:
                            wait_y(pe, bi, br)
                        project((br, "BR", hf), y_lhs)
                for t in range(T):
                    pe.wait_ge(merged_ready, t + 1)
                    transpose_blocks(("mT", t), lambda i: merged[:, t, tile_cols(i)], KD)
                for t in range(T):
                    wait_done(pe, ("mT", t))
                for hf in range(2):
                    project(("out", hf))
                meet(pe, "pe", l)

        @block.scalar
        def _(act):
            act.wait_ge(first_in, 7 * 16)
            act.activation(crow[:, 1, :], crow[:, 0, :], ACT.Tanh, scale=0.5).then_inc(init_act, 1)
            act.wait_ge(init_pe, 1)
            act.copy(csil[:, 0, :, :].rearrange("p k w -> p w k"),
                     pb[:, 7, 0:2 * KD].rearrange("p (w k) -> p w k", w=2)).then_inc(init_act, 1)

            with act.Fori(0, DEPTH) as l:
                steps = [0]

                def step(ins):
                    steps[0] += 1
                    ins.then_inc(act_step, 1)
                    act.wait_ge(act_step, steps[0])

                for i in range(4):
                    wait_full(act, ("gate", i))
                    act.copy(gate_bc[:, i // 2, (i % 2) * HALF:(i % 2 + 1) * HALF], bank(("gate", i)))\
                        .then_inc(*done(("gate", i)))
                for t in range(T):
                    wait_done(act, ("xT", t))
                    act.copy(act_T[:, 0, :, tile_cols(t)], utmp[:, t % 2, :, :]).then_inc(u_hi, 1)

                def attention(br):
                    bi = 0 if br == "A" else 1
                    if bi:
                        act.wait_ge(stored, 32)
                    for t in range(T):
                        wait_full(act, (br, "kv", t))
                        act.copy(kvt[:, t, :, :].rearrange("p a d -> p (a d)"), bank((br, "kv", t))[:, 0:256])\
                            .then_inc(*done((br, "kv", t)))
                    for t in range(T):
                        wait_full(act, (br, "q", t))
                        act.copy(tokq[:, t, :, 1, :], bank((br, "q", t)).rearrange("p (h d) -> p h d", h=NH))\
                            .then_inc(*done((br, "q", t)))
                    for t in range(T):
                        if br == "C" and t == LT:
                            wait_done(act, (br, "q", t))
                        else:
                            act.wait_ge(pre_done, bi * T + t + 1)
                        act.copy(tokq[:, t, :, 0, :].bitcast(F32R), tokq[:, t, :, 1, :]).then_inc(q_hi, 1)
                    for t in range(T):
                        wait_full(act, (br, "z", t))
                        act.activation(zt[:, t, :], bank((br, "z", t)), ACT.Tanh, scale=0.5).then_inc(z_tanh, 1)
                    for t in range(T + 1):
                        if t >= 2:
                            wait_full(act, (br, "kT", t - 2))
                        src = kvt[:, t, 0, :] if t < T else cached[:, bi, 0, :]
                        if t == T:
                            act.wait_ge(small_in, 16 * 17)
                        act.copy(ks[:, t % 2, :, 0, :, :].bitcast(F32R),
                                 src.rearrange("p (v d) -> p v d", v=KV).unsqueeze(2)
                                 .to_broadcast([P, KV, 2, HD])).then_inc(k_hi, 1)
                        if t >= 1:
                            wait_full(act, (br, "qT", t - 1))
                            act.copy(qT[:, :, tile_cols(t - 1)], pair((br, "qT", t - 1), P))\
                                .then_inc(*done((br, "qT", t - 1)))
                    wait_full(act, (br, "zT", T - 1))
                    wait_full(act, (br, "kT", T))

                    def exponent(s):
                        h, t = UNITS[s]
                        n = len(key_blocks(br, t)) * P
                        act.wait_ge(nm_ready, bi * len(UNITS) + s + 1)
                        if s >= 3:
                            wait_full(act, (br, "PT", s - 3))
                        b = psum.bank((br, "S", s))
                        src = pb[:, b:b + 2, :].rearrange("p b n -> p (b n)")[:, 0:n]
                        if br == "C":
                            act.activation(sexp[:, s % 4:s % 4 + 1], sink[:, 0, h:h + 1], ACT.Exp,
                                           bias=nm[:, s % 4:s % 4 + 1]).then_inc(sink_done, 1)
                        act.activation(pr[:, s % 3, 0:n], src, ACT.Exp, bias=nm[:, s % 4:s % 4 + 1], scale=SCALE,
                                       accum_out=lsum[:, s % 4:s % 4 + 1]).then_inc(*done((br, "S", s)))

                    def evacuate_PT(s):
                        h, t = UNITS[s]
                        key = (br, "PT", s)
                        blocks = key_blocks(br, t)
                        wait_full(act, key)
                        if h >= 2 and t == 0:
                            if h % 2:
                                wait_full(act, (br, "O", (h - 2) // 2))
                            else:
                                act.wait_ge(pv_even, bi * (NH // 2) + h // 2)
                        src = pair(key, P)
                        if t == LT:
                            act.copy(pT[:, h % 2, T * HALF:], src[:, 0, :]).then_inc(*done(key))
                            return
                        dst = pT[:, h % 2, 0:T * HALF].rearrange("p (b q) -> p b q", b=T)[:, :, tile_cols(t)]
                        if br == "A":
                            act.copy(dst, src[:, 0:T, :]).then_inc(*done(key))
                        else:
                            n = len(blocks) - 1
                            act.copy(dst[:, blocks[0]:blocks[0] + n, :], src[:, 0:n, :])
                            act.copy(dst[:, LT, :], src[:, n, :]).then_inc(*done(key))

                    for s in range(len(UNITS) + 4):
                        if s < len(UNITS):
                            exponent(s)
                        if 2 <= s < len(UNITS) + 2:
                            evacuate_PT(s - 2)
                        if s >= 4 and UNITS[s - 4][1] == LT and UNITS[s - 4][0] % 2:
                            j = UNITS[s - 4][0] // 2
                            wait_done(act, (br, "O", j))
                            act.copy(yT[:, 0, j, 0:HALF], ytmp[:, :]).then_inc(y_hi, 1)
                    wait_done(act, (br, "Octx"))
                    act.copy(yT[:, 0, :, HALF:TOK], ytmp[:, :].rearrange("p (j q) -> p j q", j=4)).then_inc(y_hi, 1)

                def mlstm():
                    for t in range(T):
                        wait_full(act, ("B", "qk", t))
                        src = bank(("B", "qk", t))
                        act.copy(tokqk[:, t, 0, :], src[:, 0:256])
                        act.mul(tokqk[:, t, 1, :], src[:, 256:512], SCALE).then_inc(*done(("B", "qk", t)))
                    act.wait_ge(rows_dve, 1)
                    act.activation(r1[0:GR, :], r1[0:GR, :], ACT.Exp).then_inc(rows_act, 1)
                    act.wait_ge(rows_act, 1)
                    act.activation(r1[0:GR, :], r1[0:GR, :], ACT.Ln, bias=1.0).then_inc(rows_act, 1)
                    for t in range(T):
                        wait_full(act, ("B", "o", t))
                        act.activation(zo[:, t, :], bank(("B", "o", t)), ACT.Tanh, scale=0.5)\
                            .then_inc(*done(("B", "o", t)))
                    for t in range(T):
                        wait_full(act, ("B", "qkT", t))
                        src = bank(("B", "qkT", t)).rearrange("p (a j q) -> p a j q", a=2, j=2)
                        act.copy(qTm[:, :, tile_cols(t)], src[:, 0])
                        act.copy(kTm[:, :, tile_cols(t)], src[:, 1]).then_inc(*done(("B", "qkT", t)))
                    act.wait_ge(rows_dve, 2)
                    act.activation(r1[0:GR, :], r1[0:GR, :], ACT.Exp, scale=-1.0)
                    act.activation(rb[0:GR, :], rb[0:GR, :], ACT.Exp, scale=-1.0).then_inc(rows_act, 1)
                    act.activation(rf[0:GR, :], rf[0:GR, :], ACT.Exp).then_inc(rows_act, 1)
                    for t in range(T):
                        wait_full(act, ("B", "z", t))
                        if t >= 2:
                            act.wait_ge(zo_ready, t - 1)
                        act.activation(em[:, t % 2, :, :].rearrange("p b n -> p (b n)"), bank(("B", "z", t)), ACT.Tanh,
                                       scale=0.5).then_inc(z_tanh, 1)
                    for k, (d, t) in enumerate(CHUNKS):
                        wait_full(act, ("B", "GB", k))
                        wait_done(act, ("B", "cols", T - 1))
                        if k == 0:
                            act.wait_ge(zo_ready, T)
                        if k >= 2:
                            wait_done(act, ("B", "ST", k - 2))
                        b = psum.bank(("B", "GB", k))
                        for h in range(MH):
                            ins = act.activation(em[:, k % 2, h % 2, tile_cols(h // 2)], pb[:, b, tile_cols(h)], ACT.Exp,
                                                 bias=cols[:, t, 0, ROW0[d] + h:ROW0[d] + h + 1], scale=-1.0)
                        ins.then_inc(*done(("B", "GB", k)))
                    for t in range(T):
                        wait_full(act, ("B", "yT", t))
                        act.copy(yT[:, 0, :, tile_cols(t)], bank(("B", "yT", t)).rearrange("p (j q) -> p j q", j=4))\
                            .then_inc(y_hi, 1)

                for bi, br in enumerate(MERGE_ORDER):
                    if br == "B":
                        mlstm()
                    else:
                        attention(br)
                    for hf in range(2):
                        for t in range(T):
                            wait_full(act, (br, "G", hf, t))
                            if hf == 0 and t == 0:
                                wait_y(act, bi, br)
                            elif hf:
                                wait_done(act, (br, "BR", 0, t))
                            act.activation(tg[:, t, :], bank((br, "G", hf, t)), ACT.Tanh, scale=0.5)\
                                .then_inc(*done((br, "G", hf, t)))
                for t in range(T):
                    wait_full(act, ("mT", t))
                    act.mul(act_T[:, 0, :, tile_cols(t)], pair(("mT", t), P), 0.5).then_inc(m_hi, 1)
                meet(act, "act", l)

        @block.vector
        def _(dve):
            dve.wait_ge(first_in, 7 * 16)
            dve.memset(ones[:, :], 1.0)
            dve.tensor_copy(masks[:, 1:5, :], cst[:, :, :])
            dve.tensor_copy(masks[:, 0, :], ident[:, :]).then_inc(init_dve, 1)
            dve.wait_ge(init_act, 1)
            dve.scalar_tensor_tensor(out=crow[:, 2, :], in0=crow[:, 1, :], scalar=1.0, in1=crow[:, 0, :],
                                     op0=ALU.add, op1=ALU.mult).then_inc(init_dve, 1)
            dve.wait_ge(init_act, 2)
            dve.tensor_tensor(csil[:, 1, :, :].rearrange("p k w -> p w k"),
                              pb[:, 7, 0:2 * KD].rearrange("p (w k) -> p w k", w=2),
                              csil[:, 0, :, :].rearrange("p k w -> p w k").bitcast(F32), ALU.subtract)\
                .then_inc(init_dve, 1)

            with dve.Fori(0, DEPTH) as l:
                steps = [0]

                def step(ins):
                    steps[0] += 1
                    ins.then_inc(dve_step, 1)
                    dve.wait_ge(dve_step, steps[0])

                for t in range(T):
                    for i in range(2):
                        ins = dve.bn_stats(out=stats[:, t, i, :], in_=xh[:, t, i * HALF:(i + 1) * HALF])
                step(ins)
                for t in range(T):
                    ins = dve.bn_aggr(out=mv[:, t, :], in_=stats[:, t, :, :].rearrange("p a b -> p (a b)"))
                step(ins)
                dve.tensor_scalar(ve[:, :], mv[:, :, 1], EPS, None, ALU.add).then_inc(var_ready, 1)
                dve.wait_ge(small_in, 16 * 17)
                for n in range(6):
                    wait_full(dve, ("mod", n))
                    cs = slice(n * HALF, (n + 1) * HALF)
                    dve.scalar_tensor_tensor(out=modrow[:, cs], in0=pb[0:2, psum.bank(("mod", n)), :], scalar=0.5,
                                             in1=bmod[:, cs], op0=ALU.mult, op1=ALU.add)\
                        .then_inc(*done(("mod", n)))
                    if n == 0:
                        dve.wait_ge(rstd_ready, 1)
                        for t in range(T):
                            dve.tensor_scalar(xh[:, t, :], xh[:, t, :], mv[:, t, 0:1], rstd[:, t:t + 1],
                                              ALU.subtract, ALU.mult).then_inc(xn_ready, 1)
                wait_full(dve, "modT")
                src = bank("modT")[:, 0:4 * KD].rearrange("p (k w) -> p k w", w=2)
                dve.tensor_copy(modc[:, 0:KD, :], src[:, 0:KD, :])
                dve.tensor_scalar(modc[:, KD:2 * KD, :], src[:, KD:2 * KD, :], 1.0, None, ALU.add)\
                    .then_inc(*done("modT"))
                wait_done(dve, "modT")

                def u_lo(t):
                    dve.wait_ge(u_hi, t + 1)
                    dve.tensor_tensor(act_T[:, 1, :, tile_cols(t)], utmp[:, t % 2, :, :],
                                      act_T[:, 0, :, tile_cols(t)].bitcast(F32), ALU.subtract).then_inc(u_ready, 1)

                for t in range(T):
                    w = 1 if t == LT else 0
                    wait_full(dve, ("xT", t))
                    if t >= 2:
                        dve.wait_ge(u_ready, t - 1)
                    src = pair(("xT", t), P)
                    for k in range(KD):
                        ins = dve.tensor_scalar(utmp[:, t % 2, k, :], src[:, k, :], modc[:, KD + k, w:w + 1],
                                                modc[:, k, w:w + 1], ALU.mult, ALU.add)
                    ins.then_inc(*done(("xT", t)))
                    if t:
                        u_lo(t - 1)
                u_lo(T - 1)

                def attention(br):
                    bi = 0 if br == "A" else 1
                    if br == "C":
                        step(dve.tensor_scalar(sink[:, 1, :], sink[:, 0, :], -1.0, None, ALU.mult))
                    if br == "A":
                        for t in range(T):
                            wait_done(dve, (br, "kv", t))
                            wait_done(dve, (br, "q", t))
                            q, k = tokq[:, t, :, 1, :], kvt[:, t, 0, :]
                            dve.tensor_tensor(rtmp[:, 0:512].rearrange("p (h d) -> p h d", h=NH), q, q, ALU.mult)
                            step(dve.tensor_tensor(rtmp[:, 512:640], k, k, ALU.mult))
                            step(dve.tensor_reduce(ms[:, t, :], rtmp[:, :].rearrange("p (h d) -> p h d", d=HD),
                                                   AX.X, ALU.add))
                            dve.tensor_scalar(ms[:, t, :], ms[:, t, :], 1.0 / HD, EPS, ALU.mult, ALU.add)\
                                .then_inc(var_ready, 1)

                    def q_lo(t):
                        dve.wait_ge(q_hi, bi * T + t + 1)
                        dve.tensor_tensor(tokq[:, t, :, 1, :], tokq[:, t, :, 1, :], tokq[:, t, :, 0, :],
                                          ALU.subtract).then_inc(q_ready, 1)

                    for t in range(T):
                        q = tokq[:, t, :, 1, :]
                        k = kvt[:, t, 0, :].rearrange("p (v d) -> p v d", v=KV)
                        if br == "A":
                            dve.wait_ge(rstd_ready, 2 + t)
                            dve.tensor_tensor(q, q, rms[:, t, 0:NH].unsqueeze(2).to_broadcast([P, NH, HD]), ALU.mult)
                            step(dve.tensor_tensor(k, k, rms[:, t, NH:NH + KV].unsqueeze(2)
                                                   .to_broadcast([P, KV, HD]), ALU.mult))
                            dve.tensor_tensor(q, q, gains[:, 0, :].unsqueeze(1).to_broadcast([P, NH, HD]), ALU.mult)
                            ins = dve.tensor_tensor(k, k, gains[:, 1, :].unsqueeze(1).to_broadcast([P, KV, HD]),
                                                    ALU.mult)
                            if t < LT:
                                step(ins)
                            else:
                                ins.then_inc(pre_done, 1)
                        else:
                            wait_done(dve, (br, "kv", t))
                            wait_done(dve, (br, "q", t))
                        if t < LT:
                            if t:
                                dve.wait_ge(pre_done, bi * T + t)
                            for x, n, o in ((q, NH, 0), (k, KV, NH * HD)):
                                tmp = rtmp[:, o:o + n * HD].rearrange("p (n a i) -> p n a i", n=n, a=4)
                                x4 = x.rearrange("p n (a i) -> p n a i", a=4)
                                sn = rope[:, 1, t, :].rearrange("p (a i) -> p a i", a=4)
                                for a in range(2):
                                    ins = dve.tensor_tensor(tmp[:, :, a::2, :], x4[:, :, 1 - a::2, :],
                                                      sn[:, a::2, :].unsqueeze(1).to_broadcast([P, n, 2, 16]),
                                                      ALU.mult)
                            step(ins)
                            for x, n in ((q, NH), (k, KV)):
                                ins = dve.tensor_tensor(x, x, rope[:, 0, t, :].unsqueeze(1)
                                                        .to_broadcast([P, n, HD]), ALU.mult)
                            step(ins)
                            dve.tensor_tensor(q, q, rtmp[:, 0:512].rearrange("p (n d) -> p n d", n=NH), ALU.add)
                            dve.tensor_tensor(k, k, rtmp[:, 512:640].rearrange("p (n d) -> p n d", n=KV), ALU.add)\
                                .then_inc(pre_done, 1)
                        if t:
                            q_lo(t - 1)
                    q_lo(T - 1)
                    for t in range(T):
                        dve.wait_ge(z_tanh, bi * T + t + 1)
                        dve.scalar_tensor_tensor(out=zt[:, t, :], in0=zt[:, t, :], scalar=1.0,
                                                 in1=bank((br, "z", t)), op0=ALU.add, op1=ALU.mult)\
                            .then_inc(*done((br, "z", t)))
                    for t in range(T + 1):
                        dve.wait_ge(k_hi, bi * (T + 1) + t + 1)
                        src = (kvt[:, t, 0, :] if t < T else cached[:, bi, 0, :]).rearrange("p (v d) -> p v d", v=KV)
                        for e in range(2):
                            ins = dve.tensor_tensor(ks[:, t % 2, :, 1, e, :], src, ks[:, t % 2, :, 0, e, :],
                                                    ALU.subtract)
                        ins.then_inc(k_ready, 1)
                        if t >= 1:
                            evacuate_kz(br, t - 1)
                    evacuate_kz(br, T)

                    def maximum(s):
                        h, t = UNITS[s]
                        n = len(key_blocks(br, t)) * P
                        wait_full(dve, (br, "S", s))
                        b = psum.bank((br, "S", s))
                        src = pb[:, b:b + 2, :].rearrange("p b n -> p (b n)")[:, 0:n]
                        o = slice(s % 4, s % 4 + 1)
                        step(dve.tensor_reduce(nmx[:, o], src, AX.X, ALU.max, negate=True))
                        if br == "A":
                            dve.tensor_scalar(nm[:, o], nmx[:, o], SCALE, None, ALU.mult).then_inc(nm_ready, 1)
                        else:
                            dve.tensor_scalar(nm[:, o], nmx[:, o], SCALE, sink[:, 1, h:h + 1], ALU.mult, ALU.min)\
                                .then_inc(nm_ready, 1)

                    def normalise(s):
                        h, t = UNITS[s]
                        n = len(key_blocks(br, t)) * P
                        o = slice(s % 4, s % 4 + 1)
                        wait_done(dve, (br, "S", s))
                        total = lsum
                        if br == "C":
                            dve.wait_ge(sink_done, s + 1)
                            step(dve.tensor_tensor(den[:, o], lsum[:, o], sexp[:, o], ALU.add))
                            total = den
                        step(dve.reciprocal(rden[:, o], total[:, o]))
                        dve.tensor_scalar(pr[:, s % 3, 0:n], pr[:, s % 3, 0:n], rden[:, o], None, ALU.mult)\
                            .then_inc(p_ready, 1)

                    def gate_out(j):
                        key = (br, "O", j)
                        wait_full(dve, key)
                        if j:
                            dve.wait_ge(y_ready, bi * T + j)
                        dve.scalar_tensor_tensor(out=ytmp[:, :], in0=bank(key), scalar=0.5, in1=zT[:, j, 0:HALF],
                                                 op0=ALU.mult, op1=ALU.mult).then_inc(*done(key))

                    def y_lo(j):
                        dve.wait_ge(y_hi, bi * T + j + 1)
                        cs = slice(0, HALF)
                        dve.tensor_tensor(yT[:, 1, j, cs], ytmp[:, :], yT[:, 0, j, cs].bitcast(F32), ALU.subtract)\
                            .then_inc(y_ready, 1)

                    for s in range(len(UNITS) + 5):
                        if s < len(UNITS):
                            maximum(s)
                        if 1 <= s < len(UNITS) + 1:
                            normalise(s - 1)
                        if 4 <= s < len(UNITS) + 4 and UNITS[s - 4][1] == LT and UNITS[s - 4][0] % 2:
                            gate_out(UNITS[s - 4][0] // 2)
                        if s >= 5 and s - 5 < len(UNITS) and UNITS[s - 5][1] == LT and UNITS[s - 5][0] % 2:
                            y_lo(UNITS[s - 5][0] // 2)
                    key = (br, "Octx")
                    wait_full(dve, key)
                    dve.wait_ge(y_ready, bi * T + LT)
                    dve.scalar_tensor_tensor(out=ytmp[:, :].rearrange("p (j q) -> p j q", j=4),
                                             in0=bank(key).rearrange("p (j q) -> p j q", j=4), scalar=0.5,
                                             in1=zT[:, :, HALF:TOK], op0=ALU.mult, op1=ALU.mult)\
                        .then_inc(*done(key))
                    dve.wait_ge(y_hi, (bi + 1) * T)
                    dve.tensor_tensor(yT[:, 1, :, HALF:TOK], ytmp[:, :].rearrange("p (j q) -> p j q", j=4),
                                      yT[:, 0, :, HALF:TOK].bitcast(F32), ALU.subtract).then_inc(y_ready, 1)

                def evacuate_kz(br, t):
                    wait_full(dve, (br, "kT", t))
                    dve.tensor_copy(kT[:, :, :, tile_cols(t)].rearrange("p v a q -> p (v a) q"),
                                    bank((br, "kT", t)).rearrange("p (v q) -> p v q", v=4))\
                        .then_inc(*done((br, "kT", t)))
                    if t < T:
                        wait_full(dve, (br, "zT", t))
                        dve.tensor_copy(zT[:, :, tile_cols(t)], bank((br, "zT", t)).rearrange("p (j q) -> p j q", j=4))\
                            .then_inc(*done((br, "zT", t)))

                def mlstm():
                    wait_full(dve, ("C", "BR", 1, T - 1))
                    step(dve.memset(gw[:, :, :, :].rearrange("p a k n -> p (a k n)").bitcast(F32), 0.0))
                    for d in range(2):
                        for g in range(2):
                            o = 64 * g + ROW0[d]
                            ins = dve.tensor_copy(gw[:, 0, :, o:o + MH], gwraw[:, :, (2 * d + g) * MH:(2 * d + g + 1) * MH])
                    step(ins)
                    for d in range(2):
                        for g in range(2):
                            o = 64 * g + ROW0[d]
                            ins = dve.tensor_tensor(gw[:, 1, :, o:o + MH],
                                                    gwraw[:, :, (2 * d + g) * MH:(2 * d + g + 1) * MH],
                                                    gw[:, 0, :, o:o + MH].bitcast(F32), ALU.subtract)
                    ins.then_inc(gw_ready, 1)
                    dve.memset(v1[:, :, :, DV:DV + 1], 1.0)
                    dve.memset(rb[0:GR, :], 0.0)
                    step(dve.memset(rg[0:GR, :], 0.0))
                    for t in range(T):
                        wait_full(dve, ("B", "v", t))
                        dve.tensor_copy(v1[:, t, :, 0:DV], bank(("B", "v", t)).rearrange("p (h d) -> p h d", h=MH))\
                            .then_inc(*done(("B", "v", t)))
                    for i, cs in enumerate((slice(0, HALF), slice(HALF, TOK))):
                        wait_full(dve, ("B", "gates", i))
                        b, n = psum.bank(("B", "gates", i)), cs.stop - cs.start
                        dve.tensor_scalar(rw[0:GR, cs], pb[0:GR, b, 0:n], gbias[0:GR, 0:1], None, ALU.add)
                        dve.tensor_scalar(rf[0:GR, cs], pb[64:64 + GR, b, 0:n], gbias[64:64 + GR, 0:1], None,
                                          ALU.add).then_inc(*done(("B", "gates", i)))
                    wait_done(dve, ("B", "gates", 1))
                    dve.scalar_tensor_tensor(out=r1[0:GR, :], in0=rf[0:GR, :], scalar=-1.0, in1=rf[0:GR, :],
                                             op0=ALU.mult, op1=ALU.min)\
                        .then_inc(rows_dve, 1)
                    dve.wait_ge(rows_act, 2)
                    step(dve.scalar_tensor_tensor(out=rf[0:GR, :], in0=rf[0:GR, :], scalar=0.0, in1=r1[0:GR, :],
                                                  op0=ALU.min, op1=ALU.subtract))

                    def along(row, d, t):
                        a = row[ROW0[d]:ROW0[d] + MH, tile_cols(t)]
                        return a if d == 0 else a[:, ::-1]

                    for d in range(2):
                        for t in range(T):
                            ins = dve.tensor_tensor_scan(along(rb, d, t), ones[ROW0[d]:ROW0[d] + MH, :],
                                                         along(rf, d, t), 0.0, ALU.mult, ALU.add)
                    step(ins)
                    step(dve.tensor_tensor(rw[0:GR, :], rw[0:GR, :], rb[0:GR, :], ALU.subtract))
                    for n, (d, t) in enumerate(CHUNKS):
                        r = slice(ROW0[d], ROW0[d] + MH)
                        last = t * P + (P - 1 if d == 0 else 0)
                        step(dve.tensor_tensor_scan(along(rg, d, t), along(rw, d, t), along(rw, d, t),
                                                    mcol[r, t:t + 1], ALU.max, ALU.max))
                        to = 5 if t == LT else t + (1 if d == 0 else -1)
                        if t == LT or 0 <= to < LT:
                            step(dve.tensor_tensor(mcol[r, to:to + 1], rb[r, last:last + 1], rg[r, last:last + 1],
                                                   ALU.add))
                    tiles = lambda row: row[0:GR, :].rearrange("p (t q) -> p t q", t=T)
                    dve.tensor_tensor(tiles(r1), tiles(rg), mcol[0:GR, 0:T].unsqueeze(2).to_broadcast([GR, T, P]),
                                      ALU.subtract)
                    dve.tensor_tensor(rb[0:GR, :], rb[0:GR, :], rg[0:GR, :], ALU.add)
                    for d in range(2):
                        r = slice(ROW0[d], ROW0[d] + MH)
                        g3 = rg[r, :].rearrange("p (t q) -> p t q", t=T)[:, :, (P - 1 if d == 0 else 0)]
                        ins = dve.tensor_tensor(rf[r, :].rearrange("p (t q) -> p t q", t=T),
                                                rw[r, :].rearrange("p (t q) -> p t q", t=T),
                                                g3.unsqueeze(2).to_broadcast([MH, T, P]), ALU.subtract)
                    ins.then_inc(rows_dve, 1)
                    wait_full(dve, ("B", "C0T"))
                    for d in range(2):
                        dve.tensor_copy(CT[:, d, :, DV:DV + 1], n0[:, d, :].unsqueeze(2))
                    dve.tensor_copy(CT[:, :, :, 0:DV].rearrange("p a j v -> p (a j) v"),
                                    bank(("B", "C0T")).rearrange("p (a v) -> p a v", a=4))\
                        .then_inc(*done(("B", "C0T")))
                    for t in range(T):
                        dve.wait_ge(z_tanh, 2 * T + t + 1)
                        z = em[:, t % 2, :, :].rearrange("p b n -> p (b n)")
                        dve.scalar_tensor_tensor(out=z, in0=z, scalar=1.0,
                                                 in1=bank(("B", "z", t)), op0=ALU.add, op1=ALU.mult)\
                            .then_inc(*done(("B", "z", t)))
                        wait_done(dve, ("B", "o", t))
                        wait_done(dve, ("B", "z", t))
                        dve.scalar_tensor_tensor(out=zo[:, t, :], in0=zo[:, t, :], scalar=1.0,
                                                 in1=z, op0=ALU.add, op1=ALU.mult)\
                            .then_inc(zo_ready, 1)
                    for t in range(T):
                        wait_full(dve, ("B", "cols", t))
                        dve.tensor_copy(cols[:, t, :, :].rearrange("p a r -> p (a r)"),
                                        bank(("B", "cols", t))[:, 0:4 * GR]).then_inc(*done(("B", "cols", t)))
                    wait_full(dve, ("B", "wcb"))
                    dve.tensor_copy(wcb[:, :, :].rearrange("p a t -> p (a t)"), bank(("B", "wcb"))[:, 0:4 * T])\
                        .then_inc(*done(("B", "wcb")))
                    wait_done(dve, ("B", "wcb"))

                    def col(k, i):
                        d, t = CHUNKS[k]
                        return cols[:, t, i, ROW0[d]:ROW0[d] + MH]

                    def by_head(a, n):
                        return a.rearrange("p (j b) -> p b j", b=2).unsqueeze(3).to_broadcast([P, 2, 2, n])

                    def decayed(k):
                        d, t = CHUNKS[k]
                        wait_done(dve, ("B", "cols", t))
                        if k >= 2:
                            wait_full(dve, ("B", "CS", k - 2))
                        dve.tensor_tensor(kw[:, k % 2, :].rearrange("p (h d) -> p h d", h=MH),
                                          tokqk[:, t, 1, :].rearrange("p (h d) -> p h d", h=MH),
                                          col(k, 3).unsqueeze(2).to_broadcast([P, MH, HD]), ALU.mult)\
                            .then_inc(kw_ready, 1)
                        wait_full(dve, ("B", "ST", k))
                        wait_done(dve, ("B", "GB", k))
                        dve.tensor_tensor(sT[:, k % 2, :, :, :].rearrange("p b j q -> p b (j q)"),
                                          pb[:, 0:2, 0:2 * P], em[:, k % 2, :, :], ALU.mult).then_inc(*done(("B", "ST", k)))

                    seen = set()

                    def combine(k):
                        d, t = CHUNKS[k]
                        b = psum.bank(("B", "ND", k))
                        wide = lambda b: pb[:, b:b + 2, :].rearrange("p b (n i) -> p b n i", i=256)[:, :, :, 0:DV + 1]
                        out = nd[:, k % 2, :, :, :]
                        if t != LT:
                            wait_full(dve, ("B", "IN", k))
                            dve.tensor_tensor(t3[:, :, :, :], wide(psum.bank(("B", "IN", k))),
                                              by_head(col(k, 1), DV + 1), ALU.mult)\
                                .then_inc(*done(("B", "IN", k)))
                            wait_done(dve, ("B", "IN", k))
                            wait_full(dve, ("B", "ND", k))
                            dve.tensor_tensor(out, wide(b), t3[:, :, :, :], ALU.add).then_inc(*done(("B", "ND", k)))
                        else:
                            wait_full(dve, ("B", "ND", k))
                            dve.tensor_copy(out, wide(b)).then_inc(*done(("B", "ND", k)))
                        wait_full(dve, ("B", "CS", k))
                        if t != LT:
                            C = CT[:, d, :, :]
                            step(dve.tensor_tensor(C, C, wcb[:, 2 * d:2 * d + 2, t:t + 1]
                                                   .to_broadcast([P, 2, DV + 1]), ALU.mult))
                            dve.tensor_tensor(C, bank(("B", "CS", k)).rearrange("p (j v) -> p j v", j=2)[:, :, 0:DV + 1],
                                              C, ALU.add).then_inc(*done(("B", "CS", k)))
                        else:
                            dve.tensor_copy(co[:, d, 0:256], bank(("B", "CS", k))[:, 0:256])
                            dve.tensor_copy(co[0:1, d, 256:512], pb[0:1, psum.bank(("B", "CS", k)), 256:512])\
                                .then_inc(*done(("B", "CS", k)))
                        wait_done(dve, ("B", "ND", k))
                        dk, rk = dn[:, k % 2, :, :], rdn[:, k % 2, :, :]
                        step(dve.scalar_tensor_tensor(out=dk, in0=out[:, :, :, DV], scalar=-1.0,
                                                      in1=col(k, 2).rearrange("p (j b) -> p b j", b=2),
                                                      op0=ALU.mult, op1=ALU.max))
                        step(dve.tensor_tensor(dk, dk, out[:, :, :, DV], ALU.max))
                        step(dve.reciprocal(rk, dk))
                        dst = hs[:, t, :] if t not in seen else t4[:, :]
                        step(dve.tensor_tensor(dst.rearrange("p (j b v) -> p b j v", j=2, b=2), out[:, :, :, 0:DV],
                                               rk.unsqueeze(3).to_broadcast([P, 2, 2, DV]), ALU.mult))
                        if t in seen:
                            step(dve.tensor_tensor(hs[:, t, :], hs[:, t, :], t4[:, :], ALU.add))
                        seen.add(t)

                    for k in range(len(CHUNKS) + 1):
                        if k < len(CHUNKS):
                            decayed(k)
                        if k >= 1:
                            combine(k - 1)
                    for t in range(T):
                        dve.scalar_tensor_tensor(out=hs[:, t, :], in0=hs[:, t, :], scalar=0.25, in1=zo[:, t, :],
                                                 op0=ALU.mult, op1=ALU.mult).then_inc(hy_ready, 1)
                    for t in range(T):
                        dve.wait_ge(y_hi, 2 * T + t + 1)
                        dve.tensor_tensor(yT[:, 1, :, tile_cols(t)],
                                          bank(("B", "yT", t)).rearrange("p (j q) -> p j q", j=4),
                                          yT[:, 0, :, tile_cols(t)].bitcast(F32), ALU.subtract)\
                            .then_inc(*done(("B", "yT", t)))

                for bi, br in enumerate(MERGE_ORDER):
                    if br == "B":
                        mlstm()
                    else:
                        attention(br)
                    for hf in range(2):
                        cs = slice(hf * HALF, (hf + 1) * HALF)
                        for t in range(T):
                            key = (br, "BR", hf, t)
                            wait_full(dve, key)
                            wait_done(dve, (br, "G", hf, t))
                            dst = merged[:, t, cs] if bi == 0 else mt[:, t % 2, :]
                            dve.scalar_tensor_tensor(out=dst, in0=tg[:, t, :], scalar=1.0, in1=bank(key),
                                                     op0=ALU.add, op1=ALU.mult).then_inc(*done(key))
                            if bi:
                                wait_done(dve, key)
                                ins = dve.tensor_tensor(merged[:, t, cs], merged[:, t, cs], mt[:, t % 2, :], ALU.add)
                                if br == MERGE_ORDER[-1] and hf == 1:
                                    ins.then_inc(merged_ready, 1)
                                else:
                                    step(ins)
                for t in range(T):
                    dve.wait_ge(m_hi, t + 1)
                    dve.scalar_tensor_tensor(out=act_T[:, 1, :, tile_cols(t)], in0=pair(("mT", t), P), scalar=0.5,
                                             in1=act_T[:, 0, :, tile_cols(t)].bitcast(F32), op0=ALU.mult,
                                             op1=ALU.subtract).then_inc(*done(("mT", t)))
                dve.wait_ge(late_in, 64)
                for hf in range(2):
                    cs = slice(hf * HALF, (hf + 1) * HALF)
                    for t in range(T):
                        key = ("out", hf, t)
                        wait_full(dve, key)
                        if hf == 0 and t == 0:
                            for i in range(4):
                                wait_done(dve, ("gate", i))
                        dve.tensor_tensor(ot[:, t % 2, :], bank(key), gate_bc[:, 1 if t == LT else 0, cs], ALU.mult)\
                            .then_inc(*done(key))
                        wait_done(dve, key)
                        step(dve.scalar_tensor_tensor(out=xh[:, t, cs], in0=xh[:, t, cs], scalar=ALPHA,
                                                      in1=ot[:, t % 2, :], op0=ALU.mult, op1=ALU.add))
                        if hf == 1:
                            for i in range(2):
                                ins = dve.bn_stats(out=stats[:, t, i, :], in_=xh[:, t, i * HALF:(i + 1) * HALF])
                            step(ins)
                            step(dve.bn_aggr(out=mv[:, t, :], in_=stats[:, t, :, :].rearrange("p a b -> p (a b)")))
                            dve.tensor_scalar(ve[:, t:t + 1], mv[:, t, 1:2], EPS, None, ALU.add)\
                                .then_inc(var_ready, 1)
                for t in range(T):
                    dve.wait_ge(rstd_ready, 2 + T + t)
                    step(dve.tensor_scalar(xh[:, t, :], xh[:, t, :], mv[:, t, 0:1], rstd[:, t:t + 1],
                                           ALU.subtract, ALU.mult))
                    step(dve.tensor_tensor(xh[:, t, :], xh[:, t, :], lnrow[:, 0, :], ALU.mult))
                    dve.tensor_tensor(xh[:, t, :], xh[:, t, :], lnrow[:, 1, :], ALU.add).then_inc(o_ready, 1)
                meet(dve, "dve", l)


def shape_constants():
    import numpy as np
    grid_w, axis = 64, HD // 2
    pos = np.arange(LT * P)
    inv = (10000.0 ** (-np.arange(0, axis, 2, dtype=np.float32) / axis)).astype(np.float32)
    ar = (pos // grid_w).astype(np.float32)[:, None] * inv
    ac = (pos % grid_w).astype(np.float32)[:, None] * inv
    ang = np.concatenate([ar, ar, ac, ac], axis=-1)
    sign = np.repeat(np.array([-1, 1, -1, 1], np.float32), 16)
    tables = [np.cos(ang), np.sin(ang) * sign]
    i = np.arange(P)
    row, col = i[:, None], i[None, :]
    big = np.float32(1e30)
    masks = [np.where(col >= row, 0, -big),
             np.where(col <= row, 0, -big),
             np.where(row <= col, 0, big),
             np.where(row >= col, 0, big)]
    parts = [np.eye(P)]
    parts += [t.reshape(LT, P, HD).transpose(1, 0, 2).reshape(P, LT * HD) for t in tables]
    parts += masks
    return np.concatenate(parts, axis=1).astype(np.float32)


_INS = ["x_prompt", "x_sample", "cache_attn_k", "cache_attn_v", "cache_win_k", "cache_win_v",
        "state_mlstm_C", "state_mlstm_n", "state_mlstm_m", "c", "c_ctx", "w_mod", "b_mod", "w_in",
        "qk_gain", "sink_logit", "mlstm_gate_bias", "w_branch", "w_out", "ln_gain", "ln_bias"]
_OUTS = [(1, P, D), (1, LT * P, D), (1, DEPTH, KV, P, HD), (1, DEPTH, KV, P, HD), (1, DEPTH, KV, P, HD),
         (1, DEPTH, KV, P, HD), (1, DEPTH, 2, MH, DV, HD), (1, DEPTH, 2, MH, HD), (1, DEPTH, 2, MH)]


def kernel(**inputs):
    import numpy as _np
    import concourse.bacc as _bacc
    from concourse.bass_utils import run_bass_kernel_spmd as _run

    nc = _bacc.Bacc("TRN2", target_bir_lowering=False, num_devices=1)
    arrays, args = {}, []
    for name in _INS:
        arrays[f"in_{name}"] = _np.ascontiguousarray(inputs[name])
    arrays["in_consts"] = shape_constants()
    for name, a in arrays.items():
        args.append(nc.dram_tensor(name, a.shape, mybir.dt.from_np(a.dtype), kind="ExternalInput").ap())
    for i, shape in enumerate(_OUTS):
        args.append(nc.dram_tensor(f"out_{i}", shape, F32, kind="ExternalOutput").ap())
    trunk_kernel(nc, *args)
    r = _run(nc, [arrays], core_ids=[0])
    return tuple(r.results[0][f"out_{i}"] for i in range(len(_OUTS)))
```

```python
from contextlib import ExitStack

import concourse.bass as bass
from concourse import mybir

F32 = mybir.dt.float32
F32R = mybir.dt.float32r
BF16 = mybir.dt.bfloat16
ALU = mybir.AluOpType
ACT = mybir.ActivationFunctionType
AX = mybir.AxisListType

P = 128
DEPTH = 2
D = 1024
KD = D // P
LT = 4
T = LT + 1
TOK = T * P
HD = 64
NH = 8
KV = 2
MH = 4
DV = 128
BW = 512
HALF = 512
SCALE = HD ** -0.5
EPS = 1e-6
ALPHA = (2.0 * DEPTH) ** 0.25

COL_A = 0
COL_B = COL_A + NH * HD + 2 * KV * HD + BW
COL_B_GATES = COL_B + 2 * MH * HD + 2 * MH * DV
COL_C = COL_B_GATES + 4 * MH + BW
COL_G = COL_C + NH * HD + 2 * KV * HD + BW
BRANCH = {"A": 0, "B": 1, "C": 2}
MERGE_ORDER = ("A", "C", "B")

CHUNKS = [(0, 0), (1, 3), (0, 1), (1, 2), (0, 2), (1, 1), (0, 3), (1, 0), (0, LT), (1, LT)]
ROW0 = (0, 32)
GR = 36

UNITS = [(h, t) for h in range(NH) for t in range(T)]

PV_AFTER = T + 2


def key_blocks(branch, t):
    if t == LT:
        return [LT]
    if branch == "A":
        return list(range(LT)) + [T]
    return [b for b in (t - 1, t, t + 1) if 0 <= b < LT] + [T]


class Pieces:

    def __init__(self):
        self.items = []
        self.first = {}
        self.chunk = {}
        self.last = {}
        self.inner = []
        self.loaded = []
        self.splits = []
        self.order = {}

    def add(self, key, matrix, blocks, *columns):
        self.first[key] = len(self.items)
        self.chunk[key] = blocks // 2
        for k in range(0, blocks, 2):
            p = len(self.items)
            same = [q for q in range(p) if (self.items[q][0] == "mod") == (matrix == "mod")]
            self.inner.append(sum(q not in self.last for q in same))
            self.loaded.append(16 * len(columns) + (self.loaded[p - 3] if p >= 3 else 0))
            if matrix != "mod":
                self.order[p] = len(self.splits)
                self.splits.append(p)
            self.items.append((matrix, k, columns))
        self.last[len(self.items) - 1] = key if key[0] == "mod" else (*key, T - 1)


class PsumPlan:

    def __init__(self):
        self.count = [0] * 8
        self.last = [None] * 8
        self.use = {}
        self.rolling = 0

    def take(self, key, *banks):
        before = sorted({self.last[b] for b in banks if self.last[b]})
        lead = banks[0]
        self.count[lead] += 1
        for b in banks:
            self.last[b] = (lead, self.count[lead])
        self.use[key] = (lead, self.count[lead], before)

    def roll(self, key):
        self.take(key, self.rolling % 8)
        self.rolling += 1

    def bank(self, key):
        return self.use[key][0]


def plan_layer():
    pieces, psum = Pieces(), PsumPlan()
    def modulation(c):
        pieces.add(("mod", c), "mod", KD, (c * HALF, HALF))

    for c in range(4):
        modulation(c)
        psum.take(("mod", c), c)
    psum.take("modT", 6)
    for t in range(T):
        b = 2 * (t % 3)
        psum.take(("xT", t), b, b + 1)
    pieces.add(("kv",), "in", KD, *((base + NH * HD, 2 * KV * HD) for base in (COL_A, COL_C)))
    for t in range(T):
        psum.roll(("kv", t))
    for br in MERGE_ORDER:
        if br != "B":
            base = COL_A if br == "A" else COL_C
            for name, col in (("q", 0), ("z", NH * HD + 2 * KV * HD)):
                pieces.add((br, name), "in", KD, (base + col, HALF))
                for t in range(T):
                    psum.roll((br, name, t))
            if br == "C":
                for c in (4, 5):
                    modulation(c)
            for t in range(T + 1):
                e = t % 2
                if t < T:
                    psum.take((br, "qT", t), 2 * e, 2 * e + 1)
                psum.take((br, "kT", t), 4 + e)
                if t < T:
                    psum.take((br, "zT", t), 6 + e)
            for s in range(len(UNITS) + PV_AFTER):
                if s < len(UNITS):
                    psum.take((br, "S", s), *((2 * (s % 2), 2 * (s % 2) + 1) if br == "A" else (s % 3,)))
                if 2 <= s < len(UNITS) + 2:
                    psum.take((br, "PT", s - 2), *((4, 5) if br == "A" else (3 + s % 2,)))
                if br == "C" and s in (0, KD):
                    psum.take(("mod", 4 + s // KD), 6)
                v = s - PV_AFTER
                if v == 0:
                    psum.take((br, "Octx"), 7)
                if v >= 0 and v % (2 * T) == 0:
                    j = v // (2 * T)
                    psum.take((br, "O", j), 6 if br == "A" else 5)
            if br == "C":
                for i in range(4):
                    psum.roll(("gate", i))
        else:
            for name, col in (("qk", 0), ("v", 512), ("gates", None), ("o", 1024),
                              ("T", None), ("z", COL_B_GATES + 4 * MH - COL_B)):
                if name == "gates":
                    psum.roll(("B", "gates", 0))
                    psum.roll(("B", "gates", 1))
                elif name == "T":
                    for t in range(T):
                        psum.roll(("B", "qkT", t))
                    psum.roll(("B", "C0T"))
                else:
                    pieces.add(("B", name), "in", KD, (COL_B + col, HALF))
                    for t in range(T):
                        psum.roll(("B", name, t))
            for t in range(T):
                psum.take(("B", "cols", t), t % 2)
            psum.take(("B", "wcb"), 2)
            for k in range(len(CHUNKS) + 1):
                if k < len(CHUNKS):
                    psum.take(("B", "ST", k), 0, 1)
                    psum.take(("B", "GB", k), 2 + k % 2)
                if k >= 1:
                    d, t = CHUNKS[k - 1]
                    psum.take(("B", "ND", k - 1), 4, 5)
                    if t != LT:
                        psum.take(("B", "IN", k - 1), 6, 7)
                    psum.take(("B", "CS", k - 1), 2 + (k - 1) % 2)
            for t in range(T):
                psum.take(("B", "yT", t), t % 2)
        for hf in range(2):
            i = BRANCH[br]
            pieces.add((br, "G", hf), "in", KD, (COL_G + i * D + hf * HALF, HALF))
            pieces.add((br, "BR", hf), ("branch", i), BW // P, (hf * HALF, HALF))
            for name in ("G", "BR"):
                for t in range(T):
                    psum.roll((br, name, hf, t))
    for t in range(T):
        b = 2 * (t % 3)
        psum.take(("mT", t), b, b + 1)
    for hf in range(2):
        pieces.add(("out", hf), "out", KD, (hf * HALF, HALF))
        for t in range(T):
            psum.roll(("out", hf, t))
    return pieces, psum


def trunk_kernel(nc, x_prompt, x_sample, cache_attn_k, cache_attn_v, cache_win_k, cache_win_v,
                 state_C, state_n, state_m, c, c_ctx, w_mod, b_mod, w_in, qk_gain, sink_logit,
                 gate_bias, w_branch, w_out, ln_gain, ln_bias, consts,
                 y_prompt, y_sample, new_attn_k, new_attn_v, new_win_k, new_win_v,
                 new_C, new_n, new_m):
    pieces, psum = plan_layer()
    NP = len(pieces.items)

    ctx = ExitStack()
    with ctx:
        ctx.enter_context(nc.allow_non_contiguous_dma(reason="states and columns of a few elements"))
        place = [0]
        base = nc.sbuf_base + (-nc.sbuf_base) % 64

        def at(name, shape, dt, offset):
            return nc.alloc_sbuf_tensor_at(name, shape, dt, offset=base + offset)

        def fixed(name, shape, dt, size=4):
            n = size
            for s in shape[1:]:
                n *= s
            n += -n % 32
            where = place[0]
            place[0] += n
            return at(name, shape, dt, where)

        def sem(name):
            return ctx.enter_context(nc.semaphore(name))

        act_T = fixed("act_T", [P, 2, KD, TOK], F32R)
        raw = fixed("raw", [P, 3, 2, HALF], F32)
        wsp = fixed("wsp", [P, 2, 2, 2, HALF], F32R)
        merged = fixed("merged", [P, T, D], F32)
        gate_at = place[0]
        gate_bc = fixed("gate_bc", [P, 2, D], F32)
        kv2 = at("kv2", [P, T, 2, KV * HD], F32, gate_at)
        ident = fixed("ident", [P, P], F32)
        rope = fixed("rope", [P, 2, LT, HD], F32)
        masks = fixed("masks", [P, 5, P], BF16, 2)
        ones = fixed("ones", [P, P], F32)
        cached = fixed("cached", [P, 2, 2, KV * HD], F32)
        C0 = fixed("C0", [P, 2, MH, HD], F32)
        n0 = fixed("n0", [P, 2, 2], F32)
        gains = fixed("gains", [P, 2, HD], F32)
        sink = fixed("sink", [P, 2, NH], F32)
        modc = fixed("modc", [P, 2 * KD, 2], F32)
        csil = fixed("csil", [P, KD, 2], F32)
        crow = fixed("crow", [2 * KD, 3, P], F32)
        gwraw = fixed("gwraw", [P, KD, 4 * MH], F32)
        gbias = fixed("gbias", [P, 1], F32)
        mcol = fixed("mcol", [P, 8], F32)
        half_neg = fixed("half_neg", [P, 16], F32)
        stats = fixed("stats", [P, T, 2, 6], F32)
        mv = fixed("mv", [P, T, 2], F32)
        ve = fixed("ve", [P, T], F32)
        rstd = fixed("rstd", [P, T], F32)
        ms = fixed("ms", [P, T, 10], F32)
        rms = fixed("rms", [P, T, 10], F32)
        nmx = fixed("nmx", [P, 4], F32)
        nm = fixed("nm", [P, 4], F32)
        lsum = fixed("lsum", [P, 4], F32)
        sexp = fixed("sexp", [P, 4], F32)
        den = fixed("den", [P, 4], F32)
        rden = fixed("rden", [P, 4], F32)
        dn = fixed("dn", [P, 2, 2, 2], F32)
        rdn = fixed("rdn", [P, 2, 2, 2], F32)
        wcb = fixed("wcb", [P, 4, T], F32)
        y_at = place[0]
        place[0] += 2 * 4 * TOK * 4
        yT = at("yT", [P, 2, 4, TOK], F32R, y_at)
        tokq = at("tokq", [P, T, NH, 2, HD], F32, y_at)
        tokqk = at("tokqk", [P, T, 2, MH * HD], F32, y_at)
        gw = at("gw", [P, 2, KD, P], F32R, y_at + T * 2048)
        kw = at("kw", [P, 2, MH * HD], F32, y_at + T * 2048 + 2 * KD * P * 4)
        arena = place[0]
        xh = at("xh", [P, T, D], F32, arena)
        modrow = at("modrow", [2, 2 * D], F32, arena + 20480)
        bmod = at("bmod", [2, 2 * D], F32, arena + 32768)
        utmp = at("utmp", [P, 2, KD, P], F32, arena + 45056)
        lnrow = at("lnrow", [P, 2, D], F32, arena + 44544)
        ot = at("ot", [P, 2, HALF], F32, arena + 52736)
        cst = at("cst", [P, 4, P], F32, arena + 53248)
        kvt = at("kvt", [P, T, 2, KV * HD], F32, arena)
        pr = at("pr", [P, 3, T * P], F32, arena + 5120)
        zt = at("zt", [P, T, HALF], F32, arena + 29696)
        zT = at("zT", [P, 4, TOK], F32, arena + 12800)
        pT = at("pT", [P, 2, T * HALF + P], F32, arena + 23040)
        rtmp = at("rtmp", [P, 640], F32, arena + 23040)
        ks = at("ks", [P, 2, KV, 2, 2, HD], F32, arena + 25600)
        ytmp = at("ytmp", [P, HALF], F32, arena + 44544)
        qT = at("qT", [P, NH, TOK], F32R, arena + 46592)
        kT = at("kT", [P, KV, 2, TOK + P], F32R, arena + 67072)
        grow = at("grow", [2, D], F32, arena)
        tg = at("tg", [P, T, HALF], F32, arena + 23040)
        mt = at("mt", [P, 2, HALF], F32, arena + 33280)
        v1 = at("v1", [P, T, MH, DV + 1], F32, arena)
        zo = at("zo", [P, T, HALF], F32, arena + 10336)
        hs = at("hs", [P, T, HALF], F32, arena + 20576)
        qTm = at("qTm", [P, 2, TOK], F32, arena + 30816)
        kTm = at("kTm", [P, 2, TOK], F32, arena + 35936)
        cols = at("cols", [P, T, 4, GR], F32, arena + 41056)
        em = at("em", [P, 2, 2, 2 * P], F32, arena + 43936)
        sT = at("sT", [P, 2, 2, 2, P], F32, arena + 48032)
        nd = at("nd", [P, 2, 2, 2, DV + 1], F32, arena + 52128)
        t3 = at("t3", [P, 2, 2, DV + 1], F32, arena + 56256)
        CT = at("CT", [P, 2, 2, DV + 1], F32, arena + 58336)
        rw, rf, rb, rg, r1 = (at(n, [P, TOK], F32, arena + 60416 + 2560 * i)
                              for i, n in enumerate(("rw", "rf", "rb", "rg", "r1")))
        co = at("co", [P, 2, HALF], F32, arena + 60416)
        t4 = at("t4", [P, HALF], F32, arena + 73216)

        pb = ctx.enter_context(nc.psum_tensor("pb", [P, 8, HALF], F32))

        bank_full = [sem(f"bank_full{b}") for b in range(8)]
        bank_done = [sem(f"bank_done{b}") for b in range(8)]
        raw_in = [sem(f"raw_in{i}") for i in range(3)]
        raw_used = sem("raw_used")
        mod_used = sem("mod_used")
        split_used = sem("split_used")
        small_in = sem("small_in")
        bgate_in = sem("bgate_in")
        late_in = sem("late_in")
        stored = sem("stored")
        var_ready = sem("var_ready")
        rstd_ready = sem("rstd_ready")
        xn_ready = sem("xn_ready")
        u_half = sem("u_half")
        u_ready = sem("u_ready")
        pre_done = sem("pre_done")
        q_hi = sem("q_hi")
        q_ready = sem("q_ready")
        k_hi = sem("k_hi")
        k_ready = sem("k_ready")
        z_tanh = sem("z_tanh")
        nm_ready = sem("nm_ready")
        sink_done = sem("sink_done")
        p_ready = sem("p_ready")
        pv_even = sem("pv_even")
        y_hi = sem("y_hi")
        y_ready = sem("y_ready")
        gw_ready = sem("gw_ready")
        rows_dve = sem("rows_dve")
        rows_act = sem("rows_act")
        zo_ready = sem("zo_ready")
        kw_ready = sem("kw_ready")
        hy_ready = sem("hy_ready")
        m_hi = sem("m_hi")
        merged_ready = sem("merged_ready")
        centred = sem("centred")
        scaled = sem("scaled")
        o_ready = sem("o_ready")
        context_ready = sem("context_ready")
        act_step, dve_step, pool_step = sem("act_step"), sem("dve_step"), sem("pool_step")
        per_layer = [*bank_full, *bank_done, *raw_in, raw_used, mod_used, split_used, small_in, bgate_in, late_in,
                     stored, var_ready, rstd_ready, xn_ready, u_half, u_ready, pre_done,
                     q_hi, q_ready, k_hi, k_ready, z_tanh, nm_ready, sink_done, p_ready, pv_even,
                     y_hi, y_ready, gw_ready, rows_dve, rows_act, zo_ready, kw_ready, hy_ready,
                     m_hi, merged_ready, centred, scaled, o_ready, context_ready, act_step, dve_step, pool_step]
        c_in = sem("c_in")
        first_in = sem("first_in")
        x_saved = sem("x_saved")
        init_dve, init_act, init_pe = sem("init_dve"), sem("init_act"), sem("init_pe")
        init_pool = sem("init_pool")
        at_end = {n: sem(f"at_end_{n}") for n in ("pe", "act", "dve", "pool")}
        go_on = sem("go_on")

        block = ctx.enter_context(nc.Block())

        def wait_full(eng, key):
            lead, n, _ = psum.use[key]
            eng.wait_ge(bank_full[lead], n)

        def wait_done(eng, key):
            lead, n, _ = psum.use[key]
            eng.wait_ge(bank_done[lead], n)

        def full(key):
            return bank_full[psum.bank(key)], 1

        def done(key):
            return bank_done[psum.bank(key)], 1

        def bank(key, second=0):
            return pb[:, psum.bank(key) + second, :]

        def pair(key, inner):
            b = psum.bank(key)
            return pb[:, b:b + 2, :].rearrange("p b (n i) -> p (b n) i", i=inner)

        def wait_y(eng, bi, br):
            if br == "B":
                for t in range(T):
                    wait_done(eng, ("B", "yT", t))
            else:
                eng.wait_ge(y_ready, T * (bi + 1))

        def meet(eng, name, l):
            eng.drain().then_inc(at_end[name], 1)
            eng.wait_ge(go_on, l + 1)

        def tile_cols(t):
            return slice(t * P, (t + 1) * P)

        @block.sync
        def _(sp):
            sp.dma_start(crow[0:KD, 0, :], c.rearrange("a (k p) -> (a k) p", p=P)).then_inc(c_in, 16)
            sp.dma_start(crow[KD:2 * KD, 0, :], c_ctx.rearrange("(k p) -> k p", p=P)).then_inc(c_in, 16)
            sp.dma_start(ident[:, :], consts[:, 0:P]).then_inc(c_in, 16)
            sp.dma_start(xh[:, 0:LT, :], x_sample.rearrange("a (t p) d -> p (a t) d", p=P)).then_inc(first_in, 16)
            sp.dma_start(xh[:, LT, :], x_prompt[0, :, :]).then_inc(first_in, 16)
            sp.dma_start(rope[:, :, :, :].rearrange("p a t d -> p (a t d)"),
                         consts[:, P:P + 2 * LT * HD]).then_inc(first_in, 16)
            sp.dma_start(cst[:, :, :].rearrange("p a q -> p (a q)"),
                         consts[:, P + 2 * LT * HD:]).then_inc(first_in, 16)
            sp.dma_start(y_sample[0, :, :], x_sample[0, :, :]).then_inc(x_saved, 16)
            sp.dma_start(y_prompt[0, :, :], x_prompt[0, :, :]).then_inc(x_saved, 16)
            sp.wait_ge(init_pool, 3)

            with sp.Fori(0, DEPTH) as l:
                def of_layer(ap, pattern, **k):
                    return ap[bass.ds(l, 1)].rearrange(pattern, **k)

                def load_piece(p):
                    matrix, k, columns = pieces.items[p]
                    if p - 3 in pieces.order:
                        sp.wait_ge(raw_used, pieces.order[p - 3] + 1)
                    elif p - 3 in pieces.last:
                        wait_full(sp, pieces.last[p - 3])
                    elif p >= 3:
                        sp.wait_ge(mod_used, pieces.inner[p - 3] + 1)
                    rows = slice(k * P, (k + 2) * P)
                    at_col = 0
                    for col, width in columns:
                        if matrix == "mod":
                            src = w_mod[bass.ds(l, 1), rows, col:col + width]
                        elif matrix == "in":
                            src = w_in[bass.ds(l, 1), rows, col:col + width]
                        elif matrix == "out":
                            src = w_out[bass.ds(l, 1), rows, col:col + width]
                        else:
                            src = w_branch[bass.ds(l, 1), matrix[1], rows, col:col + width]
                        sp.dma_start(raw[:, p % 3, :, at_col:at_col + width],
                                     src.rearrange("a (k p) n -> p (a k) n", p=P)).then_inc(raw_in[p % 3], 16)
                        at_col += width

                def store_kv(i, k_out, v_out):
                    if i == 0:
                        sp.wait_ge(pre_done, T)
                    else:
                        wait_done(sp, ("kv", LT))
                    for which, out in ((0, k_out), (1, v_out)):
                        sp.dma_start(of_layer(out[0], "a v s d -> s (a v) d"),
                                     (kvt, kv2)[i][:, LT, which, :].rearrange("s (v d) -> s v d", v=KV))\
                            .then_inc(stored, 16)

                for p in range(3):
                    load_piece(p)
                sp.dma_start(bmod[:, :], b_mod[bass.ds(l, 1), 0:2 * D].to_broadcast([2, 2 * D])).then_inc(small_in, 16)
                for i, (k, v) in enumerate(((cache_attn_k, cache_attn_v), (cache_win_k, cache_win_v))):
                    for j, a in enumerate((k, v)):
                        sp.dma_start(cached[:, i, j, :].rearrange("s (v d) -> s v d", v=KV),
                                     of_layer(a[0], "a v s d -> s (a v) d")).then_inc(small_in, 16)
                sp.dma_start(C0[:, :, :, :].rearrange("v a h d -> v (a h) d"),
                             of_layer(state_C[0], "l a h v d -> v (l a h) d")).then_inc(small_in, 16)
                for d in range(2):
                    sp.dma_start(n0[:, d, :], state_n[0, bass.ds(l, 1), d].rearrange(
                        "l (j e) d -> (l e d) j", e=2)).then_inc(small_in, 16)
                    sp.dma_start(mcol[ROW0[d]:ROW0[d] + MH, 3 * d:3 * d + 1],
                                 state_m[0, bass.ds(l, 1), d].rearrange("l h -> h l")).then_inc(small_in, 16)
                    for g in range(2):
                        r = 64 * g + ROW0[d]
                        sp.dma_start(gbias[r:r + MH, 0:1],
                                     gate_bias[bass.ds(l, 1), 2 * d + g].rearrange("l h -> h l"))\
                            .then_inc(small_in, 16)
                sp.dma_start(gains[:, :, :].rearrange("p a d -> p (a d)"),
                             of_layer(qk_gain, "l a d -> l (a d)").to_broadcast([P, 2 * HD])).then_inc(small_in, 16)
                sp.dma_start(sink[:, 0, :],
                             of_layer(sink_logit, "l v g -> l (v g)").to_broadcast([P, NH])).then_inc(small_in, 16)
                sp.dma_start(gwraw[:, :, :], w_in[bass.ds(l, 1), :, COL_B_GATES:COL_B_GATES + 4 * MH]
                             .rearrange("l (k p) n -> p (l k) n", p=P)).then_inc(small_in, 16)
                for p in range(3, NP):
                    if p == pieces.first[("A", "G", 0)]:
                        store_kv(0, new_attn_k, new_attn_v)
                    if p == pieces.first[("C", "q")]:
                        wait_full(sp, ("A", "Octx"))
                        wait_full(sp, ("A", "O", NH // 2 - 1))
                        sp.wait_ge(stored, 32)
                        sp.dma_start(grow[:, :], b_mod[bass.ds(l, 1), 2 * D:3 * D].to_broadcast([2, D]))\
                            .then_inc(bgate_in, 16)
                    if p == pieces.first[("C", "G", 0)]:
                        store_kv(1, new_win_k, new_win_v)
                    if p == pieces.first[("out", 0)]:
                        sp.wait_ge(hy_ready, T)
                        wait_full(sp, ("B", "yT", T - 1))
                        sp.wait_ge(x_saved, 32)
                        sp.dma_start(xh[:, 0:LT, :], y_sample.rearrange("a (t p) d -> p (a t) d", p=P)).then_inc(late_in, 16)
                        sp.dma_start(xh[:, LT, :], y_prompt[0, :, :]).then_inc(late_in, 16)
                        for i, a in enumerate((ln_gain, ln_bias)):
                            sp.dma_start(lnrow[:, i, :], a[bass.ds(l, 1), :].to_broadcast([P, D])).then_inc(late_in, 16)
                        for d in range(2):
                            wait_done(sp, ("B", "CS", CHUNKS.index((d, LT))))
                            sp.dma_start(of_layer(new_C[0], "l a h v d -> l a v h d")[0, d],
                                         co[:, d, 0:256].rearrange("v (h d) -> v h d", h=MH)).then_inc(stored, 16)
                            sp.dma_start(new_n[0, bass.ds(l, 1), d].rearrange("l h d -> l (h d)"),
                                         co[0:1, d, 256:512]).then_inc(stored, 16)
                            sp.dma_start(new_m[0, bass.ds(l, 1), d].rearrange("l h -> h l"),
                                         mcol[ROW0[d]:ROW0[d] + MH, 5:6]).then_inc(stored, 16)
                    load_piece(p)
                for t in range(T):
                    if t == LT:
                        sp.wait_ge(context_ready, 1)
                    else:
                        sp.wait_ge(o_ready, t + 1)
                    dst = y_prompt[0, :, :] if t == LT else y_sample[0, tile_cols(t), :]
                    sp.dma_start(dst, xh[:, t, :]).then_inc(stored, 16)
                sp.wait_ge(stored, 16 * (4 + 6 + T))
                for name in at_end:
                    sp.wait_ge(at_end[name], 1)
                for s in (*per_layer, *at_end.values()):
                    sp.sem_clear(s)
                sp.drain().then_inc(go_on, 1)

        @block.gpsimd
        def _(pool):
            pool.memset(half_neg[:, :], -0.5).then_inc(init_pool, 1)
            pool.memset(mcol[:, :], 0.0).then_inc(init_pool, 1)
            pool.memset(gbias[:, :], 0.0).then_inc(init_pool, 1)
            pool.wait_ge(init_pool, 3)
            with pool.Fori(0, DEPTH) as l:
                def inv_sqrt(dst, src, n):
                    pool.wait_ge(var_ready, n)
                    pool.tensor_tensor(dst, src, half_neg[:, 0:src.shape[1]], ALU.pow).then_inc(rstd_ready, 1)

                inv_sqrt(rstd[:, :], ve[:, :], 1)
                for i, p in enumerate(pieces.splits):
                    width = sum(w for _, w in pieces.items[p][2])
                    pool.wait_ge(raw_in[p % 3], pieces.loaded[p])
                    if i >= 2:
                        before = pieces.splits[i - 2]
                        if before in pieces.last:
                            wait_full(pool, pieces.last[before])
                        else:
                            pool.wait_ge(split_used, pieces.inner[before] + 1)
                    hi, lo = (wsp[:, i % 2, a, :, 0:width] for a in range(2))
                    pool.tensor_copy(hi, raw[:, p % 3, :, 0:width]).then_inc(pool_step, 1)
                    pool.wait_ge(pool_step, i + 1)
                    pool.tensor_tensor(lo, raw[:, p % 3, :, 0:width], hi.bitcast(F32), ALU.subtract)\
                        .then_inc(raw_used, 1)
                    if p == pieces.first[("A", "z")] + 1:
                        for t in range(T):
                            inv_sqrt(rms[:, t, :], ms[:, t, :], 2 + t)
                for t in range(T):
                    inv_sqrt(rstd[:, t:t + 1], ve[:, t:t + 1], 2 + T + t)
                    if t < LT:
                        pool.wait_ge(late_in, 64)
                        pool.wait_ge(scaled, t + 1)
                        pool.tensor_tensor(xh[:, t, :], xh[:, t, :], lnrow[:, 1, :], ALU.add).then_inc(o_ready, 1)
                meet(pool, "pool", l)

        @block.tensor
        def _(pe):
            pe.wait_ge(init_dve, 1)
            pe.transpose(pb[:, 7, 0:2 * KD], crow[:, 2, :], ident[0:2 * KD, 0:2 * KD]).then_inc(init_pe, 1)
            pe.wait_ge(init_act, 2)

            with pe.Fori(0, DEPTH) as l:
                def acquire(key):
                    for lead, n in psum.use[key][2]:
                        pe.wait_ge(bank_done[lead], n)

                def modulation(n, k):
                    key = ("mod", n)
                    p = pieces.first[key] + k // 2
                    if k == 0:
                        acquire(key)
                    if k % 2 == 0:
                        pe.wait_ge(raw_in[p % 3], pieces.loaded[p])
                    mm = pe.matmul(pb[0:2, psum.bank(key), :], csil[:, k, :], raw[:, p % 3, k % 2, :],
                                   start=(k == 0), stop=(k == KD - 1))
                    if k == KD - 1:
                        mm.then_inc(*full(key))
                    elif k % 2:
                        mm.then_inc(mod_used, 1)

                def product(chunk, lhs, keys, width=HALF, tile_ready=None):
                    first, count = pieces.first[chunk], pieces.chunk[chunk]
                    for i in range(count):
                        piece = pieces.order[first + i]
                        pe.wait_ge(raw_used, piece + 1)
                        for t in range(T):
                            if i == 0:
                                acquire(keys[t])
                                if tile_ready:
                                    tile_ready(t)
                            dst = pb[:, psum.bank(keys[t]), 0:width]
                            for j in range(2):
                                k = 2 * i + j
                                for n, (a, w) in enumerate(((0, 0), (0, 1), (1, 0))):
                                    mm = pe.matmul(dst, lhs(a, k, t), wsp[:, piece % 2, w, j, 0:width],
                                                   start=(k == 0 and n == 0),
                                                   stop=(i == count - 1 and j == 1 and n == 2))
                            if i == count - 1:
                                mm.then_inc(*full(keys[t]))
                        if i < count - 1:
                            mm.then_inc(split_used, 1)

                def act_lhs(a, k, t):
                    return act_T[:, a, k, tile_cols(t)]

                def y_lhs(a, k, t):
                    return yT[:, a, k, tile_cols(t)]

                def project(chunk, lhs=act_lhs, width=HALF, tile_ready=None):
                    product(chunk, lhs, [(*chunk, t) for t in range(T)], width, tile_ready)

                def transpose_blocks(key, src, n, ready=None):
                    acquire(key)
                    for i in range(n):
                        b = psum.bank(key) + i // 4
                        mm = pe.transpose(pb[:, b, tile_cols(i % 4)], src(i), ident[:, :])
                    mm.then_inc(*full(key))

                for n in range(4):
                    for k in range(KD):
                        modulation(n, k)
                acquire("modT")
                for n in range(4):
                    wait_done(pe, ("mod", n))
                for i in range(2 * KD):
                    mm = pe.transpose(pb[:, 6, 2 * i:2 * i + 2], modrow[:, tile_cols(i)], ident[0:2, 0:2])
                mm.then_inc(*full("modT"))
                for t in range(T):
                    pe.wait_ge(xn_ready, t + 1)
                    transpose_blocks(("xT", t), lambda i: xh[:, t, tile_cols(i)], KD)

                project(("kv",), tile_ready=lambda t: pe.wait_ge(u_ready, t + 1))

                def gates():
                    for n in (4, 5):
                        wait_done(pe, ("mod", n))
                    for i in range(4):
                        acquire(("gate", i))
                        which, hf = i // 2, i % 2
                        pe.matmul(bank(("gate", i)), ident[0:2, which:which + 1].to_broadcast([2, P]),
                                  grow[:, hf * HALF:(hf + 1) * HALF], start=True, stop=True)\
                            .then_inc(*full(("gate", i)))

                def attention(br):
                    bi = 0 if br == "A" else 1
                    kv_of = kvt if br == "A" else kv2
                    for name in ("q", "z"):
                        project((br, name))
                    for t in range(T + 1):
                        if t < T:
                            pe.wait_ge(q_ready, bi * T + t + 1)
                            transpose_blocks((br, "qT", t),
                                             lambda i: tokq[:, t, i, :, :].rearrange("p a d -> p (a d)"), NH)
                        pe.wait_ge(k_ready, bi * (T + 1) + t + 1)
                        transpose_blocks((br, "kT", t), lambda i: ks[:, t % 2, i // 2, i % 2, :, :]
                                         .rearrange("p a d -> p (a d)"), 2 * KV)
                        if t < T:
                            wait_done(pe, (br, "z", t))
                            transpose_blocks((br, "zT", t), lambda i: zt[:, t, tile_cols(i)], 4)
                    for t in range(T + 1):
                        if t < T:
                            wait_done(pe, (br, "qT", t))
                        wait_done(pe, (br, "kT", t))

                    def scores(s):
                        h, t = UNITS[s]
                        kv = h // (NH // KV)
                        key = (br, "S", s)
                        blocks = key_blocks(br, t)
                        own = [b for b in blocks if b < T]
                        n = len(own) * P
                        acquire(key)
                        q = qT[:, h, tile_cols(t)]
                        if T in blocks:
                            dst = pb[:, psum.bank(key) + 1, 0:P] if br == "A" else pb[:, psum.bank(key), n:n + P]
                            for a in range(2):
                                pe.matmul(dst, q, kT[:, kv, a, TOK:TOK + P], start=(a == 0), stop=(a == 1))
                        last = []
                        if br == "C" and t < LT:
                            last = [(own.index(b), m) for b, m in ((t - 1, 1), (t + 1, 2)) if b in own]
                        for a in range(2):
                            mm = pe.matmul(pb[:, psum.bank(key), 0:n], q,
                                           kT[:, kv, a, own[0] * P:own[0] * P + n],
                                           start=(a == 0), stop=(a == 1 and not last))
                        for i, m in last:
                            mm = pe.matmul(pb[:, psum.bank(key), tile_cols(i)], masks[:, 0, :], masks[:, m, :],
                                           start=False, stop=(i == last[-1][0]))
                        mm.then_inc(*full(key))

                    def probs_T(s):
                        h, t = UNITS[s]
                        n = len(key_blocks(br, t))
                        acquire((br, "PT", s))
                        pe.wait_ge(p_ready, bi * len(UNITS) + s + 1)
                        b = psum.bank((br, "PT", s))
                        for i in range(n):
                            mm = pe.transpose(pb[:, b + i // 4, tile_cols(i % 4)], pr[:, s % 3, tile_cols(i)],
                                              ident[:, :])
                        mm.then_inc(*full((br, "PT", s)))

                    def values(v):
                        h, i = v // T, v % T
                        kv, j, o = h // (NH // KV), h // 2, psum.bank((br, "O", h // 2))
                        r = slice((h % 2) * HD, (h % 2 + 1) * HD)
                        vs = slice(kv * HD, (kv + 1) * HD)
                        if i == 0:
                            if h == 0:
                                acquire((br, "Octx"))
                            if h % 2 == 0:
                                acquire((br, "O", j))
                            wait_done(pe, (br, "PT", UNITS.index((h, LT))))
                            mm = pe.matmul(pb[r, psum.bank((br, "Octx")), tile_cols(j)], kv_of[:, LT, 1, vs],
                                           pT[:, h % 2, T * HALF:], start=True, stop=True)
                            if h == NH - 1:
                                mm.then_inc(*full((br, "Octx")))
                            pe.matmul(pb[r, o, :], cached[:, bi, 1, vs], pT[:, h % 2, LT * HALF:T * HALF],
                                      start=True, stop=False)
                        else:
                            b = i - 1
                            q0, q1 = (0, LT) if br == "A" else (max(b - 1, 0), min(b + 2, LT))
                            mm = pe.matmul(pb[r, o, q0 * P:q1 * P], kv_of[:, b, 1, vs],
                                           pT[:, h % 2, b * HALF + q0 * P:b * HALF + q1 * P],
                                           start=False, stop=(b == LT - 1))
                            if b == LT - 1:
                                if h % 2:
                                    mm.then_inc(*full((br, "O", j)))
                                else:
                                    mm.then_inc(pv_even, 1)

                    for s in range(len(UNITS) + PV_AFTER):
                        if s < len(UNITS):
                            scores(s)
                        if 2 <= s < len(UNITS) + 2:
                            probs_T(s - 2)
                        if br == "C" and s < 2 * KD:
                            modulation(4 + s // KD, s % KD)
                        if s >= PV_AFTER:
                            values(s - PV_AFTER)
                    if br == "C":
                        gates()

                def mlstm():
                    project(("B", "qk"))
                    project(("B", "v"))
                    pe.wait_ge(gw_ready, 1)
                    for i, cs in enumerate((slice(0, HALF), slice(HALF, TOK))):
                        acquire(("B", "gates", i))
                        for k in range(KD):
                            for n, (a, w) in enumerate(((0, 0), (0, 1), (1, 0))):
                                mm = pe.matmul(pb[:, psum.bank(("B", "gates", i)), 0:cs.stop - cs.start],
                                               gw[:, w, k, :], act_T[:, a, k, cs],
                                               start=(k == 0 and n == 0), stop=(k == KD - 1 and n == 2))
                        mm.then_inc(*full(("B", "gates", i)))
                    project(("B", "o"))
                    for t in range(T):
                        wait_done(pe, ("B", "qk", t))
                        transpose_blocks(("B", "qkT", t), lambda i: tokqk[:, t, i // 2, tile_cols(i % 2)], 4)
                    transpose_blocks(("B", "C0T"), lambda i: C0[:, i // 2, 2 * (i % 2):2 * (i % 2) + 2, :]
                                     .rearrange("v h d -> v (h d)"), 4)
                    project(("B", "z"))
                    pe.wait_ge(rows_act, 4)
                    for t in range(T):
                        acquire(("B", "cols", t))
                        for i, r in enumerate((rw, r1, rb, rf)):
                            mm = pe.transpose(pb[:, psum.bank(("B", "cols", t)), i * GR:(i + 1) * GR],
                                              r[0:GR, tile_cols(t)], ident[0:GR, 0:GR])
                        mm.then_inc(*full(("B", "cols", t)))
                    acquire(("B", "wcb"))
                    for d in range(2):
                        last = r1[0:GR, (P - 1 if d == 0 else 0)::P]
                        for h in range(MH):
                            r = ROW0[d] + h
                            n = (2 * d + h // 2) * T
                            mm = pe.matmul(pb[(h % 2) * HD:(h % 2 + 1) * HD, psum.bank(("B", "wcb")), n:n + T],
                                           ident[0:GR, r:r + 1].to_broadcast([GR, HD]), last,
                                           start=True, stop=True)
                    mm.then_inc(*full(("B", "wcb")))
                    for t in range(T):
                        wait_done(pe, ("B", "qkT", t))
                        wait_done(pe, ("B", "v", t))

                    def scores(k):
                        d, t = CHUNKS[k]
                        acquire(("B", "ST", k))
                        for h in range(MH):
                            r = slice((h % 2) * HD, (h % 2 + 1) * HD)
                            mm = pe.matmul(pb[:, psum.bank(("B", "ST", k)) + h % 2, tile_cols(h // 2)],
                                           kTm[r, h // 2, tile_cols(t)], qTm[r, h // 2, tile_cols(t)],
                                           start=True, stop=True)
                        mm.then_inc(*full(("B", "ST", k)))
                        acquire(("B", "GB", k))
                        b = psum.bank(("B", "GB", k))
                        pe.matmul(pb[:, b, :].rearrange("p (h q) -> p h q", h=MH), masks[:, 0, :],
                                  masks[:, 3 + d, :].unsqueeze(1).to_broadcast([P, MH, P]), start=True, stop=False)
                        for h in range(MH):
                            r = ROW0[d] + h
                            mm = pe.matmul(pb[:, b, tile_cols(h)], ident[0:GR, r:r + 1].to_broadcast([GR, P]),
                                           rg[0:GR, tile_cols(t)], start=False, stop=(h == MH - 1))
                        mm.then_inc(*full(("B", "GB", k)))

                    def outputs(k):
                        d, t = CHUNKS[k]
                        w = DV + 1
                        acquire(("B", "ND", k))
                        wait_done(pe, ("B", "ST", k))
                        for h in range(MH):
                            dst = pb[:, psum.bank(("B", "ND", k)) + h % 2, (h // 2) * 256:(h // 2) * 256 + w]
                            mm = pe.matmul(dst, sT[:, k % 2, h % 2, h // 2, :], v1[:, t, h, :], start=True, stop=True)
                        mm.then_inc(*full(("B", "ND", k)))
                        if t != LT:
                            acquire(("B", "IN", k))
                            wait_done(pe, ("B", "CS", k - 2) if k >= 2 else ("B", "C0T"))
                            for h in range(MH):
                                r = slice((h % 2) * HD, (h % 2 + 1) * HD)
                                dst = pb[:, psum.bank(("B", "IN", k)) + h % 2, (h // 2) * 256:(h // 2) * 256 + w]
                                mm = pe.matmul(dst, qTm[r, h // 2, tile_cols(t)], CT[r, d, h // 2, :],
                                               start=True, stop=True)
                            mm.then_inc(*full(("B", "IN", k)))
                        acquire(("B", "CS", k))
                        pe.wait_ge(kw_ready, k + 1)
                        b = psum.bank(("B", "CS", k))
                        if t != LT:
                            for h in range(MH):
                                r = slice((h % 2) * HD, (h % 2 + 1) * HD)
                                mm = pe.matmul(pb[r, b, (h // 2) * 256:(h // 2) * 256 + w],
                                               kw[:, k % 2, h * HD:(h + 1) * HD], v1[:, t, h, :],
                                               start=True, stop=True)
                        else:
                            for h in range(MH):
                                pe.matmul(pb[:, b, h * HD:(h + 1) * HD], v1[:, t, h, 0:DV],
                                          kw[:, k % 2, h * HD:(h + 1) * HD], start=True, stop=True)
                            mm = pe.matmul(pb[0:1, b, 256:512], ones[:, 0:1], kw[:, k % 2, :],
                                           start=True, stop=True)
                        mm.then_inc(*full(("B", "CS", k)))

                    for t in range(T):
                        wait_done(pe, ("B", "cols", t))
                    for k in range(len(CHUNKS) + 1):
                        if k < len(CHUNKS):
                            scores(k)
                        if k >= 1:
                            outputs(k - 1)
                    for t in range(T):
                        pe.wait_ge(hy_ready, t + 1)
                        transpose_blocks(("B", "yT", t), lambda i: hs[:, t, tile_cols(i)], 4)

                for bi, br in enumerate(MERGE_ORDER):
                    if br == "B":
                        mlstm()
                    else:
                        attention(br)
                    for hf in range(2):
                        project((br, "G", hf))
                        if hf == 0:
                            wait_y(pe, bi, br)
                        project((br, "BR", hf), y_lhs)
                for t in range(T):
                    pe.wait_ge(merged_ready, t + 1)
                    transpose_blocks(("mT", t), lambda i: merged[:, t, tile_cols(i)], KD)
                for hf in range(2):
                    project(("out", hf), tile_ready=(lambda t: wait_done(pe, ("mT", t))) if hf == 0 else None)
                meet(pe, "pe", l)

        @block.scalar
        def _(act):
            act.wait_ge(c_in, 48)
            act.activation(crow[:, 1, :], crow[:, 0, :], ACT.Tanh, scale=0.5).then_inc(init_act, 1)
            act.wait_ge(init_pe, 1)
            act.mul(csil[:, :, :].rearrange("p k w -> p w k"),
                    pb[:, 7, 0:2 * KD].rearrange("p (w k) -> p w k", w=2), 0.5).then_inc(init_act, 1)

            with act.Fori(0, DEPTH) as l:
                steps = [0]

                def step(ins):
                    steps[0] += 1
                    ins.then_inc(act_step, 1)
                    act.wait_ge(act_step, steps[0])

                wait_done(act, "modT")
                for t in range(T):
                    w = 1 if t == LT else 0
                    wait_full(act, ("xT", t))
                    if t >= 2:
                        act.wait_ge(u_ready, t - 1)
                    src = pair(("xT", t), P)
                    for k in range(KD // 2, KD):
                        ins = act.activation(utmp[:, t % 2, k, :], src[:, k, :], ACT.Identity,
                                             scale=modc[:, KD + k, w:w + 1], bias=modc[:, k, w:w + 1])
                    step(ins)
                    act.wait_ge(u_half, t + 1)
                    act.copy(act_T[:, 0, :, tile_cols(t)], utmp[:, t % 2, :, :]).then_inc(*done(("xT", t)))

                for t in range(T):
                    wait_full(act, ("kv", t))
                    for i, kv in enumerate((kvt, kv2)):
                        ins = act.copy(kv[:, t, :, :].rearrange("p a d -> p (a d)"),
                                       bank(("kv", t))[:, i * 256:(i + 1) * 256])
                    ins.then_inc(*done(("kv", t)))

                def attention(br):
                    bi = 0 if br == "A" else 1
                    kv_of = kvt if br == "A" else kv2
                    for t in range(T):
                        wait_full(act, (br, "q", t))
                        act.mul(tokq[:, t, :, 1, :], bank((br, "q", t)).rearrange("p (h d) -> p h d", h=NH),
                                1.0 if br == "A" else SCALE).then_inc(*done((br, "q", t)))
                    for t in range(T):
                        if br == "C" and t == LT:
                            wait_done(act, (br, "q", t))
                        else:
                            act.wait_ge(pre_done, bi * T + t + 1)
                        act.copy(tokq[:, t, :, 0, :].bitcast(F32R), tokq[:, t, :, 1, :]).then_inc(q_hi, 1)
                    for t in range(T):
                        wait_full(act, (br, "z", t))
                        act.activation(zt[:, t, :], bank((br, "z", t)), ACT.Tanh, scale=0.5).then_inc(z_tanh, 1)
                    for t in range(T + 1):
                        if t >= 2:
                            wait_full(act, (br, "kT", t - 2))
                        src = kv_of[:, t, 0, :] if t < T else cached[:, bi, 0, :]
                        if t == T:
                            act.wait_ge(small_in, 16 * 17)
                        act.copy(ks[:, t % 2, :, 0, :, :].bitcast(F32R),
                                 src.rearrange("p (v d) -> p v d", v=KV).unsqueeze(2)
                                 .to_broadcast([P, KV, 2, HD])).then_inc(k_hi, 1)
                        if t >= 1:
                            wait_full(act, (br, "qT", t - 1))
                            act.copy(qT[:, :, tile_cols(t - 1)], pair((br, "qT", t - 1), P))\
                                .then_inc(*done((br, "qT", t - 1)))
                    wait_full(act, (br, "zT", T - 1))
                    wait_full(act, (br, "kT", T))

                    def exponent(s):
                        h, t = UNITS[s]
                        n = len(key_blocks(br, t)) * P
                        act.wait_ge(nm_ready, bi * len(UNITS) + s + 1)
                        if s >= 3:
                            wait_full(act, (br, "PT", s - 3))
                        b = psum.bank((br, "S", s))
                        src = pb[:, b:b + 2, :].rearrange("p b n -> p (b n)")[:, 0:n]
                        if br == "C":
                            act.activation(sexp[:, s % 4:s % 4 + 1], sink[:, 0, h:h + 1], ACT.Exp,
                                           bias=nm[:, s % 4:s % 4 + 1]).then_inc(sink_done, 1)
                        act.activation(pr[:, s % 3, 0:n], src, ACT.Exp, bias=nm[:, s % 4:s % 4 + 1],
                                       accum_out=lsum[:, s % 4:s % 4 + 1]).then_inc(*done((br, "S", s)))

                    def evacuate_PT(s):
                        h, t = UNITS[s]
                        key = (br, "PT", s)
                        blocks = key_blocks(br, t)
                        wait_full(act, key)
                        if h >= 2 and t == 0:
                            if h % 2:
                                wait_full(act, (br, "O", (h - 2) // 2))
                            else:
                                act.wait_ge(pv_even, bi * (NH // 2) + h // 2)
                        src = pair(key, P)
                        if t == LT:
                            act.copy(pT[:, h % 2, T * HALF:], src[:, 0, :]).then_inc(*done(key))
                            return
                        dst = pT[:, h % 2, 0:T * HALF].rearrange("p (b q) -> p b q", b=T)[:, :, tile_cols(t)]
                        if br == "A":
                            act.copy(dst, src[:, 0:T, :]).then_inc(*done(key))
                        else:
                            n = len(blocks) - 1
                            act.copy(dst[:, blocks[0]:blocks[0] + n, :], src[:, 0:n, :])
                            act.copy(dst[:, LT, :], src[:, n, :]).then_inc(*done(key))

                    for s in range(len(UNITS) + PV_AFTER + 2):
                        if 2 <= s < len(UNITS) + 2:
                            evacuate_PT(s - 2)
                        if s < len(UNITS):
                            exponent(s)
                        v = s - PV_AFTER - 1
                        if v > 0 and v % (2 * T) == 0:
                            j = v // (2 * T) - 1
                            wait_done(act, (br, "O", j))
                            act.copy(yT[:, 0, j, 0:HALF], ytmp[:, :]).then_inc(y_hi, 1)
                    wait_done(act, (br, "Octx"))
                    act.copy(yT[:, 0, :, HALF:TOK], ytmp[:, :].rearrange("p (j q) -> p j q", j=4)).then_inc(y_hi, 1)
                    if br == "C":
                        act.wait_ge(stored, 64)
                        for i in range(4):
                            wait_full(act, ("gate", i))
                            act.copy(gate_bc[:, i // 2, (i % 2) * HALF:(i % 2 + 1) * HALF], bank(("gate", i)))\
                                .then_inc(*done(("gate", i)))

                def mlstm():
                    for t in range(T):
                        wait_full(act, ("B", "qk", t))
                        src = bank(("B", "qk", t))
                        act.copy(tokqk[:, t, 0, :], src[:, 0:256])
                        act.mul(tokqk[:, t, 1, :], src[:, 256:512], SCALE).then_inc(*done(("B", "qk", t)))
                    act.wait_ge(rows_dve, 1)
                    act.activation(r1[0:GR, :], r1[0:GR, :], ACT.Exp).then_inc(rows_act, 1)
                    act.wait_ge(rows_act, 1)
                    act.activation(r1[0:GR, :], r1[0:GR, :], ACT.Ln, bias=1.0).then_inc(rows_act, 1)
                    for t in range(T):
                        wait_full(act, ("B", "o", t))
                        act.activation(zo[:, t, :], bank(("B", "o", t)), ACT.Tanh, scale=0.5)\
                            .then_inc(*done(("B", "o", t)))
                    for t in range(T):
                        wait_full(act, ("B", "qkT", t))
                        src = bank(("B", "qkT", t)).rearrange("p (a j q) -> p a j q", a=2, j=2)
                        act.copy(qTm[:, :, tile_cols(t)], src[:, 0])
                        act.copy(kTm[:, :, tile_cols(t)], src[:, 1]).then_inc(*done(("B", "qkT", t)))
                    act.wait_ge(rows_dve, 2)
                    act.activation(r1[0:GR, :], r1[0:GR, :], ACT.Exp, scale=-1.0)
                    act.activation(rb[0:GR, :], rb[0:GR, :], ACT.Exp, scale=-1.0).then_inc(rows_act, 1)
                    act.activation(rf[0:GR, :], rf[0:GR, :], ACT.Exp).then_inc(rows_act, 1)
                    for t in range(T):
                        wait_full(act, ("B", "z", t))
                        if t >= 2:
                            act.wait_ge(zo_ready, t - 1)
                        act.activation(em[:, t % 2, :, :].rearrange("p b n -> p (b n)"), bank(("B", "z", t)), ACT.Tanh,
                                       scale=0.5).then_inc(z_tanh, 1)
                    for k, (d, t) in enumerate(CHUNKS):
                        wait_full(act, ("B", "GB", k))
                        wait_done(act, ("B", "cols", T - 1))
                        if k == 0:
                            act.wait_ge(zo_ready, T)
                        if k >= 2:
                            wait_done(act, ("B", "ST", k - 2))
                        b = psum.bank(("B", "GB", k))
                        for h in range(MH):
                            ins = act.activation(em[:, k % 2, h % 2, tile_cols(h // 2)], pb[:, b, tile_cols(h)], ACT.Exp,
                                                 bias=cols[:, t, 0, ROW0[d] + h:ROW0[d] + h + 1], scale=-1.0)
                        ins.then_inc(*done(("B", "GB", k)))
                    for t in range(T):
                        wait_full(act, ("B", "yT", t))
                        act.copy(yT[:, 0, :, tile_cols(t)], bank(("B", "yT", t)).rearrange("p (j q) -> p j q", j=4))\
                            .then_inc(y_hi, 1)

                for bi, br in enumerate(MERGE_ORDER):
                    if br == "B":
                        mlstm()
                    else:
                        attention(br)
                    for hf in range(2):
                        for t in range(T):
                            wait_full(act, (br, "G", hf, t))
                            if hf == 0 and t == 0:
                                wait_y(act, bi, br)
                            elif hf:
                                wait_done(act, (br, "BR", 0, t))
                            act.activation(tg[:, t, :], bank((br, "G", hf, t)), ACT.Tanh, scale=0.5)\
                                .then_inc(*done((br, "G", hf, t)))
                for t in range(T):
                    wait_full(act, ("mT", t))
                    act.mul(act_T[:, 0, :, tile_cols(t)], pair(("mT", t), P), 0.5).then_inc(m_hi, 1)
                for t in range(LT):
                    act.wait_ge(centred, t + 1)
                    act.wait_ge(rstd_ready, 2 + T + t)
                    act.mul(xh[:, t, :], xh[:, t, :], rstd[:, t:t + 1]).then_inc(scaled, 1)
                meet(act, "act", l)

        @block.vector
        def _(dve):
            dve.wait_ge(init_act, 1)
            dve.scalar_tensor_tensor(out=crow[:, 2, :], in0=crow[:, 1, :], scalar=1.0, in1=crow[:, 0, :],
                                     op0=ALU.add, op1=ALU.mult).then_inc(init_dve, 1)
            dve.memset(ones[:, :], 1.0)
            dve.wait_ge(first_in, 4 * 16)
            dve.tensor_copy(masks[:, 1:5, :], cst[:, :, :])
            dve.tensor_copy(masks[:, 0, :], ident[:, :])

            with dve.Fori(0, DEPTH) as l:
                steps = [0]

                def step(ins):
                    steps[0] += 1
                    ins.then_inc(dve_step, 1)
                    dve.wait_ge(dve_step, steps[0])

                for t in range(T):
                    for i in range(2):
                        ins = dve.bn_stats(out=stats[:, t, i, :], in_=xh[:, t, i * HALF:(i + 1) * HALF])
                step(ins)
                for t in range(T):
                    ins = dve.bn_aggr(out=mv[:, t, :], in_=stats[:, t, :, :].rearrange("p a b -> p (a b)"))
                step(ins)
                dve.tensor_scalar(ve[:, :], mv[:, :, 1], EPS, None, ALU.add).then_inc(var_ready, 1)
                dve.wait_ge(small_in, 16 * 17)
                for n in range(4):
                    wait_full(dve, ("mod", n))
                    cs = slice(n * HALF, (n + 1) * HALF)
                    dve.tensor_tensor(modrow[:, cs], pb[0:2, psum.bank(("mod", n)), :], bmod[:, cs], ALU.add)\
                        .then_inc(*done(("mod", n)))
                    if n == 0:
                        dve.wait_ge(rstd_ready, 1)
                        for t in range(T):
                            dve.tensor_scalar(xh[:, t, :], xh[:, t, :], mv[:, t, 0:1], rstd[:, t:t + 1],
                                              ALU.subtract, ALU.mult).then_inc(xn_ready, 1)
                wait_full(dve, "modT")
                src = bank("modT")[:, 0:4 * KD].rearrange("p (k w) -> p k w", w=2)
                dve.tensor_copy(modc[:, 0:KD, :], src[:, 0:KD, :])
                dve.tensor_scalar(modc[:, KD:2 * KD, :], src[:, KD:2 * KD, :], 1.0, None, ALU.add)\
                    .then_inc(*done("modT"))
                wait_done(dve, "modT")

                def u_lo(t):
                    wait_done(dve, ("xT", t))
                    dve.tensor_tensor(act_T[:, 1, :, tile_cols(t)], utmp[:, t % 2, :, :],
                                      act_T[:, 0, :, tile_cols(t)].bitcast(F32), ALU.subtract).then_inc(u_ready, 1)

                for t in range(T):
                    w = 1 if t == LT else 0
                    wait_full(dve, ("xT", t))
                    if t >= 2:
                        dve.wait_ge(u_ready, t - 1)
                    src = pair(("xT", t), P)
                    for k in range(KD // 2):
                        ins = dve.tensor_scalar(utmp[:, t % 2, k, :], src[:, k, :], modc[:, KD + k, w:w + 1],
                                                modc[:, k, w:w + 1], ALU.mult, ALU.add)
                    ins.then_inc(u_half, 1)
                    if t:
                        u_lo(t - 1)
                u_lo(T - 1)

                def attention(br):
                    bi = 0 if br == "A" else 1
                    kv_of = kvt if br == "A" else kv2
                    if br == "C":
                        step(dve.tensor_scalar(sink[:, 1, :], sink[:, 0, :], -1.0, None, ALU.mult))
                    if br == "A":
                        step(dve.tensor_scalar(gains[:, 0, :], gains[:, 0, :], SCALE, None, ALU.mult))
                        for t in range(T):
                            wait_done(dve, ("kv", t))
                            wait_done(dve, (br, "q", t))
                            q, k = tokq[:, t, :, 1, :], kvt[:, t, 0, :]
                            dve.tensor_tensor(rtmp[:, 0:512].rearrange("p (h d) -> p h d", h=NH), q, q, ALU.mult)
                            step(dve.tensor_tensor(rtmp[:, 512:640], k, k, ALU.mult))
                            step(dve.tensor_reduce(ms[:, t, :], rtmp[:, :].rearrange("p (h d) -> p h d", d=HD),
                                                   AX.X, ALU.add))
                            dve.tensor_scalar(ms[:, t, :], ms[:, t, :], 1.0 / HD, EPS, ALU.mult, ALU.add)\
                                .then_inc(var_ready, 1)

                    def q_lo(t):
                        dve.wait_ge(q_hi, bi * T + t + 1)
                        dve.tensor_tensor(tokq[:, t, :, 1, :], tokq[:, t, :, 1, :], tokq[:, t, :, 0, :],
                                          ALU.subtract).then_inc(q_ready, 1)

                    for t in range(T):
                        q = tokq[:, t, :, 1, :]
                        k = kv_of[:, t, 0, :].rearrange("p (v d) -> p v d", v=KV)
                        if br == "A":
                            dve.wait_ge(rstd_ready, 2 + t)
                            dve.tensor_tensor(q, q, rms[:, t, 0:NH].unsqueeze(2).to_broadcast([P, NH, HD]), ALU.mult)
                            step(dve.tensor_tensor(k, k, rms[:, t, NH:NH + KV].unsqueeze(2)
                                                   .to_broadcast([P, KV, HD]), ALU.mult))
                            dve.tensor_tensor(q, q, gains[:, 0, :].unsqueeze(1).to_broadcast([P, NH, HD]), ALU.mult)
                            ins = dve.tensor_tensor(k, k, gains[:, 1, :].unsqueeze(1).to_broadcast([P, KV, HD]),
                                                    ALU.mult)
                            if t < LT:
                                step(ins)
                            else:
                                ins.then_inc(pre_done, 1)
                        else:
                            wait_done(dve, ("kv", t))
                            wait_done(dve, (br, "q", t))
                        if t < LT:
                            if t:
                                dve.wait_ge(pre_done, bi * T + t)
                            for x, n, o in ((q, NH, 0), (k, KV, NH * HD)):
                                tmp = rtmp[:, o:o + n * HD].rearrange("p (n a i) -> p n a i", n=n, a=4)
                                x4 = x.rearrange("p n (a i) -> p n a i", a=4)
                                sn = rope[:, 1, t, :].rearrange("p (a i) -> p a i", a=4)
                                for a in range(2):
                                    ins = dve.tensor_tensor(tmp[:, :, a::2, :], x4[:, :, 1 - a::2, :],
                                                      sn[:, a::2, :].unsqueeze(1).to_broadcast([P, n, 2, 16]),
                                                      ALU.mult)
                            step(ins)
                            for x, n in ((q, NH), (k, KV)):
                                ins = dve.tensor_tensor(x, x, rope[:, 0, t, :].unsqueeze(1)
                                                        .to_broadcast([P, n, HD]), ALU.mult)
                            step(ins)
                            dve.tensor_tensor(q, q, rtmp[:, 0:512].rearrange("p (n d) -> p n d", n=NH), ALU.add)
                            dve.tensor_tensor(k, k, rtmp[:, 512:640].rearrange("p (n d) -> p n d", n=KV), ALU.add)\
                                .then_inc(pre_done, 1)
                        if t:
                            q_lo(t - 1)
                    q_lo(T - 1)
                    for t in range(T):
                        dve.wait_ge(z_tanh, bi * T + t + 1)
                        dve.scalar_tensor_tensor(out=zt[:, t, :], in0=zt[:, t, :], scalar=1.0,
                                                 in1=bank((br, "z", t)), op0=ALU.add, op1=ALU.mult)\
                            .then_inc(*done((br, "z", t)))
                    for t in range(T + 1):
                        dve.wait_ge(k_hi, bi * (T + 1) + t + 1)
                        src = (kv_of[:, t, 0, :] if t < T else cached[:, bi, 0, :]).rearrange("p (v d) -> p v d", v=KV)
                        for e in range(2):
                            ins = dve.tensor_tensor(ks[:, t % 2, :, 1, e, :], src, ks[:, t % 2, :, 0, e, :],
                                                    ALU.subtract)
                        ins.then_inc(k_ready, 1)
                        if t >= 1:
                            evacuate_kz(br, t - 1)
                    evacuate_kz(br, T)

                    def maximum(s):
                        h, t = UNITS[s]
                        n = len(key_blocks(br, t)) * P
                        wait_full(dve, (br, "S", s))
                        b = psum.bank((br, "S", s))
                        src = pb[:, b:b + 2, :].rearrange("p b n -> p (b n)")[:, 0:n]
                        o = slice(s % 4, s % 4 + 1)
                        if br == "A":
                            dve.tensor_reduce(nm[:, o], src, AX.X, ALU.max, negate=True).then_inc(nm_ready, 1)
                        else:
                            step(dve.tensor_reduce(nmx[:, o], src, AX.X, ALU.max, negate=True))
                            dve.tensor_tensor(nm[:, o], nmx[:, o], sink[:, 1, h:h + 1], ALU.min)\
                                .then_inc(nm_ready, 1)

                    def normalise(s):
                        h, t = UNITS[s]
                        n = len(key_blocks(br, t)) * P
                        o = slice(s % 4, s % 4 + 1)
                        wait_done(dve, (br, "S", s))
                        total = lsum
                        if br == "C":
                            dve.wait_ge(sink_done, s + 1)
                            step(dve.tensor_tensor(den[:, o], lsum[:, o], sexp[:, o], ALU.add))
                            total = den
                        step(dve.reciprocal(rden[:, o], total[:, o]))
                        dve.tensor_scalar(pr[:, s % 3, 0:n], pr[:, s % 3, 0:n], rden[:, o], None, ALU.mult)\
                            .then_inc(p_ready, 1)

                    def gate_out(j):
                        key = (br, "O", j)
                        wait_full(dve, key)
                        if j:
                            dve.wait_ge(y_ready, bi * T + j)
                        dve.scalar_tensor_tensor(out=ytmp[:, :], in0=bank(key), scalar=0.5, in1=zT[:, j, 0:HALF],
                                                 op0=ALU.mult, op1=ALU.mult).then_inc(*done(key))

                    def y_lo(j):
                        dve.wait_ge(y_hi, bi * T + j + 1)
                        cs = slice(0, HALF)
                        dve.tensor_tensor(yT[:, 1, j, cs], ytmp[:, :], yT[:, 0, j, cs].bitcast(F32), ALU.subtract)\
                            .then_inc(y_ready, 1)

                    def gate_row(n):
                        dve.wait_ge(bgate_in, 16)
                        wait_full(dve, ("mod", n))
                        cs = slice((n - 4) * HALF, (n - 3) * HALF)
                        dve.tensor_tensor(grow[:, cs], pb[0:2, psum.bank(("mod", n)), :], grow[:, cs], ALU.add)\
                            .then_inc(*done(("mod", n)))

                    for s in range(len(UNITS) + PV_AFTER + 3):
                        if s < len(UNITS):
                            maximum(s)
                        if br == "C" and s in (KD, 2 * KD):
                            gate_row(4 + s // KD - 1)
                        v = s - PV_AFTER
                        if v > 0 and v % (2 * T) == 0:
                            gate_out(v // (2 * T) - 1)
                        if 1 <= s < len(UNITS) + 1:
                            normalise(s - 1)
                        if v > 2 and (v - 2) % (2 * T) == 0:
                            y_lo((v - 2) // (2 * T) - 1)
                    key = (br, "Octx")
                    wait_full(dve, key)
                    dve.wait_ge(y_ready, bi * T + LT)
                    dve.scalar_tensor_tensor(out=ytmp[:, :].rearrange("p (j q) -> p j q", j=4),
                                             in0=bank(key).rearrange("p (j q) -> p j q", j=4), scalar=0.5,
                                             in1=zT[:, :, HALF:TOK], op0=ALU.mult, op1=ALU.mult)\
                        .then_inc(*done(key))
                    dve.wait_ge(y_hi, (bi + 1) * T)
                    dve.tensor_tensor(yT[:, 1, :, HALF:TOK], ytmp[:, :].rearrange("p (j q) -> p j q", j=4),
                                      yT[:, 0, :, HALF:TOK].bitcast(F32), ALU.subtract).then_inc(y_ready, 1)

                def evacuate_kz(br, t):
                    wait_full(dve, (br, "kT", t))
                    dve.tensor_copy(kT[:, :, :, tile_cols(t)].rearrange("p v a q -> p (v a) q"),
                                    bank((br, "kT", t)).rearrange("p (v q) -> p v q", v=4))\
                        .then_inc(*done((br, "kT", t)))
                    if t < T:
                        wait_full(dve, (br, "zT", t))
                        dve.tensor_copy(zT[:, :, tile_cols(t)], bank((br, "zT", t)).rearrange("p (j q) -> p j q", j=4))\
                            .then_inc(*done((br, "zT", t)))

                def mlstm():
                    wait_full(dve, ("C", "BR", 1, T - 1))
                    step(dve.memset(gw[:, :, :, :].rearrange("p a k n -> p (a k n)").bitcast(F32), 0.0))
                    for d in range(2):
                        for g in range(2):
                            o = 64 * g + ROW0[d]
                            ins = dve.tensor_copy(gw[:, 0, :, o:o + MH], gwraw[:, :, (2 * d + g) * MH:(2 * d + g + 1) * MH])
                    step(ins)
                    for d in range(2):
                        for g in range(2):
                            o = 64 * g + ROW0[d]
                            ins = dve.tensor_tensor(gw[:, 1, :, o:o + MH],
                                                    gwraw[:, :, (2 * d + g) * MH:(2 * d + g + 1) * MH],
                                                    gw[:, 0, :, o:o + MH].bitcast(F32), ALU.subtract)
                    ins.then_inc(gw_ready, 1)
                    wait_full(dve, ("gate", 3))
                    dve.memset(v1[:, :, :, DV:DV + 1], 1.0)
                    dve.memset(rb[0:GR, :], 0.0)
                    step(dve.memset(rg[0:GR, :], 0.0))
                    for t in range(T):
                        wait_full(dve, ("B", "v", t))
                        dve.tensor_copy(v1[:, t, :, 0:DV], bank(("B", "v", t)).rearrange("p (h d) -> p h d", h=MH))\
                            .then_inc(*done(("B", "v", t)))
                    for i, cs in enumerate((slice(0, HALF), slice(HALF, TOK))):
                        wait_full(dve, ("B", "gates", i))
                        b, n = psum.bank(("B", "gates", i)), cs.stop - cs.start
                        dve.tensor_scalar(rw[0:GR, cs], pb[0:GR, b, 0:n], gbias[0:GR, 0:1], None, ALU.add)
                        dve.tensor_scalar(rf[0:GR, cs], pb[64:64 + GR, b, 0:n], gbias[64:64 + GR, 0:1], None,
                                          ALU.add).then_inc(*done(("B", "gates", i)))
                    wait_done(dve, ("B", "gates", 1))
                    dve.scalar_tensor_tensor(out=r1[0:GR, :], in0=rf[0:GR, :], scalar=-1.0, in1=rf[0:GR, :],
                                             op0=ALU.mult, op1=ALU.min)\
                        .then_inc(rows_dve, 1)
                    dve.wait_ge(rows_act, 2)
                    step(dve.scalar_tensor_tensor(out=rf[0:GR, :], in0=rf[0:GR, :], scalar=0.0, in1=r1[0:GR, :],
                                                  op0=ALU.min, op1=ALU.subtract))

                    def along(row, d, t):
                        a = row[ROW0[d]:ROW0[d] + MH, tile_cols(t)]
                        return a if d == 0 else a[:, ::-1]

                    for d in range(2):
                        for t in range(T):
                            ins = dve.tensor_tensor_scan(along(rb, d, t), ones[ROW0[d]:ROW0[d] + MH, :],
                                                         along(rf, d, t), 0.0, ALU.mult, ALU.add)
                    step(ins)
                    step(dve.tensor_tensor(rw[0:GR, :], rw[0:GR, :], rb[0:GR, :], ALU.subtract))
                    for n, (d, t) in enumerate(CHUNKS):
                        r = slice(ROW0[d], ROW0[d] + MH)
                        last = t * P + (P - 1 if d == 0 else 0)
                        step(dve.tensor_tensor_scan(along(rg, d, t), along(rw, d, t), along(rw, d, t),
                                                    mcol[r, t:t + 1], ALU.max, ALU.max))
                        to = 5 if t == LT else t + (1 if d == 0 else -1)
                        if t == LT or 0 <= to < LT:
                            step(dve.tensor_tensor(mcol[r, to:to + 1], rb[r, last:last + 1], rg[r, last:last + 1],
                                                   ALU.add))
                    tiles = lambda row: row[0:GR, :].rearrange("p (t q) -> p t q", t=T)
                    dve.tensor_tensor(tiles(r1), tiles(rg), mcol[0:GR, 0:T].unsqueeze(2).to_broadcast([GR, T, P]),
                                      ALU.subtract)
                    dve.tensor_tensor(rb[0:GR, :], rb[0:GR, :], rg[0:GR, :], ALU.add)
                    for d in range(2):
                        r = slice(ROW0[d], ROW0[d] + MH)
                        g3 = rg[r, :].rearrange("p (t q) -> p t q", t=T)[:, :, (P - 1 if d == 0 else 0)]
                        ins = dve.tensor_tensor(rf[r, :].rearrange("p (t q) -> p t q", t=T),
                                                rw[r, :].rearrange("p (t q) -> p t q", t=T),
                                                g3.unsqueeze(2).to_broadcast([MH, T, P]), ALU.subtract)
                    ins.then_inc(rows_dve, 1)
                    wait_full(dve, ("B", "C0T"))
                    for d in range(2):
                        dve.tensor_copy(CT[:, d, :, DV:DV + 1], n0[:, d, :].unsqueeze(2))
                    dve.tensor_copy(CT[:, :, :, 0:DV].rearrange("p a j v -> p (a j) v"),
                                    bank(("B", "C0T")).rearrange("p (a v) -> p a v", a=4))\
                        .then_inc(*done(("B", "C0T")))
                    for t in range(T):
                        dve.wait_ge(z_tanh, 2 * T + t + 1)
                        z = em[:, t % 2, :, :].rearrange("p b n -> p (b n)")
                        dve.scalar_tensor_tensor(out=z, in0=z, scalar=1.0,
                                                 in1=bank(("B", "z", t)), op0=ALU.add, op1=ALU.mult)\
                            .then_inc(*done(("B", "z", t)))
                        wait_done(dve, ("B", "o", t))
                        wait_done(dve, ("B", "z", t))
                        dve.scalar_tensor_tensor(out=zo[:, t, :], in0=zo[:, t, :], scalar=1.0,
                                                 in1=z, op0=ALU.add, op1=ALU.mult)\
                            .then_inc(zo_ready, 1)
                    for t in range(T):
                        wait_full(dve, ("B", "cols", t))
                        dve.tensor_copy(cols[:, t, :, :].rearrange("p a r -> p (a r)"),
                                        bank(("B", "cols", t))[:, 0:4 * GR]).then_inc(*done(("B", "cols", t)))
                    wait_full(dve, ("B", "wcb"))
                    dve.tensor_copy(wcb[:, :, :].rearrange("p a t -> p (a t)"), bank(("B", "wcb"))[:, 0:4 * T])\
                        .then_inc(*done(("B", "wcb")))
                    wait_done(dve, ("B", "wcb"))

                    def col(k, i):
                        d, t = CHUNKS[k]
                        return cols[:, t, i, ROW0[d]:ROW0[d] + MH]

                    def by_head(a, n):
                        return a.rearrange("p (j b) -> p b j", b=2).unsqueeze(3).to_broadcast([P, 2, 2, n])

                    def decayed(k):
                        d, t = CHUNKS[k]
                        wait_done(dve, ("B", "cols", t))
                        if k >= 2:
                            wait_full(dve, ("B", "CS", k - 2))
                        dve.tensor_tensor(kw[:, k % 2, :].rearrange("p (h d) -> p h d", h=MH),
                                          tokqk[:, t, 1, :].rearrange("p (h d) -> p h d", h=MH),
                                          col(k, 3).unsqueeze(2).to_broadcast([P, MH, HD]), ALU.mult)\
                            .then_inc(kw_ready, 1)
                        wait_full(dve, ("B", "ST", k))
                        wait_done(dve, ("B", "GB", k))
                        dve.tensor_tensor(sT[:, k % 2, :, :, :].rearrange("p b j q -> p b (j q)"),
                                          pb[:, 0:2, 0:2 * P], em[:, k % 2, :, :], ALU.mult).then_inc(*done(("B", "ST", k)))

                    seen = set()

                    def combine(k):
                        d, t = CHUNKS[k]
                        b = psum.bank(("B", "ND", k))
                        wide = lambda b: pb[:, b:b + 2, :].rearrange("p b (n i) -> p b n i", i=256)[:, :, :, 0:DV + 1]
                        out = nd[:, k % 2, :, :, :]
                        if t != LT:
                            wait_full(dve, ("B", "IN", k))
                            dve.tensor_tensor(t3[:, :, :, :], wide(psum.bank(("B", "IN", k))),
                                              by_head(col(k, 1), DV + 1), ALU.mult)\
                                .then_inc(*done(("B", "IN", k)))
                            wait_done(dve, ("B", "IN", k))
                            wait_full(dve, ("B", "ND", k))
                            dve.tensor_tensor(out, wide(b), t3[:, :, :, :], ALU.add).then_inc(*done(("B", "ND", k)))
                        else:
                            wait_full(dve, ("B", "ND", k))
                            dve.tensor_copy(out, wide(b)).then_inc(*done(("B", "ND", k)))
                        wait_full(dve, ("B", "CS", k))
                        if t != LT:
                            C = CT[:, d, :, :]
                            step(dve.tensor_tensor(C, C, wcb[:, 2 * d:2 * d + 2, t:t + 1]
                                                   .to_broadcast([P, 2, DV + 1]), ALU.mult))
                            dve.tensor_tensor(C, bank(("B", "CS", k)).rearrange("p (j v) -> p j v", j=2)[:, :, 0:DV + 1],
                                              C, ALU.add).then_inc(*done(("B", "CS", k)))
                        else:
                            dve.tensor_copy(co[:, d, 0:256], bank(("B", "CS", k))[:, 0:256])
                            dve.tensor_copy(co[0:1, d, 256:512], pb[0:1, psum.bank(("B", "CS", k)), 256:512])\
                                .then_inc(*done(("B", "CS", k)))
                        wait_done(dve, ("B", "ND", k))
                        dk, rk = dn[:, k % 2, :, :], rdn[:, k % 2, :, :]
                        step(dve.scalar_tensor_tensor(out=dk, in0=out[:, :, :, DV], scalar=-1.0,
                                                      in1=col(k, 2).rearrange("p (j b) -> p b j", b=2),
                                                      op0=ALU.mult, op1=ALU.max))
                        step(dve.tensor_tensor(dk, dk, out[:, :, :, DV], ALU.max))
                        step(dve.reciprocal(rk, dk))
                        dst = hs[:, t, :] if t not in seen else t4[:, :]
                        step(dve.tensor_tensor(dst.rearrange("p (j b v) -> p b j v", j=2, b=2), out[:, :, :, 0:DV],
                                               rk.unsqueeze(3).to_broadcast([P, 2, 2, DV]), ALU.mult))
                        if t in seen:
                            step(dve.tensor_tensor(hs[:, t, :], hs[:, t, :], t4[:, :], ALU.add))
                        seen.add(t)

                    for k in range(len(CHUNKS) + 1):
                        if k < len(CHUNKS):
                            decayed(k)
                        if k >= 1:
                            combine(k - 1)
                    for t in range(T):
                        dve.scalar_tensor_tensor(out=hs[:, t, :], in0=hs[:, t, :], scalar=0.25, in1=zo[:, t, :],
                                                 op0=ALU.mult, op1=ALU.mult).then_inc(hy_ready, 1)
                    for t in range(T):
                        dve.wait_ge(y_hi, 2 * T + t + 1)
                        dve.tensor_tensor(yT[:, 1, :, tile_cols(t)],
                                          bank(("B", "yT", t)).rearrange("p (j q) -> p j q", j=4),
                                          yT[:, 0, :, tile_cols(t)].bitcast(F32), ALU.subtract)\
                            .then_inc(*done(("B", "yT", t)))

                for bi, br in enumerate(MERGE_ORDER):
                    if br == "B":
                        mlstm()
                    else:
                        attention(br)
                    for hf in range(2):
                        cs = slice(hf * HALF, (hf + 1) * HALF)
                        for t in range(T):
                            key = (br, "BR", hf, t)
                            wait_full(dve, key)
                            wait_done(dve, (br, "G", hf, t))
                            dst = merged[:, t, cs] if bi == 0 else mt[:, t % 2, :]
                            dve.scalar_tensor_tensor(out=dst, in0=tg[:, t, :], scalar=1.0, in1=bank(key),
                                                     op0=ALU.add, op1=ALU.mult).then_inc(*done(key))
                            if bi:
                                wait_done(dve, key)
                                ins = dve.tensor_tensor(merged[:, t, cs], merged[:, t, cs], mt[:, t % 2, :], ALU.add)
                                if br == MERGE_ORDER[-1] and hf == 1:
                                    ins.then_inc(merged_ready, 1)
                                else:
                                    step(ins)
                for t in range(T):
                    dve.wait_ge(m_hi, t + 1)
                    dve.scalar_tensor_tensor(out=act_T[:, 1, :, tile_cols(t)], in0=pair(("mT", t), P), scalar=0.5,
                                             in1=act_T[:, 0, :, tile_cols(t)].bitcast(F32), op0=ALU.mult,
                                             op1=ALU.subtract).then_inc(*done(("mT", t)))
                dve.wait_ge(late_in, 64)
                for hf in range(2):
                    cs = slice(hf * HALF, (hf + 1) * HALF)
                    for t in range(T):
                        key = ("out", hf, t)
                        wait_full(dve, key)
                        if hf == 0 and t == 0:
                            for i in range(4):
                                wait_done(dve, ("gate", i))
                        dve.tensor_tensor(ot[:, t % 2, :], bank(key), gate_bc[:, 1 if t == LT else 0, cs], ALU.mult)\
                            .then_inc(*done(key))
                        wait_done(dve, key)
                        step(dve.scalar_tensor_tensor(out=xh[:, t, cs], in0=xh[:, t, cs], scalar=ALPHA,
                                                      in1=ot[:, t % 2, :], op0=ALU.mult, op1=ALU.add))
                        step(dve.bn_stats(out=stats[:, t, hf, :], in_=xh[:, t, cs]))
                        if hf == 1:
                            step(dve.bn_aggr(out=mv[:, t, :], in_=stats[:, t, :, :].rearrange("p a b -> p (a b)")))
                            dve.tensor_scalar(ve[:, t:t + 1], mv[:, t, 1:2], EPS, None, ALU.add)\
                                .then_inc(var_ready, 1)
                            dve.scalar_tensor_tensor(out=xh[:, t, :], in0=xh[:, t, :], scalar=mv[:, t, 0:1],
                                                     in1=lnrow[:, 0, :], op0=ALU.subtract, op1=ALU.mult)\
                                .then_inc(centred, 1)
                dve.wait_ge(rstd_ready, 2 + T + LT)
                dve.wait_ge(centred, T)
                dve.scalar_tensor_tensor(out=xh[:, LT, :], in0=xh[:, LT, :], scalar=rstd[:, LT:LT + 1],
                                         in1=lnrow[:, 1, :], op0=ALU.mult, op1=ALU.add).then_inc(context_ready, 1)
                meet(dve, "dve", l)


def shape_constants():
    import numpy as np
    grid_w, axis = 64, HD // 2
    pos = np.arange(LT * P)
    inv = (10000.0 ** (-np.arange(0, axis, 2, dtype=np.float32) / axis)).astype(np.float32)
    ar = (pos // grid_w).astype(np.float32)[:, None] * inv
    ac = (pos % grid_w).astype(np.float32)[:, None] * inv
    ang = np.concatenate([ar, ar, ac, ac], axis=-1)
    sign = np.repeat(np.array([-1, 1, -1, 1], np.float32), 16)
    tables = [np.cos(ang), np.sin(ang) * sign]
    i = np.arange(P)
    row, col = i[:, None], i[None, :]
    big = np.float32(1e30)
    masks = [np.where(col >= row, 0, -big),
             np.where(col <= row, 0, -big),
             np.where(row <= col, 0, big),
             np.where(row >= col, 0, big)]
    parts = [np.eye(P)]
    parts += [t.reshape(LT, P, HD).transpose(1, 0, 2).reshape(P, LT * HD) for t in tables]
    parts += masks
    return np.concatenate(parts, axis=1).astype(np.float32)


_INS = ["x_prompt", "x_sample", "cache_attn_k", "cache_attn_v", "cache_win_k", "cache_win_v",
        "state_mlstm_C", "state_mlstm_n", "state_mlstm_m", "c", "c_ctx", "w_mod", "b_mod", "w_in",
        "qk_gain", "sink_logit", "mlstm_gate_bias", "w_branch", "w_out", "ln_gain", "ln_bias"]
_OUTS = [(1, P, D), (1, LT * P, D), (1, DEPTH, KV, P, HD), (1, DEPTH, KV, P, HD), (1, DEPTH, KV, P, HD),
         (1, DEPTH, KV, P, HD), (1, DEPTH, 2, MH, DV, HD), (1, DEPTH, 2, MH, HD), (1, DEPTH, 2, MH)]


def kernel(**inputs):
    import numpy as _np
    import concourse.bacc as _bacc
    from concourse.bass_utils import run_bass_kernel_spmd as _run

    nc = _bacc.Bacc("TRN2", target_bir_lowering=False, num_devices=1)
    arrays, args = {}, []
    for name in _INS:
        arrays[f"in_{name}"] = _np.ascontiguousarray(inputs[name])
    arrays["in_consts"] = shape_constants()
    for name, a in arrays.items():
        args.append(nc.dram_tensor(name, a.shape, mybir.dt.from_np(a.dtype), kind="ExternalInput").ap())
    for i, shape in enumerate(_OUTS):
        args.append(nc.dram_tensor(f"out_{i}", shape, F32, kind="ExternalOutput").ap())
    trunk_kernel(nc, *args)
    r = _run(nc, [arrays], core_ids=[0])
    return tuple(r.results[0][f"out_{i}"] for i in range(len(_OUTS)))
```

```python
from contextlib import ExitStack

import concourse.bass as bass
from concourse import mybir

F32 = mybir.dt.float32
F32R = mybir.dt.float32r
BF16 = mybir.dt.bfloat16
ALU = mybir.AluOpType
ACT = mybir.ActivationFunctionType
AX = mybir.AxisListType

P = 128
DEPTH = 2
D = 1024
KD = D // P
LT = 4
T = LT + 1
TOK = T * P
HD = 64
NH = 8
KV = 2
MH = 4
DV = 128
BW = 512
HALF = 512
SCALE = HD ** -0.5
EPS = 1e-6
ALPHA = (2.0 * DEPTH) ** 0.25

COL_A = 0
COL_B = COL_A + NH * HD + 2 * KV * HD + BW
COL_B_GATES = COL_B + 2 * MH * HD + 2 * MH * DV
COL_C = COL_B_GATES + 4 * MH + BW
COL_G = COL_C + NH * HD + 2 * KV * HD + BW
BRANCH = {"A": 0, "B": 1, "C": 2}
MERGE_ORDER = ("A", "C", "B")

CHUNKS = [(0, 0), (1, 3), (0, 1), (1, 2), (0, 2), (1, 1), (0, 3), (1, 0), (0, LT), (1, LT)]
ROW0 = (0, 32)
GR = 36

UNITS = [(h, t) for h in range(NH) for t in range(LT)] + [(h, LT) for h in range(NH)]

PV_AFTER = LT + 2
NL = NH * LT
STEPS = NL + NH + 3


def key_blocks(branch, t):
    if t == LT:
        return [LT]
    if branch == "A":
        return list(range(LT)) + [T]
    return [b for b in (t - 1, t, t + 1) if 0 <= b < LT] + [T]


class Pieces:

    def __init__(self):
        self.items = []
        self.first = {}
        self.chunk = {}
        self.last = {}
        self.inner = []
        self.loaded = []
        self.splits = []
        self.order = {}
        self.by_act = {}

    def add(self, key, matrix, blocks, *columns):
        self.first[key] = len(self.items)
        self.chunk[key] = blocks // 2
        for k in range(0, blocks, 2):
            p = len(self.items)
            same = [q for q in range(p) if (self.items[q][0] == "mod") == (matrix == "mod")]
            self.inner.append(sum(q not in self.last for q in same))
            self.loaded.append(16 * len(columns) + (self.loaded[p - 3] if p >= 3 else 0))
            if matrix != "mod":
                self.order[p] = len(self.splits)
                self.splits.append(p)
            if key == ("A", "z"):
                self.by_act[p] = len(self.by_act)
            self.items.append((matrix, k, columns))
        self.last[len(self.items) - 1] = key if key[0] == "mod" else (*key, T - 1)


class PsumPlan:

    def __init__(self):
        self.count = [0] * 8
        self.last = [None] * 8
        self.use = {}
        self.rolling = 0

    def take(self, key, *banks):
        before = sorted({self.last[b] for b in banks if self.last[b]})
        lead = banks[0]
        self.count[lead] += 1
        for b in banks:
            self.last[b] = (lead, self.count[lead])
        self.use[key] = (lead, self.count[lead], before)

    def roll(self, key):
        self.take(key, self.rolling % 8)
        self.rolling += 1

    def bank(self, key):
        return self.use[key][0]


def plan_layer():
    pieces, psum = Pieces(), PsumPlan()
    def modulation(c):
        pieces.add(("mod", c), "mod", KD, (c * HALF, HALF))

    for c in range(4):
        modulation(c)
        psum.take(("mod", c), c)
    psum.take("modT", 6)
    for t in range(T):
        b = 2 * (t % 3)
        psum.take(("xT", t), b, b + 1)
    pieces.add(("kv",), "in", KD, *((base + NH * HD, 2 * KV * HD) for base in (COL_A, COL_C)))
    for t in range(T):
        psum.roll(("kv", t))
    for br in MERGE_ORDER:
        if br != "B":
            base = COL_A if br == "A" else COL_C
            for name, col in (("q", 0), ("z", NH * HD + 2 * KV * HD)):
                pieces.add((br, name), "in", KD, (base + col, HALF))
                for t in range(T):
                    psum.roll((br, name, t))
                if name == "q":
                    for t in range(T + 1):
                        psum.roll((br, "kT", t))
            if br == "C":
                for c in (4, 5):
                    modulation(c)
            for t in range(T):
                e = t % 2
                psum.take((br, "qT", t), 2 * e, 2 * e + 1)
                psum.take((br, "zT", t), 6 + e)
            for s in range(STEPS):
                if s < len(UNITS):
                    psum.take((br, "S", s), *((2 * (s % 2), 2 * (s % 2) + 1) if br == "A" else (s % 3,)))
                if 2 <= s < len(UNITS) + 2:
                    psum.take((br, "PT", s - 2), (4 if br == "A" else 3) + s % 2)
                    if br == "A" and s - 2 < NL:
                        psum.take((br, "P5", s - 2), 6)
                if br == "C" and s in (0, KD):
                    psum.take(("mod", 4 + s // KD), 6)
                v = s - PV_AFTER
                if 0 <= v < NL and v % (2 * LT) == 0:
                    psum.take((br, "O", v // (2 * LT)), 7 if br == "A" else 5)
                if s == NL + 3:
                    psum.take((br, "Octx"), 6 if br == "A" else 7)
            if br == "C":
                for i in range(4):
                    psum.roll(("gate", i))
        else:
            for name, col in (("qk", 0), ("v", 512), ("gates", None), ("o", 1024),
                              ("T", None), ("z", COL_B_GATES + 4 * MH - COL_B)):
                if name == "gates":
                    psum.roll(("B", "gates", 0))
                    psum.roll(("B", "gates", 1))
                elif name == "T":
                    for t in range(T):
                        psum.roll(("B", "qkT", t))
                    psum.roll(("B", "C0T"))
                else:
                    pieces.add(("B", name), "in", KD, (COL_B + col, HALF))
                    for t in range(T):
                        psum.roll(("B", name, t))
            for t in range(T):
                psum.take(("B", "cols", t), t % 2)
            psum.take(("B", "wcb"), 2)
            for k in range(len(CHUNKS) + 1):
                if k < len(CHUNKS):
                    psum.take(("B", "ST", k), k % 2)
                    psum.take(("B", "GB", k), 2 + k % 2)
                if k >= 1:
                    d, t = CHUNKS[k - 1]
                    psum.take(("B", "ND", k - 1), 4, 5)
                    if t != LT:
                        psum.take(("B", "IN", k - 1), 6, 7)
                    psum.take(("B", "CS", k - 1), 2 + (k - 1) % 2)
            for t in range(T):
                psum.take(("B", "yT", t), t % 2)
        for hf in range(2):
            i = BRANCH[br]
            pieces.add((br, "G", hf), "in", KD, (COL_G + i * D + hf * HALF, HALF))
            pieces.add((br, "BR", hf), ("branch", i), BW // P, (hf * HALF, HALF))
            for name in ("G", "BR"):
                for t in range(T):
                    psum.roll((br, name, hf, t))
    for t in range(T):
        b = 2 * (t % 3)
        psum.take(("mT", t), b, b + 1)
    for hf in range(2):
        pieces.add(("out", hf), "out", KD, (hf * HALF, HALF))
        for t in range(T):
            psum.roll(("out", hf, t))
    return pieces, psum


def trunk_kernel(nc, x_prompt, x_sample, cache_attn_k, cache_attn_v, cache_win_k, cache_win_v,
                 state_C, state_n, state_m, c, c_ctx, w_mod, b_mod, w_in, qk_gain, sink_logit,
                 gate_bias, w_branch, w_out, ln_gain, ln_bias, consts,
                 y_prompt, y_sample, new_attn_k, new_attn_v, new_win_k, new_win_v,
                 new_C, new_n, new_m):
    pieces, psum = plan_layer()
    NP = len(pieces.items)

    ctx = ExitStack()
    with ctx:
        ctx.enter_context(nc.allow_non_contiguous_dma(reason="states and columns of a few elements"))
        place = [0]
        base = nc.sbuf_base + (-nc.sbuf_base) % 64

        def at(name, shape, dt, offset):
            return nc.alloc_sbuf_tensor_at(name, shape, dt, offset=base + offset)

        def fixed(name, shape, dt, size=4):
            n = size
            for s in shape[1:]:
                n *= s
            n += -n % 32
            where = place[0]
            place[0] += n
            return at(name, shape, dt, where)

        def sem(name):
            return ctx.enter_context(nc.semaphore(name))

        act_T = fixed("act_T", [P, 2, KD, TOK], F32R)
        raw = fixed("raw", [P, 3, 2, HALF], F32)
        wsp = fixed("wsp", [P, 2, 2, 2, HALF], F32R)
        merged = fixed("merged", [P, T, D], F32)
        gate_at = place[0]
        gate_bc = fixed("gate_bc", [P, 2, D], F32)
        kv2 = at("kv2", [P, T, 2, KV * HD], F32, gate_at)
        ident = fixed("ident", [P, P], F32)
        rope = fixed("rope", [P, 2, LT, HD], F32)
        masks = fixed("masks", [P, 5, P], BF16, 2)
        ones = fixed("ones", [P, P], F32)
        cached = fixed("cached", [P, 2, 2, KV * HD], F32)
        C0 = fixed("C0", [P, 2, MH, HD], F32)
        n0 = fixed("n0", [P, 2, 2], F32)
        gains = fixed("gains", [P, 2, HD], F32)
        sink = fixed("sink", [P, 2, NH], F32)
        modc = fixed("modc", [P, 2 * KD, 2], F32)
        csil = fixed("csil", [P, KD, 2], F32)
        crow = fixed("crow", [2 * KD, 3, P], F32)
        gwraw = fixed("gwraw", [P, KD, 4 * MH], F32)
        gbias = fixed("gbias", [P, 1], F32)
        mcol = fixed("mcol", [P, 8], F32)
        half_neg = fixed("half_neg", [P, 16], F32)
        stats = fixed("stats", [P, T, 2, 6], F32)
        mv = fixed("mv", [P, T, 2], F32)
        ve = fixed("ve", [P, T], F32)
        rstd = fixed("rstd", [P, T], F32)
        ms = fixed("ms", [P, T, NH], F32)
        rms = fixed("rms", [P, T, NH], F32)
        msk = fixed("msk", [P, T * KV], F32)
        rmsk = fixed("rmsk", [P, T * KV], F32)
        nmx = fixed("nmx", [P, 4], F32)
        nm = fixed("nm", [P, 4], F32)
        lsum = fixed("lsum", [P, 4], F32)
        sexp = fixed("sexp", [P, 4], F32)
        den = fixed("den", [P, 4], F32)
        rden = fixed("rden", [P, 4], F32)
        dn = fixed("dn", [P, 2, 2, 2], F32)
        rdn = fixed("rdn", [P, 2, 2, 2], F32)
        wcb = fixed("wcb", [P, 4, T], F32)
        y_at = place[0]
        place[0] += 2 * 4 * TOK * 4
        yT = at("yT", [P, 2, 4, TOK], F32R, y_at)
        tokq = at("tokq", [P, T, NH, 2, HD], F32, y_at)
        tokqk = at("tokqk", [P, T, 2, MH * HD], F32, y_at)
        gw = at("gw", [P, 2, KD, P], F32R, y_at + T * 2048)
        qz = at("qz", [P, T, 2, 2, P], F32, y_at + T * 2048)
        arena = place[0]
        xh = at("xh", [P, T, D], F32, arena)
        modrow = at("modrow", [2, 2 * D], F32, arena + 20480)
        bmod = at("bmod", [2, 2 * D], F32, arena + 32768)
        utmp = at("utmp", [P, 2, KD, P], F32, arena + 45056)
        lnrow = at("lnrow", [P, 2, D], F32, arena + 44544)
        ot = at("ot", [P, 2, HALF], F32, arena + 52736)
        cst = at("cst", [P, 4, P], F32, arena + 53248)
        kvt = at("kvt", [P, T, 2, KV * HD], F32, arena)
        pr = at("pr", [P, 3, T * P], F32, arena + 5120)
        zt = at("zt", [P, T, HALF], F32, arena + 29696)
        zT = at("zT", [P, 4, TOK], F32, arena + 12800)
        pT = at("pT", [P, 2, T * HALF + P], F32, arena + 23040)
        rtmp = at("rtmp", [P, 640], F32, arena + 23040)
        ks = at("ks", [P, T + 1, KV, 2, 2, HD], F32, arena + 5120)
        ytmp = at("ytmp", [P, HALF], F32, arena + 44544)
        qT = at("qT", [P, NH, TOK], F32R, arena + 46592)
        kT = at("kT", [P, KV, 2, TOK + P], F32R, arena + 67072)
        grow = at("grow", [2, D], F32, arena)
        tg = at("tg", [P, T, HALF], F32, arena + 23040)
        mt = at("mt", [P, 2, HALF], F32, arena + 33280)
        v1 = at("v1", [P, T, MH, DV + 1], F32, arena)
        zo = at("zo", [P, T, HALF], F32, arena + 10336)
        hs = at("hs", [P, T, HALF], F32, arena + 20576)
        kw = at("kw", [P, 2, MH * HD], F32, arena + 30816)
        kTm = at("kTm", [P, 2, TOK], F32, arena + 35936)
        cols = at("cols", [P, T, 4, GR], F32, arena + 41056)
        em = at("em", [P, 2, 2, 2 * P], F32, arena + 43936)
        sT = at("sT", [P, 2, 2, 2, P], F32, arena + 48032)
        nd = at("nd", [P, 2, 2, 2, DV + 1], F32, arena + 52128)
        t3 = at("t3", [P, 2, 2, DV + 1], F32, arena + 56256)
        CT = at("CT", [P, 2, 2, DV + 1], F32, arena + 58336)
        rw, rf, rb, rg, r1 = (at(n, [P, TOK], F32, arena + 60416 + 2560 * i)
                              for i, n in enumerate(("rw", "rf", "rb", "rg", "r1")))
        co = at("co", [P, 2, HALF], F32, arena + 60416)
        t4 = at("t4", [P, HALF], F32, arena + 73216)
        rgd = at("rgd", [P, 2, MH, P], F32, arena + 75264)

        pb = ctx.enter_context(nc.psum_tensor("pb", [P, 8, HALF], F32))

        bank_full = [sem(f"bank_full{b}") for b in range(8)]
        bank_done = [sem(f"bank_done{b}") for b in range(8)]
        raw_in = [sem(f"raw_in{i}") for i in range(3)]
        raw_used = sem("raw_used")
        mod_used = sem("mod_used")
        hi_by_act = sem("hi_by_act")
        split_used = sem("split_used")
        small_in = sem("small_in")
        bgate_in = sem("bgate_in")
        late_in = sem("late_in")
        var_ready = sem("var_ready")
        rstd_ready = sem("rstd_ready")
        xn_ready = sem("xn_ready")
        u_half = sem("u_half")
        u_ready = sem("u_ready")
        k_done = sem("k_done")
        pre_done = sem("pre_done")
        q_hi = sem("q_hi")
        q_ready = sem("q_ready")
        k_hi = sem("k_hi")
        k_ready = sem("k_ready")
        z_tanh = sem("z_tanh")
        nm_ready = sem("nm_ready")
        sink_done = sem("sink_done")
        p_ready = sem("p_ready")
        pv_even = sem("pv_even")
        pv_context = sem("pv_context")
        y_hi = sem("y_hi")
        y_ready = sem("y_ready")
        gw_ready = sem("gw_ready")
        rows_dve = sem("rows_dve")
        rows_act = sem("rows_act")
        qz_zero = sem("qz_zero")
        rgd_ready = sem("rgd_ready")
        zo_ready = sem("zo_ready")
        kw_ready = sem("kw_ready")
        hy_ready = sem("hy_ready")
        m_hi = sem("m_hi")
        merged_ready = sem("merged_ready")
        centred = sem("centred")
        scaled = sem("scaled")
        o_ready = sem("o_ready")
        context_ready = sem("context_ready")
        act_step, dve_step, pool_step = sem("act_step"), sem("dve_step"), sem("pool_step")
        at_end = {n: sem(f"at_end_{n}") for n in ("pe", "act", "dve", "pool")}
        stored = sem("stored")
        c_in = sem("c_in")
        first_in = sem("first_in")
        x_saved = sem("x_saved")
        init_dve, init_act, init_pe = sem("init_dve"), sem("init_act"), sem("init_pe")
        init_pool = sem("init_pool")
        go_on = sem("go_on")

        block = ctx.enter_context(nc.Block())

        def wait_full(eng, key):
            lead, n, _ = psum.use[key]
            eng.wait_ge(bank_full[lead], n)

        def wait_done(eng, key):
            lead, n, _ = psum.use[key]
            eng.wait_ge(bank_done[lead], n)

        def full(key):
            return bank_full[psum.bank(key)], 1

        def done(key):
            return bank_done[psum.bank(key)], 1

        def bank(key, second=0):
            return pb[:, psum.bank(key) + second, :]

        def pair(key, inner):
            b = psum.bank(key)
            return pb[:, b:b + 2, :].rearrange("p b (n i) -> p (b n) i", i=inner)

        def wait_piece(eng, p):
            eng.wait_ge(raw_in[p % 3], pieces.loaded[p])
            if pieces.order[p] >= 2:
                before = pieces.splits[pieces.order[p] - 2]
                if before in pieces.last:
                    wait_full(eng, pieces.last[before])
                else:
                    eng.wait_ge(split_used, pieces.inner[before] + 1)

        def wait_y(eng, bi, br):
            if br == "B":
                for t in range(T):
                    wait_done(eng, ("B", "yT", t))
            else:
                eng.wait_ge(y_ready, T * (bi + 1))

        def meet(eng, name, l):
            eng.drain().then_inc(at_end[name], 1)
            eng.wait_ge(go_on, l + 1)

        def tile_cols(t):
            return slice(t * P, (t + 1) * P)

        @block.sync
        def _(sp):
            sp.dma_start(crow[0:KD, 0, :], c.rearrange("a (k p) -> (a k) p", p=P)).then_inc(c_in, 16)
            sp.dma_start(crow[KD:2 * KD, 0, :], c_ctx.rearrange("(k p) -> k p", p=P)).then_inc(c_in, 16)
            sp.dma_start(ident[:, :], consts[:, 0:P]).then_inc(c_in, 16)
            sp.wait_ge(init_pool, 3)

            with sp.Fori(0, DEPTH) as l:
                def of_layer(ap, pattern, **k):
                    return ap[bass.ds(l, 1)].rearrange(pattern, **k)

                def load_piece(p):
                    matrix, k, columns = pieces.items[p]
                    if p - 3 in pieces.order:
                        sp.wait_ge(raw_used, pieces.order[p - 3] + 1)
                    elif p - 3 in pieces.last:
                        wait_full(sp, pieces.last[p - 3])
                    elif p >= 3:
                        sp.wait_ge(mod_used, pieces.inner[p - 3] + 1)
                    rows = slice(k * P, (k + 2) * P)
                    at_col = 0
                    for col, width in columns:
                        if matrix == "mod":
                            src = w_mod[bass.ds(l, 1), rows, col:col + width]
                        elif matrix == "in":
                            src = w_in[bass.ds(l, 1), rows, col:col + width]
                        elif matrix == "out":
                            src = w_out[bass.ds(l, 1), rows, col:col + width]
                        else:
                            src = w_branch[bass.ds(l, 1), matrix[1], rows, col:col + width]
                        sp.dma_start(raw[:, p % 3, :, at_col:at_col + width],
                                     src.rearrange("a (k p) n -> p (a k) n", p=P)).then_inc(raw_in[p % 3], 16)
                        at_col += width

                def store_kv(i, k_out, v_out):
                    if i == 0:
                        sp.wait_ge(k_done, 1)
                    else:
                        wait_done(sp, ("kv", LT))
                    for which, out in ((0, k_out), (1, v_out)):
                        sp.dma_start(of_layer(out[0], "a v s d -> s (a v) d"),
                                     (kvt, kv2)[i][:, LT, which, :].rearrange("s (v d) -> s v d", v=KV))\
                            .then_inc(stored, 16)

                for p in range(3):
                    load_piece(p)
                sp.dma_start(bmod[:, :], b_mod[bass.ds(l, 1), 0:2 * D].to_broadcast([2, 2 * D])).then_inc(small_in, 16)
                for i, (k, v) in enumerate(((cache_attn_k, cache_attn_v), (cache_win_k, cache_win_v))):
                    for j, a in enumerate((k, v)):
                        sp.dma_start(cached[:, i, j, :].rearrange("s (v d) -> s v d", v=KV),
                                     of_layer(a[0], "a v s d -> s (a v) d")).then_inc(small_in, 16)
                sp.dma_start(C0[:, :, :, :].rearrange("v a h d -> v (a h) d"),
                             of_layer(state_C[0], "l a h v d -> v (l a h) d")).then_inc(small_in, 16)
                for d in range(2):
                    sp.dma_start(n0[:, d, :], state_n[0, bass.ds(l, 1), d].rearrange(
                        "l (j e) d -> (l e d) j", e=2)).then_inc(small_in, 16)
                    sp.dma_start(mcol[ROW0[d]:ROW0[d] + MH, 3 * d:3 * d + 1],
                                 state_m[0, bass.ds(l, 1), d].rearrange("l h -> h l")).then_inc(small_in, 16)
                    for g in range(2):
                        r = 64 * g + ROW0[d]
                        sp.dma_start(gbias[r:r + MH, 0:1],
                                     gate_bias[bass.ds(l, 1), 2 * d + g].rearrange("l h -> h l"))\
                            .then_inc(small_in, 16)
                sp.dma_start(gains[:, :, :].rearrange("p a d -> p (a d)"),
                             of_layer(qk_gain, "l a d -> l (a d)").to_broadcast([P, 2 * HD])).then_inc(small_in, 16)
                sp.dma_start(sink[:, 0, :],
                             of_layer(sink_logit, "l v g -> l (v g)").to_broadcast([P, NH])).then_inc(small_in, 16)
                sp.dma_start(gwraw[:, :, :], w_in[bass.ds(l, 1), :, COL_B_GATES:COL_B_GATES + 4 * MH]
                             .rearrange("l (k p) n -> p (l k) n", p=P)).then_inc(small_in, 16)
                for p in range(3, NP):
                    if p == pieces.first[("A", "G", 0)]:
                        store_kv(0, new_attn_k, new_attn_v)
                    if p == pieces.first[("C", "q")]:
                        wait_full(sp, ("A", "Octx"))
                        wait_full(sp, ("A", "O", NH // 2 - 1))
                        sp.wait_ge(stored, 32)
                        sp.dma_start(grow[:, :], b_mod[bass.ds(l, 1), 2 * D:3 * D].to_broadcast([2, D]))\
                            .then_inc(bgate_in, 16)
                    if p == pieces.first[("C", "G", 0)]:
                        store_kv(1, new_win_k, new_win_v)
                    if p == pieces.first[("out", 0)]:
                        sp.wait_ge(hy_ready, T)
                        wait_full(sp, ("B", "yT", T - 1))
                        sp.wait_ge(x_saved, 32)
                        sp.dma_start(xh[:, 0:LT, :], y_sample.rearrange("a (t p) d -> p (a t) d", p=P)).then_inc(late_in, 16)
                        sp.dma_start(xh[:, LT, :], y_prompt[0, :, :]).then_inc(late_in, 16)
                        for i, a in enumerate((ln_gain, ln_bias)):
                            sp.dma_start(lnrow[:, i, :], a[bass.ds(l, 1), :].to_broadcast([P, D])).then_inc(late_in, 16)
                        for d in range(2):
                            wait_done(sp, ("B", "CS", CHUNKS.index((d, LT))))
                            sp.dma_start(of_layer(new_C[0], "l a h v d -> l a v h d")[0, d],
                                         co[:, d, 0:256].rearrange("v (h d) -> v h d", h=MH)).then_inc(stored, 16)
                            sp.dma_start(new_n[0, bass.ds(l, 1), d].rearrange("l h d -> l (h d)"),
                                         co[0:1, d, 256:512]).then_inc(stored, 16)
                            sp.dma_start(new_m[0, bass.ds(l, 1), d].rearrange("l h -> h l"),
                                         mcol[ROW0[d]:ROW0[d] + MH, 5:6]).then_inc(stored, 16)
                    load_piece(p)
                for t in range(T):
                    if t == LT:
                        sp.wait_ge(context_ready, 1)
                    else:
                        sp.wait_ge(o_ready, t + 1)
                    dst = y_prompt[0, :, :] if t == LT else y_sample[0, tile_cols(t), :]
                    sp.dma_start(dst, xh[:, t, :]).then_inc(stored, 16)
                for name in at_end:
                    sp.wait_ge(at_end[name], 1)
                sp.sem_clear(range(bank_full[0].num, at_end["pool"].num + 1))
                sp.wait_ge(stored, 16 * (4 + 6 + T))
                sp.sem_clear(stored)
                sp.drain().then_inc(go_on, 1)

        @block.gpsimd
        def _(pool):
            pool.memset(half_neg[:, :], -0.5).then_inc(init_pool, 1)
            pool.memset(mcol[:, :], 0.0).then_inc(init_pool, 1)
            pool.memset(gbias[:, :], 0.0).then_inc(init_pool, 1)
            pool.wait_ge(init_pool, 3)
            with pool.Fori(0, DEPTH) as l:
                def inv_sqrt(dst, src, n):
                    pool.wait_ge(var_ready, n)
                    pool.tensor_tensor(dst, src, half_neg[:, 0:src.shape[1]], ALU.pow).then_inc(rstd_ready, 1)

                inv_sqrt(rstd[:, :], ve[:, :], 1)
                copies = 0
                for i, p in enumerate(pieces.splits):
                    width = sum(w for _, w in pieces.items[p][2])
                    wait_piece(pool, p)
                    hi, lo = (wsp[:, i % 2, a, :, 0:width] for a in range(2))
                    if p in pieces.by_act:
                        pool.wait_ge(hi_by_act, pieces.by_act[p] + 1)
                    else:
                        copies += 1
                        pool.tensor_copy(hi, raw[:, p % 3, :, 0:width]).then_inc(pool_step, 1)
                        pool.wait_ge(pool_step, copies)
                    pool.tensor_tensor(lo, raw[:, p % 3, :, 0:width], hi.bitcast(F32), ALU.subtract)\
                        .then_inc(raw_used, 1)
                    if p == pieces.first[("A", "q")] + 2:
                        inv_sqrt(rmsk[:, :], msk[:, :], 2)
                    if p == pieces.first[("A", "z")] + 1:
                        for t in range(3):
                            inv_sqrt(rms[:, t, :], ms[:, t, :], 3 + t)
                    if p == pieces.first[("A", "z")] + 2:
                        for t in range(3, T):
                            inv_sqrt(rms[:, t, :], ms[:, t, :], 3 + t)
                for t in range(T):
                    inv_sqrt(rstd[:, t:t + 1], ve[:, t:t + 1], 3 + T + t)
                    if t:
                        pool.wait_ge(late_in, 64)
                        pool.wait_ge(scaled, t)
                        pool.tensor_tensor(xh[:, t - 1, :], xh[:, t - 1, :], lnrow[:, 1, :], ALU.add)\
                            .then_inc(o_ready, 1)
                meet(pool, "pool", l)

        @block.tensor
        def _(pe):
            pe.wait_ge(init_dve, 1)
            pe.transpose(pb[:, 7, 0:2 * KD], crow[:, 2, :], ident[0:2 * KD, 0:2 * KD]).then_inc(init_pe, 1)
            pe.wait_ge(init_act, 2)

            with pe.Fori(0, DEPTH) as l:
                def acquire(key):
                    for lead, n in psum.use[key][2]:
                        pe.wait_ge(bank_done[lead], n)

                def modulation(n, k):
                    key = ("mod", n)
                    p = pieces.first[key] + k // 2
                    if k == 0:
                        acquire(key)
                    if k % 2 == 0:
                        pe.wait_ge(raw_in[p % 3], pieces.loaded[p])
                    mm = pe.matmul(pb[0:2, psum.bank(key), :], csil[:, k, :], raw[:, p % 3, k % 2, :],
                                   start=(k == 0), stop=(k == KD - 1))
                    if k == KD - 1:
                        mm.then_inc(*full(key))
                    elif k % 2:
                        mm.then_inc(mod_used, 1)

                def product(chunk, lhs, keys, width=HALF, tile_ready=None):
                    first, count = pieces.first[chunk], pieces.chunk[chunk]
                    for i in range(count):
                        piece = pieces.order[first + i]
                        pe.wait_ge(raw_used, piece + 1)
                        for t in range(T):
                            if i == 0:
                                acquire(keys[t])
                                if tile_ready:
                                    tile_ready(t)
                            dst = pb[:, psum.bank(keys[t]), 0:width]
                            for j in range(2):
                                k = 2 * i + j
                                for n, (a, w) in enumerate(((0, 0), (0, 1), (1, 0))):
                                    mm = pe.matmul(dst, lhs(a, k, t), wsp[:, piece % 2, w, j, 0:width],
                                                   start=(k == 0 and n == 0),
                                                   stop=(i == count - 1 and j == 1 and n == 2))
                            if i == count - 1:
                                mm.then_inc(*full(keys[t]))
                        if i < count - 1:
                            mm.then_inc(split_used, 1)

                def act_lhs(a, k, t):
                    return act_T[:, a, k, tile_cols(t)]

                def y_lhs(a, k, t):
                    return yT[:, a, k, tile_cols(t)]

                def project(chunk, lhs=act_lhs, width=HALF, tile_ready=None):
                    product(chunk, lhs, [(*chunk, t) for t in range(T)], width, tile_ready)

                def transpose_blocks(key, src, n, ready=None):
                    acquire(key)
                    for i in range(n):
                        b = psum.bank(key) + i // 4
                        mm = pe.transpose(pb[:, b, tile_cols(i % 4)], src(i), ident[:, :])
                    mm.then_inc(*full(key))

                for n in range(4):
                    for k in range(KD):
                        modulation(n, k)
                acquire("modT")
                for n in range(4):
                    wait_done(pe, ("mod", n))
                for i in range(2 * KD):
                    mm = pe.transpose(pb[:, 6, 2 * i:2 * i + 2], modrow[:, tile_cols(i)], ident[0:2, 0:2])
                mm.then_inc(*full("modT"))
                for t in range(T):
                    pe.wait_ge(xn_ready, t + 1)
                    transpose_blocks(("xT", t), lambda i: xh[:, t, tile_cols(i)], KD)

                project(("kv",), tile_ready=lambda t: pe.wait_ge(u_ready, t + 1))

                def gates():
                    for n in (4, 5):
                        wait_done(pe, ("mod", n))
                    for i in range(4):
                        acquire(("gate", i))
                        which, hf = i // 2, i % 2
                        pe.matmul(bank(("gate", i)), ident[0:2, which:which + 1].to_broadcast([2, P]),
                                  grow[:, hf * HALF:(hf + 1) * HALF], start=True, stop=True)\
                            .then_inc(*full(("gate", i)))

                def attention(br):
                    bi = 0 if br == "A" else 1
                    kv_of = kvt if br == "A" else kv2
                    project((br, "q"))
                    for t in range(T + 1):
                        pe.wait_ge(k_ready, bi * (T + 1) + t + 1)
                        transpose_blocks((br, "kT", t), lambda i: ks[:, t, i // 2, i % 2, :, :]
                                         .rearrange("p a d -> p (a d)"), 2 * KV)
                    project((br, "z"))
                    for t in range(T):
                        pe.wait_ge(q_ready, bi * T + t + 1)
                        transpose_blocks((br, "qT", t),
                                         lambda i: tokq[:, t, i, :, :].rearrange("p a d -> p (a d)"), NH)
                        wait_done(pe, (br, "z", t))
                        transpose_blocks((br, "zT", t), lambda i: zt[:, t, tile_cols(i)], 4)
                    for t in range(T + 1):
                        if t < T:
                            wait_done(pe, (br, "qT", t))
                        wait_done(pe, (br, "kT", t))

                    def scores(s):
                        h, t = UNITS[s]
                        kv = h // (NH // KV)
                        key = (br, "S", s)
                        blocks = key_blocks(br, t)
                        own = [b for b in blocks if b < T]
                        n = len(own) * P
                        acquire(key)
                        q = qT[:, h, tile_cols(t)]
                        if T in blocks:
                            dst = pb[:, psum.bank(key) + 1, 0:P] if br == "A" else pb[:, psum.bank(key), n:n + P]
                            for a in range(2):
                                pe.matmul(dst, q, kT[:, kv, a, TOK:TOK + P], start=(a == 0), stop=(a == 1))
                        last = []
                        if br == "C" and t < LT:
                            last = [(own.index(b), m) for b, m in ((t - 1, 1), (t + 1, 2)) if b in own]
                        for a in range(2):
                            mm = pe.matmul(pb[:, psum.bank(key), 0:n], q,
                                           kT[:, kv, a, own[0] * P:own[0] * P + n],
                                           start=(a == 0), stop=(a == 1 and not last))
                        for i, m in last:
                            mm = pe.matmul(pb[:, psum.bank(key), tile_cols(i)], masks[:, 0, :], masks[:, m, :],
                                           start=False, stop=(i == last[-1][0]))
                        mm.then_inc(*full(key))

                    def probs_T(s):
                        h, t = UNITS[s]
                        n = len(key_blocks(br, t))
                        pe.wait_ge(p_ready, bi * len(UNITS) + s + 1)
                        for i in range(n):
                            key = (br, "P5" if i == 4 else "PT", s)
                            if i % 4 == 0:
                                acquire(key)
                            mm = pe.transpose(pb[:, psum.bank(key), tile_cols(i % 4)], pr[:, s % 3, tile_cols(i)],
                                              ident[:, :])
                            if i in (3, n - 1):
                                mm.then_inc(*full(key))

                    def values(v):
                        h, b = v // LT, v % LT
                        kv, j, o = h // (NH // KV), h // 2, psum.bank((br, "O", h // 2))
                        r = slice((h % 2) * HD, (h % 2 + 1) * HD)
                        vs = slice(kv * HD, (kv + 1) * HD)
                        if b == 0:
                            if h % 2 == 0:
                                acquire((br, "O", j))
                            wait_done(pe, (br, "P5" if br == "A" else "PT", LT * h + LT - 1))
                            pe.matmul(pb[r, o, :], cached[:, bi, 1, vs], pT[:, h % 2, LT * HALF:T * HALF],
                                      start=True, stop=False)
                        q0, q1 = (0, LT) if br == "A" else (max(b - 1, 0), min(b + 2, LT))
                        mm = pe.matmul(pb[r, o, q0 * P:q1 * P], kv_of[:, b, 1, vs],
                                       pT[:, h % 2, b * HALF + q0 * P:b * HALF + q1 * P],
                                       start=False, stop=(b == LT - 1))
                        if b == LT - 1:
                            if h % 2:
                                mm.then_inc(*full((br, "O", j)))
                            else:
                                mm.then_inc(pv_even, 1)

                    def context_values(h):
                        kv, r = h // (NH // KV), slice((h % 2) * HD, (h % 2 + 1) * HD)
                        if h == 0:
                            acquire((br, "Octx"))
                        wait_done(pe, (br, "PT", NL + h))
                        mm = pe.matmul(pb[r, psum.bank((br, "Octx")), tile_cols(h // 2)],
                                       kv_of[:, LT, 1, kv * HD:(kv + 1) * HD], pT[:, h % 2, T * HALF:],
                                       start=True, stop=True)
                        if h == NH - 1:
                            mm.then_inc(*full((br, "Octx")))
                        else:
                            mm.then_inc(pv_context, 1)

                    for s in range(STEPS):
                        if s < len(UNITS):
                            scores(s)
                        if 2 <= s < len(UNITS) + 2:
                            probs_T(s - 2)
                        if br == "C" and s < 2 * KD:
                            modulation(4 + s // KD, s % KD)
                        if 0 <= s - PV_AFTER < NL:
                            values(s - PV_AFTER)
                        if s >= NL + 3:
                            context_values(s - NL - 3)
                    if br == "C":
                        gates()

                def mlstm():
                    project(("B", "qk"))
                    project(("B", "v"))
                    pe.wait_ge(gw_ready, 1)
                    for i, cs in enumerate((slice(0, HALF), slice(HALF, TOK))):
                        acquire(("B", "gates", i))
                        for k in range(KD):
                            for n, (a, w) in enumerate(((0, 0), (0, 1), (1, 0))):
                                mm = pe.matmul(pb[:, psum.bank(("B", "gates", i)), 0:cs.stop - cs.start],
                                               gw[:, w, k, :], act_T[:, a, k, cs],
                                               start=(k == 0 and n == 0), stop=(k == KD - 1 and n == 2))
                        mm.then_inc(*full(("B", "gates", i)))
                    project(("B", "o"))
                    for t in range(T):
                        wait_done(pe, ("B", "qk", t))
                        transpose_blocks(("B", "qkT", t), lambda i: tokqk[:, t, i // 2, tile_cols(i % 2)], 4)
                    transpose_blocks(("B", "C0T"), lambda i: C0[:, i // 2, 2 * (i % 2):2 * (i % 2) + 2, :]
                                     .rearrange("v h d -> v (h d)"), 4)
                    project(("B", "z"))
                    pe.wait_ge(rows_act, 4)
                    for t in range(T):
                        acquire(("B", "cols", t))
                        for i, r in enumerate((rw, r1, rb, rf)):
                            mm = pe.transpose(pb[:, psum.bank(("B", "cols", t)), i * GR:(i + 1) * GR],
                                              r[0:GR, tile_cols(t)], ident[0:GR, 0:GR])
                        mm.then_inc(*full(("B", "cols", t)))
                    acquire(("B", "wcb"))
                    for d in range(2):
                        last = r1[0:GR, (P - 1 if d == 0 else 0)::P]
                        for h in range(MH):
                            r = ROW0[d] + h
                            n = (2 * d + h // 2) * T
                            mm = pe.matmul(pb[(h % 2) * HD:(h % 2 + 1) * HD, psum.bank(("B", "wcb")), n:n + T],
                                           ident[0:GR, r:r + 1].to_broadcast([GR, HD]), last,
                                           start=True, stop=True)
                    mm.then_inc(*full(("B", "wcb")))
                    for t in range(T):
                        wait_done(pe, ("B", "qkT", t))
                        wait_done(pe, ("B", "v", t))

                    def scores(k):
                        d, t = CHUNKS[k]
                        acquire(("B", "ST", k))
                        for j in range(2):
                            mm = pe.matmul(pb[:, psum.bank(("B", "ST", k)), j * 2 * P:(j + 1) * 2 * P],
                                           kTm[:, j, tile_cols(t)], qz[:, t, j, :, :].rearrange("p b q -> p (b q)"),
                                           start=True, stop=True)
                        mm.then_inc(*full(("B", "ST", k)))
                        acquire(("B", "GB", k))
                        b = psum.bank(("B", "GB", k))
                        pe.matmul(pb[:, b, :].rearrange("p (h q) -> p h q", h=MH), masks[:, 0, :],
                                  masks[:, 3 + d, :].unsqueeze(1).to_broadcast([P, MH, P]), start=True, stop=False)
                        pe.wait_ge(rgd_ready, k + 1)
                        pe.matmul(pb[:, b, :], ones[:, :], rgd[:, k % 2, :, :].rearrange("p h q -> p (h q)"),
                                  start=False, stop=True).then_inc(*full(("B", "GB", k)))

                    def outputs(k):
                        d, t = CHUNKS[k]
                        w = DV + 1
                        acquire(("B", "ND", k))
                        wait_done(pe, ("B", "ST", k))
                        for h in range(MH):
                            dst = pb[:, psum.bank(("B", "ND", k)) + h % 2, (h // 2) * 256:(h // 2) * 256 + w]
                            mm = pe.matmul(dst, sT[:, k % 2, h % 2, h // 2, :], v1[:, t, h, :], start=True, stop=True)
                        mm.then_inc(*full(("B", "ND", k)))
                        if t != LT:
                            acquire(("B", "IN", k))
                            wait_done(pe, ("B", "CS", k - 2) if k >= 2 else ("B", "C0T"))
                            for h in range(MH):
                                dst = pb[:, psum.bank(("B", "IN", k)) + h % 2, (h // 2) * 256:(h // 2) * 256 + w]
                                mm = pe.matmul(dst, qz[:, t, h // 2, h % 2, :], CT[:, d, h // 2, :],
                                               start=True, stop=True)
                            mm.then_inc(*full(("B", "IN", k)))
                        acquire(("B", "CS", k))
                        pe.wait_ge(kw_ready, k + 1)
                        b = psum.bank(("B", "CS", k))
                        if t != LT:
                            for h in range(MH):
                                r = slice((h % 2) * HD, (h % 2 + 1) * HD)
                                mm = pe.matmul(pb[r, b, (h // 2) * 256:(h // 2) * 256 + w],
                                               kw[:, k % 2, h * HD:(h + 1) * HD], v1[:, t, h, :],
                                               start=True, stop=True)
                        else:
                            for h in range(MH):
                                pe.matmul(pb[:, b, h * HD:(h + 1) * HD], v1[:, t, h, 0:DV],
                                          kw[:, k % 2, h * HD:(h + 1) * HD], start=True, stop=True)
                            mm = pe.matmul(pb[0:1, b, 256:512], ones[:, 0:1], kw[:, k % 2, :],
                                           start=True, stop=True)
                        mm.then_inc(*full(("B", "CS", k)))

                    for t in range(T):
                        wait_done(pe, ("B", "cols", t))
                    for k in range(len(CHUNKS) + 1):
                        if k < len(CHUNKS):
                            scores(k)
                        if k >= 1:
                            outputs(k - 1)
                    for t in range(T):
                        pe.wait_ge(hy_ready, t + 1)
                        transpose_blocks(("B", "yT", t), lambda i: hs[:, t, tile_cols(i)], 4)

                for bi, br in enumerate(MERGE_ORDER):
                    if br == "B":
                        mlstm()
                    else:
                        attention(br)
                    for hf in range(2):
                        project((br, "G", hf))
                        if hf == 0:
                            wait_y(pe, bi, br)
                        project((br, "BR", hf), y_lhs)
                for t in range(T):
                    pe.wait_ge(merged_ready, t + 1)
                    transpose_blocks(("mT", t), lambda i: merged[:, t, tile_cols(i)], KD)
                for hf in range(2):
                    project(("out", hf), tile_ready=(lambda t: wait_done(pe, ("mT", t))) if hf == 0 else None)
                meet(pe, "pe", l)

        @block.scalar
        def _(act):
            act.dma_start(xh[:, 0:LT, :], x_sample.rearrange("a (t p) d -> p (a t) d", p=P)).then_inc(first_in, 16)
            act.dma_start(xh[:, LT, :], x_prompt[0, :, :]).then_inc(first_in, 16)
            act.dma_start(rope[:, :, :, :].rearrange("p a t d -> p (a t d)"),
                          consts[:, P:P + 2 * LT * HD]).then_inc(first_in, 16)
            act.dma_start(cst[:, :, :].rearrange("p a q -> p (a q)"),
                          consts[:, P + 2 * LT * HD:]).then_inc(first_in, 16)
            act.dma_start(y_sample[0, :, :], x_sample[0, :, :]).then_inc(x_saved, 16)
            act.dma_start(y_prompt[0, :, :], x_prompt[0, :, :]).then_inc(x_saved, 16)
            act.wait_ge(c_in, 48)
            act.activation(crow[:, 1, :], crow[:, 0, :], ACT.Tanh, scale=0.5).then_inc(init_act, 1)
            act.wait_ge(init_pe, 1)
            act.mul(csil[:, :, :].rearrange("p k w -> p w k"),
                    pb[:, 7, 0:2 * KD].rearrange("p (w k) -> p w k", w=2), 0.5).then_inc(init_act, 1)

            with act.Fori(0, DEPTH) as l:
                steps = [0]

                def step(ins):
                    steps[0] += 1
                    ins.then_inc(act_step, 1)
                    act.wait_ge(act_step, steps[0])

                wait_done(act, "modT")
                for t in range(T):
                    w = 1 if t == LT else 0
                    wait_full(act, ("xT", t))
                    if t >= 2:
                        act.wait_ge(u_ready, t - 1)
                    src = pair(("xT", t), P)
                    for k in range(KD // 2, KD):
                        ins = act.activation(utmp[:, t % 2, k, :], src[:, k, :], ACT.Identity,
                                             scale=modc[:, KD + k, w:w + 1], bias=modc[:, k, w:w + 1])
                    step(ins)
                    act.wait_ge(u_half, t + 1)
                    act.copy(act_T[:, 0, :, tile_cols(t)], utmp[:, t % 2, :, :]).then_inc(*done(("xT", t)))

                for t in range(T):
                    wait_full(act, ("kv", t))
                    for i, kv in enumerate((kvt, kv2)):
                        ins = act.copy(kv[:, t, :, :].rearrange("p a d -> p (a d)"),
                                       bank(("kv", t))[:, i * 256:(i + 1) * 256])
                    ins.then_inc(*done(("kv", t)))

                def attention(br):
                    bi = 0 if br == "A" else 1
                    kv_of = kvt if br == "A" else kv2

                    def hi_part(i):
                        if br == "A":
                            p = pieces.first[("A", "z")] + i
                            wait_piece(act, p)
                            act.copy(wsp[:, pieces.order[p] % 2, 0, :, :], raw[:, p % 3, :, :]).then_inc(hi_by_act, 1)

                    act.wait_ge(k_done, bi + 1)
                    if br == "A":
                        act.wait_ge(small_in, 16 * 17)
                    for t in range(T + 1):
                        src = kv_of[:, t, 0, :] if t < T else cached[:, bi, 0, :]
                        act.copy(ks[:, t, :, 0, :, :].bitcast(F32R),
                                 src.rearrange("p (v d) -> p v d", v=KV).unsqueeze(2)
                                 .to_broadcast([P, KV, 2, HD])).then_inc(k_hi, 1)
                    hi_part(0)
                    for t in range(T):
                        if t == 3:
                            hi_part(1)
                        wait_full(act, (br, "q", t))
                        act.mul(tokq[:, t, :, 1, :], bank((br, "q", t)).rearrange("p (h d) -> p h d", h=NH),
                                1.0 if br == "A" else SCALE).then_inc(*done((br, "q", t)))
                    for t in range(T + 1):
                        wait_full(act, (br, "kT", t))
                        act.copy(kT[:, :, :, tile_cols(t)].rearrange("p v a q -> p (v a) q"),
                                 bank((br, "kT", t)).rearrange("p (v q) -> p v q", v=4))\
                            .then_inc(*done((br, "kT", t)))
                    for t in range(T):
                        if t < 2:
                            hi_part(2 + t)
                        if br == "C" and t == LT:
                            wait_done(act, (br, "q", t))
                        else:
                            act.wait_ge(pre_done, bi * T + t + 1)
                        act.copy(tokq[:, t, :, 0, :].bitcast(F32R), tokq[:, t, :, 1, :]).then_inc(q_hi, 1)
                    for t in range(T):
                        wait_full(act, (br, "z", t))
                        act.activation(zt[:, t, :], bank((br, "z", t)), ACT.Tanh, scale=0.5).then_inc(z_tanh, 1)
                    for t in range(T):
                        wait_full(act, (br, "qT", t))
                        act.copy(qT[:, :, tile_cols(t)], pair((br, "qT", t), P)).then_inc(*done((br, "qT", t)))
                    wait_full(act, (br, "zT", T - 1))

                    def exponent(s):
                        h, t = UNITS[s]
                        n = len(key_blocks(br, t)) * P
                        act.wait_ge(nm_ready, bi * len(UNITS) + s + 1)
                        if s >= 3:
                            wait_full(act, (br, "PT", s - 3))
                        b = psum.bank((br, "S", s))
                        src = pb[:, b:b + 2, :].rearrange("p b n -> p (b n)")[:, 0:n]
                        if br == "C":
                            act.activation(sexp[:, s % 4:s % 4 + 1], sink[:, 0, h:h + 1], ACT.Exp,
                                           bias=nm[:, s % 4:s % 4 + 1]).then_inc(sink_done, 1)
                        act.activation(pr[:, s % 3, 0:n], src, ACT.Exp, bias=nm[:, s % 4:s % 4 + 1],
                                       accum_out=lsum[:, s % 4:s % 4 + 1]).then_inc(*done((br, "S", s)))

                    def evacuate_PT(s):
                        h, t = UNITS[s]
                        key = (br, "PT", s)
                        blocks = key_blocks(br, t)
                        wait_full(act, key)
                        src = bank(key).rearrange("p (b q) -> p b q", q=P)
                        if t == LT:
                            if h >= 2:
                                act.wait_ge(pv_context, bi * (NH - 1) + h - 1)
                            act.copy(pT[:, h % 2, T * HALF:], src[:, 0, :]).then_inc(*done(key))
                            return
                        if h >= 2 and t == 0:
                            if h % 2:
                                wait_full(act, (br, "O", (h - 2) // 2))
                            else:
                                act.wait_ge(pv_even, bi * (NH // 2) + h // 2)
                        dst = pT[:, h % 2, 0:T * HALF].rearrange("p (b q) -> p b q", b=T)[:, :, tile_cols(t)]
                        if br == "A":
                            act.copy(dst[:, 0:LT, :], src).then_inc(*done(key))
                            key = (br, "P5", s)
                            wait_full(act, key)
                            act.copy(dst[:, LT, :], bank(key)[:, 0:P]).then_inc(*done(key))
                        else:
                            n = len(blocks) - 1
                            act.copy(dst[:, blocks[0]:blocks[0] + n, :], src[:, 0:n, :])
                            act.copy(dst[:, LT, :], src[:, n, :]).then_inc(*done(key))

                    for s in range(STEPS + 1):
                        if br == "C" and s < len(UNITS):
                            exponent(s)
                        if 2 <= s < len(UNITS) + 2:
                            evacuate_PT(s - 2)
                        if br == "A" and s < len(UNITS):
                            exponent(s)
                        v = s - PV_AFTER - 1
                        if 0 < v <= NL and v % (2 * LT) == 0:
                            j = v // (2 * LT) - 1
                            wait_done(act, (br, "O", j))
                            act.copy(yT[:, 0, j, 0:HALF], ytmp[:, :]).then_inc(y_hi, 1)
                    wait_done(act, (br, "Octx"))
                    act.copy(yT[:, 0, :, HALF:TOK], ytmp[:, :].rearrange("p (j q) -> p j q", j=4)).then_inc(y_hi, 1)
                    if br == "C":
                        act.wait_ge(stored, 64)
                        for i in range(4):
                            wait_full(act, ("gate", i))
                            act.copy(gate_bc[:, i // 2, (i % 2) * HALF:(i % 2 + 1) * HALF], bank(("gate", i)))\
                                .then_inc(*done(("gate", i)))

                def mlstm():
                    for t in range(T):
                        wait_full(act, ("B", "qk", t))
                        src = bank(("B", "qk", t))
                        act.copy(tokqk[:, t, 0, :], src[:, 0:256])
                        act.mul(tokqk[:, t, 1, :], src[:, 256:512], SCALE).then_inc(*done(("B", "qk", t)))
                    act.wait_ge(rows_dve, 1)
                    act.activation(r1[0:GR, :], r1[0:GR, :], ACT.Exp).then_inc(rows_act, 1)
                    act.wait_ge(rows_act, 1)
                    act.activation(r1[0:GR, :], r1[0:GR, :], ACT.Ln, bias=1.0).then_inc(rows_act, 1)
                    for t in range(T):
                        wait_full(act, ("B", "o", t))
                        act.activation(zo[:, t, :], bank(("B", "o", t)), ACT.Tanh, scale=0.5)\
                            .then_inc(*done(("B", "o", t)))
                    for t in range(T):
                        wait_full(act, ("B", "qkT", t))
                        src = bank(("B", "qkT", t)).rearrange("p (a j q) -> p a j q", a=2, j=2)
                        if t == 0:
                            act.wait_ge(qz_zero, 1)
                        for b in range(2):
                            r = slice(b * HD, (b + 1) * HD)
                            act.copy(qz[r, t, :, b, :], src[r, 0])
                        act.copy(kTm[:, :, tile_cols(t)], src[:, 1]).then_inc(*done(("B", "qkT", t)))
                    act.wait_ge(rows_dve, 2)
                    act.activation(r1[0:GR, :], r1[0:GR, :], ACT.Exp, scale=-1.0)
                    act.activation(rb[0:GR, :], rb[0:GR, :], ACT.Exp, scale=-1.0).then_inc(rows_act, 1)
                    act.activation(rf[0:GR, :], rf[0:GR, :], ACT.Exp).then_inc(rows_act, 1)
                    for t in range(T):
                        wait_full(act, ("B", "z", t))
                        if t >= 2:
                            act.wait_ge(zo_ready, t - 1)
                        act.activation(em[:, t % 2, :, :].rearrange("p b n -> p (b n)"), bank(("B", "z", t)), ACT.Tanh,
                                       scale=0.5).then_inc(z_tanh, 1)
                    for k, (d, t) in enumerate(CHUNKS):
                        wait_full(act, ("B", "GB", k))
                        wait_done(act, ("B", "cols", T - 1))
                        if k == 0:
                            act.wait_ge(zo_ready, T)
                        if k >= 2:
                            wait_done(act, ("B", "ST", k - 2))
                        b = psum.bank(("B", "GB", k))
                        for h in range(MH):
                            ins = act.activation(em[:, k % 2, h % 2, tile_cols(h // 2)], pb[:, b, tile_cols(h)], ACT.Exp,
                                                 bias=cols[:, t, 0, ROW0[d] + h:ROW0[d] + h + 1], scale=-1.0)
                        ins.then_inc(*done(("B", "GB", k)))
                    for t in range(T):
                        wait_full(act, ("B", "yT", t))
                        act.copy(yT[:, 0, :, tile_cols(t)], bank(("B", "yT", t)).rearrange("p (j q) -> p j q", j=4))\
                            .then_inc(y_hi, 1)

                for bi, br in enumerate(MERGE_ORDER):
                    if br == "B":
                        mlstm()
                    else:
                        attention(br)
                    for hf in range(2):
                        for t in range(T):
                            wait_full(act, (br, "G", hf, t))
                            if hf == 0 and t == 0:
                                wait_y(act, bi, br)
                            elif hf:
                                wait_done(act, (br, "BR", 0, t))
                            act.activation(tg[:, t, :], bank((br, "G", hf, t)), ACT.Tanh, scale=0.5)\
                                .then_inc(*done((br, "G", hf, t)))
                for t in range(T):
                    wait_full(act, ("mT", t))
                    act.mul(act_T[:, 0, :, tile_cols(t)], pair(("mT", t), P), 0.5).then_inc(m_hi, 1)
                for t in range(LT):
                    act.wait_ge(centred, t + 1)
                    act.wait_ge(rstd_ready, 3 + T + t)
                    act.mul(xh[:, t, :], xh[:, t, :], rstd[:, t:t + 1]).then_inc(scaled, 1)
                meet(act, "act", l)

        @block.vector
        def _(dve):
            dve.wait_ge(init_act, 1)
            dve.scalar_tensor_tensor(out=crow[:, 2, :], in0=crow[:, 1, :], scalar=1.0, in1=crow[:, 0, :],
                                     op0=ALU.add, op1=ALU.mult).then_inc(init_dve, 1)
            dve.memset(ones[:, :], 1.0)
            dve.wait_ge(first_in, 4 * 16)
            dve.tensor_copy(masks[:, 1:5, :], cst[:, :, :])
            dve.tensor_copy(masks[:, 0, :], ident[:, :])

            with dve.Fori(0, DEPTH) as l:
                steps = [0]

                def step(ins):
                    steps[0] += 1
                    ins.then_inc(dve_step, 1)
                    dve.wait_ge(dve_step, steps[0])

                def marked(ins):
                    steps[0] += 1
                    ins.then_inc(dve_step, 1)
                    return steps[0]

                for t in range(T):
                    for i in range(2):
                        ins = dve.bn_stats(out=stats[:, t, i, :], in_=xh[:, t, i * HALF:(i + 1) * HALF])
                step(ins)
                for t in range(T):
                    ins = dve.bn_aggr(out=mv[:, t, :], in_=stats[:, t, :, :].rearrange("p a b -> p (a b)"))
                step(ins)
                dve.tensor_scalar(ve[:, :], mv[:, :, 1], EPS, None, ALU.add).then_inc(var_ready, 1)
                dve.wait_ge(small_in, 16 * 17)
                for n in range(4):
                    wait_full(dve, ("mod", n))
                    cs = slice(n * HALF, (n + 1) * HALF)
                    dve.tensor_tensor(modrow[:, cs], pb[0:2, psum.bank(("mod", n)), :], bmod[:, cs], ALU.add)\
                        .then_inc(*done(("mod", n)))
                    if n == 0:
                        dve.wait_ge(rstd_ready, 1)
                        for t in range(T):
                            dve.tensor_scalar(xh[:, t, :], xh[:, t, :], mv[:, t, 0:1], rstd[:, t:t + 1],
                                              ALU.subtract, ALU.mult).then_inc(xn_ready, 1)
                wait_full(dve, "modT")
                src = bank("modT")[:, 0:4 * KD].rearrange("p (k w) -> p k w", w=2)
                dve.tensor_copy(modc[:, 0:KD, :], src[:, 0:KD, :])
                dve.tensor_scalar(modc[:, KD:2 * KD, :], src[:, KD:2 * KD, :], 1.0, None, ALU.add)\
                    .then_inc(*done("modT"))
                wait_done(dve, "modT")

                def u_lo(t):
                    wait_done(dve, ("xT", t))
                    dve.tensor_tensor(act_T[:, 1, :, tile_cols(t)], utmp[:, t % 2, :, :],
                                      act_T[:, 0, :, tile_cols(t)].bitcast(F32), ALU.subtract).then_inc(u_ready, 1)

                for t in range(T):
                    w = 1 if t == LT else 0
                    wait_full(dve, ("xT", t))
                    if t >= 2:
                        dve.wait_ge(u_ready, t - 1)
                    src = pair(("xT", t), P)
                    for k in range(KD // 2):
                        ins = dve.tensor_scalar(utmp[:, t % 2, k, :], src[:, k, :], modc[:, KD + k, w:w + 1],
                                                modc[:, k, w:w + 1], ALU.mult, ALU.add)
                    ins.then_inc(u_half, 1)
                    if t:
                        u_lo(t - 1)
                u_lo(T - 1)

                def attention(br):
                    bi = 0 if br == "A" else 1
                    kv_of = kvt if br == "A" else kv2
                    if br == "C":
                        step(dve.tensor_scalar(sink[:, 1, :], sink[:, 0, :], -1.0, None, ALU.mult))
                    if br == "A":
                        step(dve.tensor_scalar(gains[:, 0, :], gains[:, 0, :], SCALE, None, ALU.mult))
                    wait_done(dve, ("kv", T - 1))
                    k = kv_of[:, :, 0, :].rearrange("p t (v d) -> p t v d", v=KV)
                    rk = rtmp[:, :].rearrange("p (t v d) -> p t v d", t=T, v=KV)
                    if br == "A":
                        step(dve.tensor_tensor(rk, k, k, ALU.mult))
                        step(dve.tensor_reduce(msk[:, :], rtmp[:, :].rearrange("p (n d) -> p n d", d=HD),
                                               AX.X, ALU.add))
                        dve.tensor_scalar(msk[:, :], msk[:, :], 1.0 / HD, EPS, ALU.mult, ALU.add)\
                            .then_inc(var_ready, 1)
                        dve.wait_ge(rstd_ready, 2)
                        step(dve.tensor_tensor(k, k, rmsk[:, :].rearrange("p (t v) -> p t v", t=T).unsqueeze(3)
                                               .to_broadcast([P, T, KV, HD]), ALU.mult))
                        step(dve.tensor_tensor(k, k, gains[:, 1, :].unsqueeze(1).unsqueeze(1)
                                               .to_broadcast([P, T, KV, HD]), ALU.mult))
                    for v in range(KV):
                        x4, r4 = (x[:, 0:LT, v, :].rearrange("p t (a i) -> p t a i", a=4) for x in (k, rk))
                        s4 = rope[:, 1, :, :].rearrange("p t (a i) -> p t a i", a=4)
                        for a in range(2):
                            ins = dve.tensor_tensor(r4[:, :, a::2, :], x4[:, :, 1 - a::2, :], s4[:, :, a::2, :], ALU.mult)
                    step(ins)
                    step(dve.tensor_tensor(k[:, 0:LT], k[:, 0:LT], rope[:, 0, :, :].unsqueeze(2)
                                           .to_broadcast([P, LT, KV, HD]), ALU.mult))
                    dve.tensor_tensor(k[:, 0:LT], k[:, 0:LT], rk[:, 0:LT], ALU.add).then_inc(k_done, 1)
                    dve.wait_ge(k_done, bi + 1)
                    for t in range(T + 1):
                        dve.wait_ge(k_hi, bi * (T + 1) + t + 1)
                        src = (kv_of[:, t, 0, :] if t < T else cached[:, bi, 0, :]).rearrange("p (v d) -> p v d", v=KV)
                        for e in range(2):
                            ins = dve.tensor_tensor(ks[:, t, :, 1, e, :], src, ks[:, t, :, 0, e, :],
                                                    ALU.subtract)
                        ins.then_inc(k_ready, 1)
                    if br == "A":
                        for t in range(T):
                            wait_done(dve, (br, "q", t))
                            q = tokq[:, t, :, 1, :]
                            step(dve.tensor_tensor(rtmp[:, 0:512].rearrange("p (h d) -> p h d", h=NH), q, q, ALU.mult))
                            step(dve.tensor_reduce(ms[:, t, :], rtmp[:, 0:512].rearrange("p (h d) -> p h d", d=HD),
                                                   AX.X, ALU.add))
                            dve.tensor_scalar(ms[:, t, :], ms[:, t, :], 1.0 / HD, EPS, ALU.mult, ALU.add)\
                                .then_inc(var_ready, 1)

                    def q_lo(t):
                        dve.wait_ge(q_hi, bi * T + t + 1)
                        dve.tensor_tensor(tokq[:, t, :, 1, :], tokq[:, t, :, 1, :], tokq[:, t, :, 0, :],
                                          ALU.subtract).then_inc(q_ready, 1)

                    for t in range(T):
                        q = tokq[:, t, :, 1, :]
                        if br == "A":
                            dve.wait_ge(rstd_ready, 3 + t)
                            step(dve.tensor_tensor(q, q, rms[:, t, :].unsqueeze(2).to_broadcast([P, NH, HD]), ALU.mult))
                            ins = dve.tensor_tensor(q, q, gains[:, 0, :].unsqueeze(1).to_broadcast([P, NH, HD]),
                                                    ALU.mult)
                            if t < LT:
                                step(ins)
                            else:
                                ins.then_inc(pre_done, 1)
                        else:
                            wait_done(dve, (br, "q", t))
                        if t < LT:
                            if t:
                                dve.wait_ge(pre_done, bi * T + t)
                            tmp = rtmp[:, 0:512].rearrange("p (n a i) -> p n a i", n=NH, a=4)
                            x4 = q.rearrange("p n (a i) -> p n a i", a=4)
                            sn = rope[:, 1, t, :].rearrange("p (a i) -> p a i", a=4)
                            for a in range(2):
                                ins = dve.tensor_tensor(tmp[:, :, a::2, :], x4[:, :, 1 - a::2, :],
                                                        sn[:, a::2, :].unsqueeze(1).to_broadcast([P, NH, 2, 16]),
                                                        ALU.mult)
                            step(ins)
                            step(dve.tensor_tensor(q, q, rope[:, 0, t, :].unsqueeze(1)
                                                   .to_broadcast([P, NH, HD]), ALU.mult))
                            dve.tensor_tensor(q, q, rtmp[:, 0:512].rearrange("p (n d) -> p n d", n=NH), ALU.add)\
                                .then_inc(pre_done, 1)
                        if t:
                            q_lo(t - 1)
                    q_lo(T - 1)
                    for t in range(T):
                        dve.wait_ge(z_tanh, bi * T + t + 1)
                        dve.scalar_tensor_tensor(out=zt[:, t, :], in0=zt[:, t, :], scalar=1.0,
                                                 in1=bank((br, "z", t)), op0=ALU.add, op1=ALU.mult)\
                            .then_inc(*done((br, "z", t)))
                    for t in range(T):
                        wait_full(dve, (br, "zT", t))
                        dve.tensor_copy(zT[:, :, tile_cols(t)], bank((br, "zT", t)).rearrange("p (j q) -> p j q", j=4))\
                            .then_inc(*done((br, "zT", t)))

                    def maximum(s):
                        h, t = UNITS[s]
                        n = len(key_blocks(br, t)) * P
                        wait_full(dve, (br, "S", s))
                        b = psum.bank((br, "S", s))
                        src = pb[:, b:b + 2, :].rearrange("p b n -> p (b n)")[:, 0:n]
                        o = slice(s % 4, s % 4 + 1)
                        if br == "A":
                            dve.tensor_reduce(nm[:, o], src, AX.X, ALU.max, negate=True).then_inc(nm_ready, 1)
                            return
                        reduced = marked(dve.tensor_reduce(nmx[:, o], src, AX.X, ALU.max, negate=True))
                        if s:
                            denominator(s - 1)
                        dve.wait_ge(dve_step, reduced)
                        dve.tensor_tensor(nm[:, o], nmx[:, o], sink[:, 1, h:h + 1], ALU.min).then_inc(nm_ready, 1)

                    den_at = {}

                    def denominator(s):
                        o = slice(s % 4, s % 4 + 1)
                        wait_done(dve, (br, "S", s))
                        dve.wait_ge(sink_done, s + 1)
                        den_at[s] = marked(dve.tensor_tensor(den[:, o], lsum[:, o], sexp[:, o], ALU.add))

                    def normalise(s):
                        h, t = UNITS[s]
                        n = len(key_blocks(br, t)) * P
                        o = slice(s % 4, s % 4 + 1)
                        if br == "C":
                            if s == len(UNITS) - 1:
                                denominator(s)
                            dve.wait_ge(dve_step, den_at[s])
                        else:
                            wait_done(dve, (br, "S", s))
                        total = den if br == "C" else lsum
                        step(dve.reciprocal(rden[:, o], total[:, o]))
                        dve.tensor_scalar(pr[:, s % 3, 0:n], pr[:, s % 3, 0:n], rden[:, o], None, ALU.mult)\
                            .then_inc(p_ready, 1)

                    def gate_out(j):
                        key = (br, "O", j)
                        wait_full(dve, key)
                        if j:
                            dve.wait_ge(y_ready, bi * T + j)
                        dve.scalar_tensor_tensor(out=ytmp[:, :], in0=bank(key), scalar=0.5, in1=zT[:, j, 0:HALF],
                                                 op0=ALU.mult, op1=ALU.mult).then_inc(*done(key))

                    def y_lo(j):
                        dve.wait_ge(y_hi, bi * T + j + 1)
                        cs = slice(0, HALF)
                        dve.tensor_tensor(yT[:, 1, j, cs], ytmp[:, :], yT[:, 0, j, cs].bitcast(F32), ALU.subtract)\
                            .then_inc(y_ready, 1)

                    def gate_row(n):
                        dve.wait_ge(bgate_in, 16)
                        wait_full(dve, ("mod", n))
                        cs = slice((n - 4) * HALF, (n - 3) * HALF)
                        dve.tensor_tensor(grow[:, cs], pb[0:2, psum.bank(("mod", n)), :], grow[:, cs], ALU.add)\
                            .then_inc(*done(("mod", n)))

                    for s in range(STEPS):
                        if s < len(UNITS):
                            maximum(s)
                        if br == "C" and s in (KD, 2 * KD):
                            gate_row(4 + s // KD - 1)
                        v = s - PV_AFTER
                        if 0 < v <= NL and v % (2 * LT) == 0:
                            gate_out(v // (2 * LT) - 1)
                        if 1 <= s < len(UNITS) + 1:
                            normalise(s - 1)
                        if 2 < v <= NL + 2 and (v - 2) % (2 * LT) == 0:
                            y_lo((v - 2) // (2 * LT) - 1)
                    key = (br, "Octx")
                    wait_full(dve, key)
                    dve.wait_ge(y_ready, bi * T + LT)
                    dve.scalar_tensor_tensor(out=ytmp[:, :].rearrange("p (j q) -> p j q", j=4),
                                             in0=bank(key).rearrange("p (j q) -> p j q", j=4), scalar=0.5,
                                             in1=zT[:, :, HALF:TOK], op0=ALU.mult, op1=ALU.mult)\
                        .then_inc(*done(key))
                    dve.wait_ge(y_hi, (bi + 1) * T)
                    dve.tensor_tensor(yT[:, 1, :, HALF:TOK], ytmp[:, :].rearrange("p (j q) -> p j q", j=4),
                                      yT[:, 0, :, HALF:TOK].bitcast(F32), ALU.subtract).then_inc(y_ready, 1)

                def mlstm():
                    wait_full(dve, ("C", "BR", 1, T - 1))
                    step(dve.memset(gw[:, :, :, :].rearrange("p a k n -> p (a k n)").bitcast(F32), 0.0))
                    for d in range(2):
                        for g in range(2):
                            o = 64 * g + ROW0[d]
                            ins = dve.tensor_copy(gw[:, 0, :, o:o + MH], gwraw[:, :, (2 * d + g) * MH:(2 * d + g + 1) * MH])
                    step(ins)
                    for d in range(2):
                        for g in range(2):
                            o = 64 * g + ROW0[d]
                            ins = dve.tensor_tensor(gw[:, 1, :, o:o + MH],
                                                    gwraw[:, :, (2 * d + g) * MH:(2 * d + g + 1) * MH],
                                                    gw[:, 0, :, o:o + MH].bitcast(F32), ALU.subtract)
                    ins.then_inc(gw_ready, 1)
                    wait_full(dve, ("gate", 3))
                    dve.memset(v1[:, :, :, DV:DV + 1], 1.0)
                    dve.memset(rgd[:, :, :, :].rearrange("p a h q -> p (a h q)"), 0.0)
                    dve.memset(rb[0:GR, :], 0.0)
                    step(dve.memset(rg[0:GR, :], 0.0))
                    for t in range(T):
                        wait_full(dve, ("B", "v", t))
                        dve.tensor_copy(v1[:, t, :, 0:DV], bank(("B", "v", t)).rearrange("p (h d) -> p h d", h=MH))\
                            .then_inc(*done(("B", "v", t)))
                    for i, cs in enumerate((slice(0, HALF), slice(HALF, TOK))):
                        wait_full(dve, ("B", "gates", i))
                        b, n = psum.bank(("B", "gates", i)), cs.stop - cs.start
                        dve.tensor_scalar(rw[0:GR, cs], pb[0:GR, b, 0:n], gbias[0:GR, 0:1], None, ALU.add)
                        dve.tensor_scalar(rf[0:GR, cs], pb[64:64 + GR, b, 0:n], gbias[64:64 + GR, 0:1], None,
                                          ALU.add).then_inc(*done(("B", "gates", i)))
                    dve.memset(qz[:, :, :, :, :].rearrange("p t j b q -> p (t j b q)"), 0.0).then_inc(qz_zero, 1)
                    wait_done(dve, ("B", "gates", 1))
                    dve.scalar_tensor_tensor(out=r1[0:GR, :], in0=rf[0:GR, :], scalar=-1.0, in1=rf[0:GR, :],
                                             op0=ALU.mult, op1=ALU.min)\
                        .then_inc(rows_dve, 1)
                    dve.wait_ge(rows_act, 2)
                    step(dve.scalar_tensor_tensor(out=rf[0:GR, :], in0=rf[0:GR, :], scalar=0.0, in1=r1[0:GR, :],
                                                  op0=ALU.min, op1=ALU.subtract))

                    def along(row, d, t):
                        a = row[ROW0[d]:ROW0[d] + MH, tile_cols(t)]
                        return a if d == 0 else a[:, ::-1]

                    for d in range(2):
                        for t in range(T):
                            ins = dve.tensor_tensor_scan(along(rb, d, t), ones[ROW0[d]:ROW0[d] + MH, :],
                                                         along(rf, d, t), 0.0, ALU.mult, ALU.add)
                    step(ins)
                    step(dve.tensor_tensor(rw[0:GR, :], rw[0:GR, :], rb[0:GR, :], ALU.subtract))
                    for n, (d, t) in enumerate(CHUNKS):
                        r = slice(ROW0[d], ROW0[d] + MH)
                        last = t * P + (P - 1 if d == 0 else 0)
                        step(dve.tensor_tensor_scan(along(rg, d, t), along(rw, d, t), along(rw, d, t),
                                                    mcol[r, t:t + 1], ALU.max, ALU.max))
                        to = 5 if t == LT else t + (1 if d == 0 else -1)
                        if t == LT or 0 <= to < LT:
                            step(dve.tensor_tensor(mcol[r, to:to + 1], rb[r, last:last + 1], rg[r, last:last + 1],
                                                   ALU.add))
                    tiles = lambda row: row[0:GR, :].rearrange("p (t q) -> p t q", t=T)
                    dve.tensor_tensor(tiles(r1), tiles(rg), mcol[0:GR, 0:T].unsqueeze(2).to_broadcast([GR, T, P]),
                                      ALU.subtract)
                    dve.tensor_tensor(rb[0:GR, :], rb[0:GR, :], rg[0:GR, :], ALU.add)
                    for d in range(2):
                        r = slice(ROW0[d], ROW0[d] + MH)
                        g3 = rg[r, :].rearrange("p (t q) -> p t q", t=T)[:, :, (P - 1 if d == 0 else 0)]
                        ins = dve.tensor_tensor(rf[r, :].rearrange("p (t q) -> p t q", t=T),
                                                rw[r, :].rearrange("p (t q) -> p t q", t=T),
                                                g3.unsqueeze(2).to_broadcast([MH, T, P]), ALU.subtract)
                    ins.then_inc(rows_dve, 1)
                    wait_full(dve, ("B", "C0T"))
                    for d in range(2):
                        dve.tensor_copy(CT[:, d, :, DV:DV + 1], n0[:, d, :].unsqueeze(2))
                    dve.tensor_copy(CT[:, :, :, 0:DV].rearrange("p a j v -> p (a j) v"),
                                    bank(("B", "C0T")).rearrange("p (a v) -> p a v", a=4))\
                        .then_inc(*done(("B", "C0T")))
                    for t in range(T):
                        dve.wait_ge(z_tanh, 2 * T + t + 1)
                        z = em[:, t % 2, :, :].rearrange("p b n -> p (b n)")
                        dve.scalar_tensor_tensor(out=z, in0=z, scalar=1.0,
                                                 in1=bank(("B", "z", t)), op0=ALU.add, op1=ALU.mult)\
                            .then_inc(*done(("B", "z", t)))
                        wait_done(dve, ("B", "o", t))
                        wait_done(dve, ("B", "z", t))
                        dve.scalar_tensor_tensor(out=zo[:, t, :], in0=zo[:, t, :], scalar=1.0,
                                                 in1=z, op0=ALU.add, op1=ALU.mult)\
                            .then_inc(zo_ready, 1)
                    for t in range(T):
                        wait_full(dve, ("B", "cols", t))
                        dve.tensor_copy(cols[:, t, :, :].rearrange("p a r -> p (a r)"),
                                        bank(("B", "cols", t))[:, 0:4 * GR]).then_inc(*done(("B", "cols", t)))
                    wait_full(dve, ("B", "wcb"))
                    dve.tensor_copy(wcb[:, :, :].rearrange("p a t -> p (a t)"), bank(("B", "wcb"))[:, 0:4 * T])\
                        .then_inc(*done(("B", "wcb")))
                    wait_done(dve, ("B", "wcb"))

                    def col(k, i):
                        d, t = CHUNKS[k]
                        return cols[:, t, i, ROW0[d]:ROW0[d] + MH]

                    def by_head(a, n):
                        return a.rearrange("p (j b) -> p b j", b=2).unsqueeze(3).to_broadcast([P, 2, 2, n])

                    def spread(k):
                        d, t = CHUNKS[k]
                        if k >= 2:
                            wait_full(dve, ("B", "GB", k - 2))
                        own = ident[0:GR, ROW0[d]:ROW0[d] + MH].unsqueeze(2).to_broadcast([GR, MH, P])
                        dve.tensor_tensor(rgd[0:GR, k % 2, :, :], own, rg[0:GR, tile_cols(t)].unsqueeze(1)
                                          .to_broadcast([GR, MH, P]), ALU.mult).then_inc(rgd_ready, 1)

                    def decayed(k):
                        d, t = CHUNKS[k]
                        wait_done(dve, ("B", "cols", t))
                        if k >= 2:
                            wait_full(dve, ("B", "CS", k - 2))
                        dve.tensor_tensor(kw[:, k % 2, :].rearrange("p (h d) -> p h d", h=MH),
                                          tokqk[:, t, 1, :].rearrange("p (h d) -> p h d", h=MH),
                                          col(k, 3).unsqueeze(2).to_broadcast([P, MH, HD]), ALU.mult)\
                            .then_inc(kw_ready, 1)
                        wait_full(dve, ("B", "ST", k))
                        wait_done(dve, ("B", "GB", k))
                        dve.tensor_tensor(sT[:, k % 2, :, :, :],
                                          bank(("B", "ST", k)).rearrange("p (j b q) -> p b j q", j=2, b=2),
                                          em[:, k % 2, :, :].rearrange("p b (j q) -> p b j q", j=2), ALU.mult).then_inc(*done(("B", "ST", k)))
                        if k + 2 < len(CHUNKS):
                            spread(k + 2)

                    seen = set()

                    def combine(k):
                        d, t = CHUNKS[k]
                        b = psum.bank(("B", "ND", k))
                        wide = lambda b: pb[:, b:b + 2, :].rearrange("p b (n i) -> p b n i", i=256)[:, :, :, 0:DV + 1]
                        out = nd[:, k % 2, :, :, :]
                        if t != LT:
                            wait_full(dve, ("B", "IN", k))
                            dve.tensor_tensor(t3[:, :, :, :], wide(psum.bank(("B", "IN", k))),
                                              by_head(col(k, 1), DV + 1), ALU.mult)\
                                .then_inc(*done(("B", "IN", k)))
                            wait_done(dve, ("B", "IN", k))
                            wait_full(dve, ("B", "ND", k))
                            dve.tensor_tensor(out, wide(b), t3[:, :, :, :], ALU.add).then_inc(*done(("B", "ND", k)))
                        else:
                            wait_full(dve, ("B", "ND", k))
                            dve.tensor_copy(out, wide(b)).then_inc(*done(("B", "ND", k)))
                        wait_full(dve, ("B", "CS", k))
                        if t != LT:
                            C = CT[:, d, :, :]
                            step(dve.tensor_tensor(C, C, wcb[:, 2 * d:2 * d + 2, t:t + 1]
                                                   .to_broadcast([P, 2, DV + 1]), ALU.mult))
                            dve.tensor_tensor(C, bank(("B", "CS", k)).rearrange("p (j v) -> p j v", j=2)[:, :, 0:DV + 1],
                                              C, ALU.add).then_inc(*done(("B", "CS", k)))
                        else:
                            dve.tensor_copy(co[:, d, 0:256], bank(("B", "CS", k))[:, 0:256])
                            dve.tensor_copy(co[0:1, d, 256:512], pb[0:1, psum.bank(("B", "CS", k)), 256:512])\
                                .then_inc(*done(("B", "CS", k)))
                        wait_done(dve, ("B", "ND", k))
                        dk, rk = dn[:, k % 2, :, :], rdn[:, k % 2, :, :]
                        step(dve.scalar_tensor_tensor(out=dk, in0=out[:, :, :, DV], scalar=-1.0,
                                                      in1=col(k, 2).rearrange("p (j b) -> p b j", b=2),
                                                      op0=ALU.mult, op1=ALU.max))
                        step(dve.tensor_tensor(dk, dk, out[:, :, :, DV], ALU.max))
                        step(dve.reciprocal(rk, dk))
                        dst = hs[:, t, :] if t not in seen else t4[:, :]
                        step(dve.tensor_tensor(dst.rearrange("p (j b v) -> p b j v", j=2, b=2), out[:, :, :, 0:DV],
                                               rk.unsqueeze(3).to_broadcast([P, 2, 2, DV]), ALU.mult))
                        if t in seen:
                            step(dve.tensor_tensor(hs[:, t, :], hs[:, t, :], t4[:, :], ALU.add))
                        seen.add(t)

                    spread(0)
                    spread(1)
                    for k in range(len(CHUNKS) + 1):
                        if k < len(CHUNKS):
                            decayed(k)
                        if k >= 1:
                            combine(k - 1)
                    for t in range(T):
                        dve.scalar_tensor_tensor(out=hs[:, t, :], in0=hs[:, t, :], scalar=0.25, in1=zo[:, t, :],
                                                 op0=ALU.mult, op1=ALU.mult).then_inc(hy_ready, 1)
                    for t in range(T):
                        dve.wait_ge(y_hi, 2 * T + t + 1)
                        dve.tensor_tensor(yT[:, 1, :, tile_cols(t)],
                                          bank(("B", "yT", t)).rearrange("p (j q) -> p j q", j=4),
                                          yT[:, 0, :, tile_cols(t)].bitcast(F32), ALU.subtract)\
                            .then_inc(*done(("B", "yT", t)))

                for bi, br in enumerate(MERGE_ORDER):
                    if br == "B":
                        mlstm()
                    else:
                        attention(br)
                    for hf in range(2):
                        cs = slice(hf * HALF, (hf + 1) * HALF)
                        for t in range(T):
                            key = (br, "BR", hf, t)
                            wait_full(dve, key)
                            wait_done(dve, (br, "G", hf, t))
                            dst = merged[:, t, cs] if bi == 0 else mt[:, t % 2, :]
                            dve.scalar_tensor_tensor(out=dst, in0=tg[:, t, :], scalar=1.0, in1=bank(key),
                                                     op0=ALU.add, op1=ALU.mult).then_inc(*done(key))
                            if bi:
                                wait_done(dve, key)
                                ins = dve.tensor_tensor(merged[:, t, cs], merged[:, t, cs], mt[:, t % 2, :], ALU.add)
                                if br == MERGE_ORDER[-1] and hf == 1:
                                    ins.then_inc(merged_ready, 1)
                                else:
                                    step(ins)
                for t in range(T):
                    dve.wait_ge(m_hi, t + 1)
                    dve.scalar_tensor_tensor(out=act_T[:, 1, :, tile_cols(t)], in0=pair(("mT", t), P), scalar=0.5,
                                             in1=act_T[:, 0, :, tile_cols(t)].bitcast(F32), op0=ALU.mult,
                                             op1=ALU.subtract).then_inc(*done(("mT", t)))
                dve.wait_ge(late_in, 64)
                def gated(hf, t):
                    key = ("out", hf, t)
                    cs = slice(hf * HALF, (hf + 1) * HALF)
                    wait_full(dve, key)
                    dve.tensor_tensor(ot[:, t % 2, :], bank(key), gate_bc[:, 1 if t == LT else 0, cs], ALU.mult)\
                        .then_inc(*done(key))

                def centre(t):
                    dve.tensor_scalar(ve[:, t:t + 1], mv[:, t, 1:2], EPS, None, ALU.add).then_inc(var_ready, 1)
                    dve.scalar_tensor_tensor(out=xh[:, t, :], in0=xh[:, t, :], scalar=mv[:, t, 0:1],
                                             in1=lnrow[:, 0, :], op0=ALU.subtract, op1=ALU.mult)\
                        .then_inc(centred, 1)

                for i in range(4):
                    wait_done(dve, ("gate", i))
                order = [(hf, t) for hf in range(2) for t in range(T)]
                aggregated = 0
                gated(*order[0])
                for n, (hf, t) in enumerate(order):
                    cs = slice(hf * HALF, (hf + 1) * HALF)
                    wait_done(dve, ("out", hf, t))
                    added = marked(dve.scalar_tensor_tensor(out=xh[:, t, cs], in0=xh[:, t, cs], scalar=ALPHA,
                                                            in1=ot[:, t % 2, :], op0=ALU.mult, op1=ALU.add))
                    if hf and t:
                        dve.wait_ge(dve_step, aggregated)
                        centre(t - 1)
                    dve.wait_ge(dve_step, added)
                    counted = marked(dve.bn_stats(out=stats[:, t, hf, :], in_=xh[:, t, cs]))
                    if n + 1 < len(order):
                        gated(*order[n + 1])
                    if hf:
                        dve.wait_ge(dve_step, counted)
                        aggregated = marked(dve.bn_aggr(out=mv[:, t, :],
                                                        in_=stats[:, t, :, :].rearrange("p a b -> p (a b)")))
                dve.wait_ge(dve_step, aggregated)
                centre(LT)
                dve.wait_ge(rstd_ready, 3 + T + LT)
                dve.wait_ge(centred, T)
                dve.scalar_tensor_tensor(out=xh[:, LT, :], in0=xh[:, LT, :], scalar=rstd[:, LT:LT + 1],
                                         in1=lnrow[:, 1, :], op0=ALU.mult, op1=ALU.add).then_inc(context_ready, 1)
                meet(dve, "dve", l)


def shape_constants():
    import numpy as np
    grid_w, axis = 64, HD // 2
    pos = np.arange(LT * P)
    inv = (10000.0 ** (-np.arange(0, axis, 2, dtype=np.float32) / axis)).astype(np.float32)
    ar = (pos // grid_w).astype(np.float32)[:, None] * inv
    ac = (pos % grid_w).astype(np.float32)[:, None] * inv
    ang = np.concatenate([ar, ar, ac, ac], axis=-1)
    sign = np.repeat(np.array([-1, 1, -1, 1], np.float32), 16)
    tables = [np.cos(ang), np.sin(ang) * sign]
    i = np.arange(P)
    row, col = i[:, None], i[None, :]
    big = np.float32(1e30)
    masks = [np.where(col >= row, 0, -big),
             np.where(col <= row, 0, -big),
             np.where(row <= col, 0, big),
             np.where(row >= col, 0, big)]
    parts = [np.eye(P)]
    parts += [t.reshape(LT, P, HD).transpose(1, 0, 2).reshape(P, LT * HD) for t in tables]
    parts += masks
    return np.concatenate(parts, axis=1).astype(np.float32)


_INS = ["x_prompt", "x_sample", "cache_attn_k", "cache_attn_v", "cache_win_k", "cache_win_v",
        "state_mlstm_C", "state_mlstm_n", "state_mlstm_m", "c", "c_ctx", "w_mod", "b_mod", "w_in",
        "qk_gain", "sink_logit", "mlstm_gate_bias", "w_branch", "w_out", "ln_gain", "ln_bias"]
_OUTS = [(1, P, D), (1, LT * P, D), (1, DEPTH, KV, P, HD), (1, DEPTH, KV, P, HD), (1, DEPTH, KV, P, HD),
         (1, DEPTH, KV, P, HD), (1, DEPTH, 2, MH, DV, HD), (1, DEPTH, 2, MH, HD), (1, DEPTH, 2, MH)]


def kernel(**inputs):
    import numpy as _np
    import concourse.bacc as _bacc
    from concourse.bass_utils import run_bass_kernel_spmd as _run

    nc = _bacc.Bacc("TRN2", target_bir_lowering=False, num_devices=1)
    arrays, args = {}, []
    for name in _INS:
        arrays[f"in_{name}"] = _np.ascontiguousarray(inputs[name])
    arrays["in_consts"] = shape_constants()
    for name, a in arrays.items():
        args.append(nc.dram_tensor(name, a.shape, mybir.dt.from_np(a.dtype), kind="ExternalInput").ap())
    for i, shape in enumerate(_OUTS):
        args.append(nc.dram_tensor(f"out_{i}", shape, F32, kind="ExternalOutput").ap())
    trunk_kernel(nc, *args)
    r = _run(nc, [arrays], core_ids=[0])
    return tuple(r.results[0][f"out_{i}"] for i in range(len(_OUTS)))
```
